# Optimizing a Trainium2 kernel written in Bass

```python
import math
import jax, jax.numpy as jnp
from jax import lax
import numpy as np
import jax
import jax.numpy as jnp

D_MODEL = 1024
BATCH = 1
SEQ = 256
DEPTH = 2

CHUNK = 64
HEAD_DIM = 64
N_MIX_HEADS = D_MODEL // HEAD_DIM
MEM_HEADS = 4
SELF_HEADS = N_MIX_HEADS - MEM_HEADS
SWA_KV_HEADS = 3
SWA_GROUP = SELF_HEADS // SWA_KV_HEADS
WINDOW = 128
WINDOW_CHUNKS = WINDOW // CHUNK
ROT_DIM = HEAD_DIM // 4
ROT_HALF = ROT_DIM // 2
ROPE_THETA = 500000.0
FOX_BLOCK = 128
MEM_LEN = 256
D_FF = ((8 * D_MODEL // 3 + 127) // 128) * 128
N_EXPERTS = 8
TOP_K = 2
EXPERT_BLOCK = 128
LN_EPS = 1e-5
NEG = -1e30
ATTN_SCALE = HEAD_DIM ** -0.5
DN_ALPHA = (2.0 * DEPTH) ** 0.25
DN_BETA = (8.0 * DEPTH) ** -0.25
N_SWA_LAYERS = (DEPTH + 1) // 2
N_FOX_LAYERS = DEPTH // 2
SWA_IN = (SELF_HEADS + 2 * SWA_KV_HEADS + MEM_HEADS) * HEAD_DIM
FOX_IN = (3 * SELF_HEADS + MEM_HEADS) * HEAD_DIM + SELF_HEADS


def layer_norm(x, g, b):
    xf = x.astype(jnp.float32)
    mu = jnp.mean(xf, axis=-1, keepdims=True)
    var = jnp.mean(jnp.square(xf - mu), axis=-1, keepdims=True)
    return ((xf - mu) * lax.rsqrt(var + LN_EPS) * g + b).astype(x.dtype)

def rope_tables(positions):
    inv_freq = ROPE_THETA ** (-jnp.arange(0, ROT_DIM, 2, dtype=jnp.float32) / ROT_DIM)
    ang = positions.astype(jnp.float32)[..., None] * inv_freq
    return jnp.cos(ang)[:, :, None, :], jnp.sin(ang)[:, :, None, :]

def partial_rope(t, cos, sin):
    r = t[..., :ROT_DIM].astype(jnp.float32)
    r1, r2 = r[..., :ROT_HALF], r[..., ROT_HALF:]
    rot = jnp.concatenate([r1 * cos - r2 * sin, r2 * cos + r1 * sin], axis=-1)
    return jnp.concatenate([rot.astype(t.dtype), t[..., ROT_DIM:]], axis=-1)

def swa_sink_attention(q, k, v, sinks):
    B, S = q.shape[0], q.shape[1]
    n_c = S // CHUNK
    pad = WINDOW_CHUNKS * CHUNK
    n_keys = (WINDOW_CHUNKS + 1) * CHUNK
    qb = q.reshape(B, n_c, CHUNK, SWA_KV_HEADS, SWA_GROUP, HEAD_DIM)

    def band(t):
        tp = jnp.pad(t, ((0, 0), (pad, 0), (0, 0), (0, 0)))
        tp = tp.reshape(B, n_c + WINDOW_CHUNKS, CHUNK, SWA_KV_HEADS, HEAD_DIM)
        return jnp.concatenate([tp[:, m:m + n_c] for m in range(WINDOW_CHUNKS + 1)], axis=2)

    kb, vb = band(k), band(v)
    s = jnp.einsum('bnqhgd,bnkhd->bnhgqk', qb, kb).astype(jnp.float32) * ATTN_SCALE
    key_chunk = jnp.arange(n_c)[:, None] - WINDOW_CHUNKS + (jnp.arange(n_keys) // CHUNK)[None, :]
    valid = key_chunk >= 0
    s = jnp.where(valid[None, :, None, None, None, :], s, NEG)
    sk = sinks.astype(jnp.float32).reshape(SWA_KV_HEADS, SWA_GROUP)[None, None, :, :, None]
    m = jnp.maximum(jnp.max(s, axis=-1), sk)
    p = jnp.exp(s - m[..., None])
    den = jnp.sum(p, axis=-1) + jnp.exp(sk - m)
    probs = (p / den[..., None]).astype(v.dtype)
    o = jnp.einsum('bnhgqk,bnkhd->bnqhgd', probs, vb)
    return o.reshape(B, S, SELF_HEADS * HEAD_DIM)

def forgetting_attention(q, k, v, log_f):
    B, S = q.shape[0], q.shape[1]
    cum = jnp.cumsum(log_f, axis=1).transpose(0, 2, 1)
    outs = []
    for i in range(S // FOX_BLOCK):
        lo, hi = i * FOX_BLOCK, (i + 1) * FOX_BLOCK
        s = jnp.einsum('bqhd,bkhd->bhqk', q[:, lo:hi], k[:, :hi]).astype(jnp.float32) * ATTN_SCALE
        bias = cum[:, :, lo:hi, None] - cum[:, :, None, :hi]
        causal = jnp.arange(lo, hi)[:, None] >= jnp.arange(hi)[None, :]
        s = jnp.where(causal, s + bias, NEG)
        p = jax.nn.softmax(s, axis=-1).astype(v.dtype)
        outs.append(jnp.einsum('bhqk,bkhd->bqhd', p, v[:, :hi]))
    return jnp.concatenate(outs, axis=1).reshape(B, S, SELF_HEADS * HEAD_DIM)

def memory_attention(qc, km, vm):
    B, S = qc.shape[0], qc.shape[1]
    s = jnp.einsum('bshd,bmhd->bhsm', qc, km).astype(jnp.float32) * ATTN_SCALE
    p = jax.nn.softmax(s, axis=-1).astype(vm.dtype)
    return jnp.einsum('bhsm,bmhd->bshd', p, vm).reshape(B, S, MEM_HEADS * HEAD_DIM)

def swiglu(x, w_in, w_out):
    h = x @ w_in
    a, b = h[..., :D_FF], h[..., D_FF:]
    return (jax.nn.silu(a) * b) @ w_out

def moe_swiglu(x, w_router, b_router, w_in, w_out):
    shp = x.shape
    x2 = x.reshape(-1, shp[-1])
    n_tok = x2.shape[0]
    logits = (x2 @ w_router).astype(jnp.float32) + b_router.astype(jnp.float32)
    top_vals, top_idx = lax.top_k(logits, TOP_K)
    gates = jax.nn.softmax(top_vals, axis=-1)
    n_asg = n_tok * TOP_K
    e_flat = top_idx.reshape(-1)
    t_flat = jnp.repeat(jnp.arange(n_tok, dtype=jnp.int32), TOP_K)
    g_flat = gates.reshape(-1)
    order = jnp.argsort(e_flat)
    se, st, sg = e_flat[order], t_flat[order], g_flat[order]
    counts = jnp.bincount(e_flat, length=N_EXPERTS)
    starts = jnp.cumsum(counts) - counts
    pcounts = (counts + EXPERT_BLOCK - 1) // EXPERT_BLOCK * EXPERT_BLOCK
    pends = jnp.cumsum(pcounts)
    pstarts = pends - pcounts
    dest = pstarts[se] + (jnp.arange(n_asg) - starts[se])
    n_blocks = -(-n_asg // EXPERT_BLOCK) + N_EXPERTS
    n_slots = n_blocks * EXPERT_BLOCK
    slot_tok = jnp.zeros((n_slots,), jnp.int32).at[dest].set(st)
    slot_gate = jnp.zeros((n_slots,), x2.dtype).at[dest].set(sg.astype(x2.dtype))
    block_exp = jnp.minimum(
        jnp.searchsorted(pends, jnp.arange(n_blocks) * EXPERT_BLOCK, side='right'), N_EXPERTS - 1)
    xs = x2[slot_tok].reshape(n_blocks, EXPERT_BLOCK, shp[-1])

    def expert_block(args):
        xb, e = args
        h = xb @ w_in[e]
        return (jax.nn.silu(h[:, :D_FF]) * h[:, D_FF:]) @ w_out[e]

    ys = lax.map(expert_block, (xs, block_exp)).reshape(n_slots, shp[-1])
    y = jnp.zeros_like(x2).at[slot_tok].add((ys * slot_gate[:, None]).astype(x2.dtype))
    return y.reshape(shp)

def first_inputs(seed: int = 0) -> dict:
    key = jax.random.key(seed)
    ks = jax.random.split(key, 20)
    nrm = jax.random.normal
    f32 = jnp.float32
    x = nrm(ks[0], (BATCH, SEQ, D_MODEL), f32)
    mem = nrm(ks[1], (BATCH, MEM_LEN, D_MODEL), f32)
    offset = jax.random.randint(ks[2], (BATCH, 1), 0, 1 << 16, dtype=jnp.int32)
    positions = offset + jnp.arange(SEQ, dtype=jnp.int32)[None, :]
    sd = D_MODEL ** -0.5
    sf = D_FF ** -0.5
    return {
        "x": x,
        "mem": mem,
        "positions": positions,
        "w_in_swa": nrm(ks[3], (N_SWA_LAYERS, D_MODEL, SWA_IN), f32) * sd,
        "attn_sinks": nrm(ks[4], (N_SWA_LAYERS, SELF_HEADS), f32) * 0.5,
        "w_in_fox": nrm(ks[5], (N_FOX_LAYERS, D_MODEL, FOX_IN), f32) * sd,
        "b_forget": jax.random.uniform(ks[6], (N_FOX_LAYERS, SELF_HEADS), f32, 1.0, 4.0),
        "w_mem_kv": nrm(ks[7], (DEPTH, D_MODEL, 2 * MEM_HEADS * HEAD_DIM), f32) * sd,
        "w_out": nrm(ks[8], (DEPTH, D_MODEL, D_MODEL), f32) * sd * DN_BETA,
        "ln_attn_g": 1.0 + 0.02 * nrm(ks[9], (DEPTH, D_MODEL), f32),
        "ln_attn_b": 0.02 * nrm(ks[10], (DEPTH, D_MODEL), f32),
        "w_ffn_in": nrm(ks[11], (N_SWA_LAYERS, D_MODEL, 2 * D_FF), f32) * sd,
        "w_ffn_out": nrm(ks[12], (N_SWA_LAYERS, D_FF, D_MODEL), f32) * sf * DN_BETA,
        "w_router": nrm(ks[13], (N_FOX_LAYERS, D_MODEL, N_EXPERTS), f32) * sd,
        "b_router": 0.01 * nrm(ks[14], (N_FOX_LAYERS, N_EXPERTS), f32),
        "w_exp_in": nrm(ks[15], (N_FOX_LAYERS, N_EXPERTS, D_MODEL, 2 * D_FF), f32) * sd,
        "w_exp_out": nrm(ks[16], (N_FOX_LAYERS, N_EXPERTS, D_FF, D_MODEL), f32) * sf * DN_BETA,
        "ln_ffn_g": 1.0 + 0.02 * nrm(ks[17], (DEPTH, D_MODEL), f32),
        "ln_ffn_b": 0.02 * nrm(ks[18], (DEPTH, D_MODEL), f32),
    }

def first_block(x, mem, positions, w_in_swa, attn_sinks, w_in_fox, b_forget, w_mem_kv, w_out,
              ln_attn_g, ln_attn_b, w_ffn_in, w_ffn_out, w_router, b_router, w_exp_in,
              w_exp_out, ln_ffn_g, ln_ffn_b):
    B, S = x.shape[0], x.shape[1]
    cos, sin = rope_tables(positions)
    hq = SELF_HEADS * HEAD_DIM
    hkv = SWA_KV_HEADS * HEAD_DIM
    hm = MEM_HEADS * HEAD_DIM
    for i in range(DEPTH):
        j = i // 2
        kvm = mem @ w_mem_kv[i]
        km = kvm[..., :hm].reshape(B, MEM_LEN, MEM_HEADS, HEAD_DIM)
        vm = kvm[..., hm:].reshape(B, MEM_LEN, MEM_HEADS, HEAD_DIM)
        if i % 2 == 0:
            proj = x @ w_in_swa[j]
            q = proj[..., :hq].reshape(B, S, SELF_HEADS, HEAD_DIM)
            k = proj[..., hq:hq + hkv].reshape(B, S, SWA_KV_HEADS, HEAD_DIM)
            v = proj[..., hq + hkv:hq + 2 * hkv].reshape(B, S, SWA_KV_HEADS, HEAD_DIM)
            qc = proj[..., hq + 2 * hkv:].reshape(B, S, MEM_HEADS, HEAD_DIM)
            q, k = partial_rope(q, cos, sin), partial_rope(k, cos, sin)
            self_out = swa_sink_attention(q, k, v, attn_sinks[j])
        else:
            proj = x @ w_in_fox[j]
            q = proj[..., :hq].reshape(B, S, SELF_HEADS, HEAD_DIM)
            k = proj[..., hq:2 * hq].reshape(B, S, SELF_HEADS, HEAD_DIM)
            v = proj[..., 2 * hq:3 * hq].reshape(B, S, SELF_HEADS, HEAD_DIM)
            qc = proj[..., 3 * hq:3 * hq + hm].reshape(B, S, MEM_HEADS, HEAD_DIM)
            f_logit = proj[..., 3 * hq + hm:].astype(jnp.float32) + b_forget[j].astype(jnp.float32)
            log_f = jax.nn.log_sigmoid(f_logit)
            self_out = forgetting_attention(q, k, v, log_f)
        cross_out = memory_attention(qc, km, vm)
        mix = jnp.concatenate([self_out, cross_out], axis=-1) @ w_out[i]
        x = layer_norm(DN_ALPHA * x + mix, ln_attn_g[i], ln_attn_b[i])
        if i % 2 == 0:
            ffn = swiglu(x, w_ffn_in[j], w_ffn_out[j])
        else:
            ffn = moe_swiglu(x, w_router[j], b_router[j], w_exp_in[j], w_exp_out[j])
        x = layer_norm(DN_ALPHA * x + ffn, ln_ffn_g[i], ln_ffn_b[i])
    return x


DEPTH_2 = 1

D_RWKV = D_MODEL // 2
RWKV_HEADS = D_RWKV // HEAD_DIM
DECAY_LORA = 64
ICL_LORA = 64
GATE_LORA = 128
RWKV_GN_EPS = 64e-5
D_MOBA = D_MODEL // 2
MOBA_HEADS = D_MOBA // HEAD_DIM
MOBA_BLOCK = 256
MOBA_TOPK = 3
MOBA_Q_CHUNK = 32
D_SSM = D_MODEL // 2
SSM_GROUP = 16
SSM_GROUPS = D_SSM // SSM_GROUP
SSM_STATE = 64
N_BRANCHES = 3
N_EXPERT_GROUPS = 4
EXPERTS_PER_GROUP = 8
N_EXPERTS_2 = N_EXPERT_GROUPS * EXPERTS_PER_GROUP
EXPERT_TOPK = 2
D_EXPERT = D_MODEL // 4
MOE_BLOCK = 512
DEEPNORM_ALPHA = (2 * DEPTH_2) ** 0.25
DEEPNORM_BETA = (8 * DEPTH_2) ** -0.25
NEG_INF = -1e30
RWKV_COLS = 3 * D_RWKV + DECAY_LORA + ICL_LORA + GATE_LORA
MOBA_COLS = 3 * D_MOBA
OFF_MOBA = RWKV_COLS
OFF_SSM = OFF_MOBA + MOBA_COLS
OFF_GATE = OFF_SSM + D_SSM
D_IN_PROJ = OFF_GATE + N_BRANCHES * D_MODEL


def layer_norm_2(x, w, b):
    xf = x.astype(jnp.float32)
    mu = jnp.mean(xf, -1, keepdims=True)
    var = jnp.mean(jnp.square(xf - mu), -1, keepdims=True)
    y = (xf - mu) * lax.rsqrt(var + LN_EPS) * w.astype(jnp.float32) + b.astype(jnp.float32)
    return y.astype(x.dtype)

def wkv7_scan(r, w, k, v, a, b):
    Bsz, L, H, N = r.shape

    def step(S, inp):
        r_t, w_t, k_t, v_t, a_t, b_t = inp
        sa = jnp.einsum('bhij,bhj->bhi', S, a_t)
        S = S * w_t[:, :, None, :] + sa[..., None] * b_t[:, :, None, :] + v_t[..., None] * k_t[:, :, None, :]
        return S, jnp.einsum('bhij,bhj->bhi', S, r_t)

    xs = tuple(jnp.moveaxis(t, 1, 0) for t in (r, w, k, v, a, b))
    S0 = jnp.zeros((Bsz, H, N, N), jnp.float32)
    _, y = lax.scan(step, S0, xs)
    return jnp.moveaxis(y, 0, 1)

def rwkv7_mixer(z, mu, w0, w2, a0, a2, g2, k_k, k_a, r_k, ln_w, ln_b):
    f32 = jnp.float32
    Bsz, L, _ = z.shape
    z = z.astype(f32)
    z_prev = jnp.pad(z, ((0, 0), (1, 0), (0, 0)))[:, :-1]
    z = z + (z_prev - z) * mu.astype(f32)
    cuts = np.cumsum([D_RWKV, D_RWKV, D_RWKV, DECAY_LORA, ICL_LORA]).tolist()
    r, k, v, xw, xa, xg = jnp.split(z, cuts, axis=-1)
    w_log = -jax.nn.softplus(-(w0.astype(f32) + jnp.tanh(xw) @ w2.astype(f32))) - 0.5
    decay = jnp.exp(-jnp.exp(w_log))
    a = jax.nn.sigmoid(a0.astype(f32) + xa @ a2.astype(f32))
    g = jax.nn.sigmoid(xg) @ g2.astype(f32)

    def heads(t):
        return t.reshape(Bsz, L, RWKV_HEADS, HEAD_DIM)

    kk = heads(k * k_k.astype(f32))
    kk = kk * lax.rsqrt(jnp.maximum(jnp.sum(kk * kk, -1, keepdims=True), 1e-24))
    k = k * (1.0 + (a - 1.0) * k_a.astype(f32))
    rh, kh, vh, ah = heads(r), heads(k), heads(v), heads(a)
    y = wkv7_scan(rh, heads(decay), kh, vh, -kk, kk * ah)
    mean = jnp.mean(y, -1, keepdims=True)
    var = jnp.mean(jnp.square(y - mean), -1, keepdims=True)
    y = ((y - mean) * lax.rsqrt(var + RWKV_GN_EPS)).reshape(Bsz, L, D_RWKV)
    y = y * ln_w.astype(f32) + ln_b.astype(f32)
    bonus = jnp.sum(rh * kh * r_k.astype(f32), -1, keepdims=True) * vh
    return (y + bonus.reshape(Bsz, L, D_RWKV)) * g

def alibi_slopes(n_heads):
    return 2.0 ** (-8.0 * jnp.arange(1, n_heads + 1, dtype=jnp.float32) / n_heads)

def moba_attention(q, k, v):
    f32 = jnp.float32
    Bsz, L, H, Dh = q.shape
    n_blk = -(-L // MOBA_BLOCK)
    Lp = n_blk * MOBA_BLOCK
    k_sel = min(MOBA_TOPK, n_blk)
    pad = ((0, 0), (0, Lp - L), (0, 0), (0, 0))
    q = jnp.pad(q, pad) * (Dh ** -0.5)
    kbt = jnp.pad(k, pad).reshape(Bsz, n_blk, MOBA_BLOCK, H, Dh).transpose(0, 3, 1, 2, 4)
    vbt = jnp.pad(v, pad).reshape(Bsz, n_blk, MOBA_BLOCK, H, Dh).transpose(0, 3, 1, 2, 4)
    kmean = jnp.mean(kbt.astype(f32), axis=3)
    n_chunk = Lp // MOBA_Q_CHUNK
    qc = q.reshape(Bsz, n_chunk, MOBA_Q_CHUNK, H, Dh).transpose(1, 0, 3, 2, 4)
    slopes = alibi_slopes(H)
    bi = jnp.arange(Bsz)[:, None, None, None]
    hi = jnp.arange(H)[None, :, None, None]
    blk_ids = jnp.arange(n_blk)
    offs = jnp.arange(MOBA_BLOCK)

    def one_chunk(args):
        c, qb = args
        q0 = c * MOBA_Q_CHUNK
        blk = q0 // MOBA_BLOCK
        tpos = q0 + jnp.arange(MOBA_Q_CHUNK)
        gate = jnp.einsum('bhqd,bhnd->bhqn', qb.astype(f32), kmean)
        gate = jnp.where(blk_ids < blk, gate, -jnp.inf)
        _, idx = lax.top_k(gate, k_sel)
        valid = idx < blk
        kg = kbt[bi, hi, idx]
        vg = vbt[bi, hi, idx]
        s_sel = jnp.einsum('bhqd,bhqknd->bhqkn', qb, kg, preferred_element_type=f32)
        spos = idx[..., None] * MOBA_BLOCK + offs
        s_sel = s_sel - slopes[:, None, None, None] * (tpos[:, None, None] - spos).astype(f32)
        s_sel = jnp.where(valid[..., None], s_sel, NEG_INF)
        k_own = lax.dynamic_index_in_dim(kbt, blk, axis=2, keepdims=False)
        v_own = lax.dynamic_index_in_dim(vbt, blk, axis=2, keepdims=False)
        s_own = jnp.einsum('bhqd,bhnd->bhqn', qb, k_own, preferred_element_type=f32)
        dist = tpos[:, None] - (blk * MOBA_BLOCK + offs)[None, :]
        s_own = jnp.where(dist >= 0, s_own - slopes[:, None, None] * dist.astype(f32), NEG_INF)
        s = jnp.concatenate([s_sel.reshape(Bsz, H, MOBA_Q_CHUNK, k_sel * MOBA_BLOCK), s_own], -1)
        p = jax.nn.softmax(s, axis=-1)
        p_sel = p[..., :k_sel * MOBA_BLOCK].reshape(Bsz, H, MOBA_Q_CHUNK, k_sel, MOBA_BLOCK).astype(vg.dtype)
        p_own = p[..., k_sel * MOBA_BLOCK:].astype(v_own.dtype)
        return (jnp.einsum('bhqkn,bhqknd->bhqd', p_sel, vg)
                + jnp.einsum('bhqn,bhnd->bhqd', p_own, v_own))

    out = lax.map(one_chunk, (jnp.arange(n_chunk), qc))
    return out.transpose(1, 0, 3, 2, 4).reshape(Bsz, Lp, H * Dh)[:, :L]

def _complex_affine_combine(e1, e2):
    ar1, ai1, br1, bi1 = e1
    ar2, ai2, br2, bi2 = e2
    return (ar2 * ar1 - ai2 * ai1, ar2 * ai1 + ai2 * ar1,
            ar2 * br1 - ai2 * bi1 + br2, ar2 * bi1 + ai2 * br1 + bi2)

def s5_mixer(u, a_re, a_im, b_re, b_im, c_re, c_im, d, log_dt, glu_w, glu_b):
    f32 = jnp.float32
    Bsz, L, _ = u.shape
    u = u.astype(f32)
    a_re = a_re.astype(f32)
    a_im = a_im.astype(f32)
    dt = jnp.exp(log_dt.astype(f32))[:, None]
    mag = jnp.exp(a_re * dt)
    lam_re = mag * jnp.cos(a_im * dt)
    lam_im = mag * jnp.sin(a_im * dt)
    den = a_re * a_re + a_im * a_im
    nr = lam_re - 1.0
    coef_re = (nr * a_re + lam_im * a_im) / den
    coef_im = (lam_im * a_re - nr * a_im) / den
    b_re = b_re.astype(f32)
    b_im = b_im.astype(f32)
    bb_re = coef_re[..., None] * b_re - coef_im[..., None] * b_im
    bb_im = coef_re[..., None] * b_im + coef_im[..., None] * b_re
    ug = u.reshape(Bsz, L, SSM_GROUPS, SSM_GROUP)
    bu_re = jnp.einsum('blgh,gph->blgp', ug, bb_re)
    bu_im = jnp.einsum('blgh,gph->blgp', ug, bb_im)
    lr = jnp.broadcast_to(lam_re, bu_re.shape)
    li = jnp.broadcast_to(lam_im, bu_re.shape)
    _, _, h_re, h_im = lax.associative_scan(_complex_affine_combine, (lr, li, bu_re, bu_im), axis=1)
    y = (jnp.einsum('blgp,ghp->blgh', h_re, c_re.astype(f32))
         - jnp.einsum('blgp,ghp->blgh', h_im, c_im.astype(f32)))
    y = y.reshape(Bsz, L, D_SSM) + d.astype(f32) * u
    y = jax.nn.gelu(y)
    zg = y @ glu_w.astype(f32) + glu_b.astype(f32)
    return zg[..., :D_SSM] * jax.nn.sigmoid(zg[..., D_SSM:])

def hybrid_mixer(x, w_in, rwkv_mu, rwkv_w0, rwkv_w2, rwkv_a0, rwkv_a2, rwkv_g2, rwkv_k_k, rwkv_k_a,
                 rwkv_r_k, rwkv_ln_w, rwkv_ln_b, ssm_a_re, ssm_a_im, ssm_b_re, ssm_b_im, ssm_c_re,
                 ssm_c_im, ssm_d, ssm_log_dt, ssm_glu_w, ssm_glu_b, w_up_rwkv, w_up_moba, w_up_ssm,
                 gate_b, w_out):
    Bsz, L, _ = x.shape
    proj = x @ w_in
    y_a = rwkv7_mixer(proj[..., :OFF_MOBA], rwkv_mu, rwkv_w0, rwkv_w2, rwkv_a0, rwkv_a2, rwkv_g2,
                      rwkv_k_k, rwkv_k_a, rwkv_r_k, rwkv_ln_w, rwkv_ln_b).astype(x.dtype)
    q, k, v = jnp.split(proj[..., OFF_MOBA:OFF_SSM], 3, axis=-1)

    def heads(t):
        return t.reshape(Bsz, L, MOBA_HEADS, HEAD_DIM)

    y_b = moba_attention(heads(q), heads(k), heads(v))
    y_c = s5_mixer(proj[..., OFF_SSM:OFF_GATE], ssm_a_re, ssm_a_im, ssm_b_re, ssm_b_im, ssm_c_re,
                   ssm_c_im, ssm_d, ssm_log_dt, ssm_glu_w, ssm_glu_b).astype(x.dtype)
    gates = jax.nn.sigmoid(proj[..., OFF_GATE:] + gate_b).reshape(Bsz, L, N_BRANCHES, D_MODEL)
    merged = (gates[..., 0, :] * (y_a @ w_up_rwkv)
              + gates[..., 1, :] * (y_b @ w_up_moba)
              + gates[..., 2, :] * (y_c @ w_up_ssm))
    return merged @ w_out

def hier_moe(x, router_group_w, router_group_b, router_expert_w, router_expert_b,
             expert_w_gate, expert_w_up, expert_w_down):
    f32 = jnp.float32
    Bsz, L, D = x.shape
    T = Bsz * L
    TK = T * EXPERT_TOPK
    xt = x.reshape(T, D)
    xf = xt.astype(f32)
    g_logits = xf @ router_group_w.astype(f32) + router_group_b.astype(f32)
    g_sel = jnp.argmax(g_logits, axis=-1)
    p_group = jnp.take_along_axis(jax.nn.softmax(g_logits, -1), g_sel[:, None], axis=-1)
    e_logits = (xf @ router_expert_w.astype(f32) + router_expert_b.astype(f32)).reshape(
        T, N_EXPERT_GROUPS, EXPERTS_PER_GROUP)
    e_logits = jnp.take_along_axis(e_logits, g_sel[:, None, None], axis=1)[:, 0]
    top_logit, top_local = lax.top_k(e_logits, EXPERT_TOPK)
    weight = p_group * jax.nn.softmax(top_logit, axis=-1)
    expert = g_sel[:, None] * EXPERTS_PER_GROUP + top_local
    flat_e = expert.reshape(TK)
    order = jnp.argsort(flat_e)
    e_sorted = flat_e[order]
    tok_sorted = order // EXPERT_TOPK
    counts = jnp.bincount(flat_e, length=N_EXPERTS_2)
    starts = jnp.cumsum(counts) - counts
    padded = (counts + MOE_BLOCK - 1) // MOE_BLOCK * MOE_BLOCK
    p_ends = jnp.cumsum(padded)
    p_starts = p_ends - padded
    dest = p_starts[e_sorted] + jnp.arange(TK) - starts[e_sorted]
    n_blocks = -(-TK // MOE_BLOCK) + N_EXPERTS_2
    buf = jnp.zeros((n_blocks * MOE_BLOCK, D), x.dtype).at[dest].set(xt[tok_sorted])
    blk_e = jnp.minimum(jnp.searchsorted(p_ends, jnp.arange(n_blocks) * MOE_BLOCK, side='right'),
                        N_EXPERTS_2 - 1)
    xb = buf.reshape(n_blocks, MOE_BLOCK, D)
    hid = (jax.nn.silu(jnp.einsum('nbd,ndf->nbf', xb, expert_w_gate[blk_e]))
           * jnp.einsum('nbd,ndf->nbf', xb, expert_w_up[blk_e]))
    yb = jnp.einsum('nbf,nfd->nbd', hid, expert_w_down[blk_e]).reshape(n_blocks * MOE_BLOCK, D)
    w_sorted = weight.reshape(TK)[order].astype(x.dtype)
    y = jnp.zeros((T, D), x.dtype).at[tok_sorted].add(yb[dest] * w_sorted[:, None])
    return y.reshape(Bsz, L, D)

def second_inputs(seed: int = 0) -> dict:
    key = jax.random.key(seed)
    keys = iter(jax.random.split(key, 48))
    f32 = jnp.float32

    def nrm(shape, scale):
        return scale * jax.random.normal(next(keys), shape, f32)

    def near(shape, center, spread):
        return center + spread * jax.random.normal(next(keys), shape, f32)

    Ld = DEPTH_2
    ratio = jnp.arange(D_RWKV, dtype=f32) / (D_RWKV - 1)
    w0_base = -7.0 + 5.0 * ratio ** 0.85 + 0.5
    a_im_base = jnp.pi * jnp.arange(SSM_STATE, dtype=f32)
    return {
        'x': nrm((BATCH, SEQ, D_MODEL), 1.0),
        'w_in': nrm((Ld, D_MODEL, D_IN_PROJ), D_MODEL ** -0.5),
        'rwkv_mu': jax.random.uniform(next(keys), (Ld, RWKV_COLS), f32),
        'rwkv_w0': w0_base + nrm((Ld, D_RWKV), 0.1),
        'rwkv_w2': nrm((Ld, DECAY_LORA, D_RWKV), 0.5 * DECAY_LORA ** -0.5),
        'rwkv_a0': nrm((Ld, D_RWKV), 0.1),
        'rwkv_a2': nrm((Ld, ICL_LORA, D_RWKV), ICL_LORA ** -0.5),
        'rwkv_g2': nrm((Ld, GATE_LORA, D_RWKV), GATE_LORA ** -0.5),
        'rwkv_k_k': near((Ld, D_RWKV), 0.85, 0.05),
        'rwkv_k_a': near((Ld, D_RWKV), 1.0, 0.05),
        'rwkv_r_k': nrm((Ld, RWKV_HEADS, HEAD_DIM), 0.1),
        'rwkv_ln_w': near((Ld, D_RWKV), 1.0, 0.05),
        'rwkv_ln_b': nrm((Ld, D_RWKV), 0.02),
        'ssm_a_re': near((Ld, SSM_GROUPS, SSM_STATE), -0.5, 0.01),
        'ssm_a_im': jnp.broadcast_to(a_im_base, (Ld, SSM_GROUPS, SSM_STATE)) + nrm((Ld, SSM_GROUPS, SSM_STATE), 0.01),
        'ssm_b_re': nrm((Ld, SSM_GROUPS, SSM_STATE, SSM_GROUP), (2 * SSM_GROUP) ** -0.5),
        'ssm_b_im': nrm((Ld, SSM_GROUPS, SSM_STATE, SSM_GROUP), (2 * SSM_GROUP) ** -0.5),
        'ssm_c_re': nrm((Ld, SSM_GROUPS, SSM_GROUP, SSM_STATE), 0.5),
        'ssm_c_im': nrm((Ld, SSM_GROUPS, SSM_GROUP, SSM_STATE), 0.5),
        'ssm_d': nrm((Ld, D_SSM), 1.0),
        'ssm_log_dt': jax.random.uniform(next(keys), (Ld, SSM_GROUPS), f32,
                                         minval=float(np.log(1e-3)), maxval=float(np.log(1e-1))),
        'ssm_glu_w': nrm((Ld, D_SSM, 2 * D_SSM), D_SSM ** -0.5),
        'ssm_glu_b': nrm((Ld, 2 * D_SSM), 0.02),
        'w_up_rwkv': nrm((Ld, D_RWKV, D_MODEL), D_RWKV ** -0.5),
        'w_up_moba': nrm((Ld, D_MOBA, D_MODEL), D_MOBA ** -0.5),
        'w_up_ssm': nrm((Ld, D_SSM, D_MODEL), D_SSM ** -0.5),
        'gate_b': nrm((Ld, N_BRANCHES * D_MODEL), 0.1),
        'w_out': nrm((Ld, D_MODEL, D_MODEL), DEEPNORM_BETA * D_MODEL ** -0.5),
        'ln1_w': near((Ld, D_MODEL), 1.0, 0.05),
        'ln1_b': nrm((Ld, D_MODEL), 0.02),
        'router_group_w': nrm((Ld, D_MODEL, N_EXPERT_GROUPS), D_MODEL ** -0.5),
        'router_group_b': nrm((Ld, N_EXPERT_GROUPS), 0.01),
        'router_expert_w': nrm((Ld, D_MODEL, N_EXPERTS_2), D_MODEL ** -0.5),
        'router_expert_b': nrm((Ld, N_EXPERTS_2), 0.01),
        'expert_w_gate': nrm((Ld, N_EXPERTS_2, D_MODEL, D_EXPERT), D_MODEL ** -0.5),
        'expert_w_up': nrm((Ld, N_EXPERTS_2, D_MODEL, D_EXPERT), D_MODEL ** -0.5),
        'expert_w_down': nrm((Ld, N_EXPERTS_2, D_EXPERT, D_MODEL), DEEPNORM_BETA * D_EXPERT ** -0.5),
        'ln2_w': near((Ld, D_MODEL), 1.0, 0.05),
        'ln2_b': nrm((Ld, D_MODEL), 0.02),
    }

def second_block(x, w_in, rwkv_mu, rwkv_w0, rwkv_w2, rwkv_a0, rwkv_a2, rwkv_g2, rwkv_k_k, rwkv_k_a,
              rwkv_r_k, rwkv_ln_w, rwkv_ln_b, ssm_a_re, ssm_a_im, ssm_b_re, ssm_b_im, ssm_c_re,
              ssm_c_im, ssm_d, ssm_log_dt, ssm_glu_w, ssm_glu_b, w_up_rwkv, w_up_moba, w_up_ssm,
              gate_b, w_out, ln1_w, ln1_b, router_group_w, router_group_b, router_expert_w,
              router_expert_b, expert_w_gate, expert_w_up, expert_w_down, ln2_w, ln2_b):
    for l in range(DEPTH_2):
        h = hybrid_mixer(x, w_in[l], rwkv_mu[l], rwkv_w0[l], rwkv_w2[l], rwkv_a0[l], rwkv_a2[l],
                         rwkv_g2[l], rwkv_k_k[l], rwkv_k_a[l], rwkv_r_k[l], rwkv_ln_w[l], rwkv_ln_b[l],
                         ssm_a_re[l], ssm_a_im[l], ssm_b_re[l], ssm_b_im[l], ssm_c_re[l], ssm_c_im[l],
                         ssm_d[l], ssm_log_dt[l], ssm_glu_w[l], ssm_glu_b[l], w_up_rwkv[l],
                         w_up_moba[l], w_up_ssm[l], gate_b[l], w_out[l])
        x = layer_norm_2(DEEPNORM_ALPHA * x + h, ln1_w[l], ln1_b[l])
        h = hier_moe(x, router_group_w[l], router_group_b[l], router_expert_w[l], router_expert_b[l],
                     expert_w_gate[l], expert_w_up[l], expert_w_down[l])
        x = layer_norm_2(DEEPNORM_ALPHA * x + h, ln2_w[l], ln2_b[l])
    return x


def setup_inputs(seed=0):
    out = dict(first_inputs(seed))
    for name, value in second_inputs(seed + 1).items():
        if name != "x":
            out[name + "_2"] = value
    return out


def reference(
    x, mem, positions, w_in_swa, attn_sinks, w_in_fox, b_forget, w_mem_kv, w_out, ln_attn_g,
    ln_attn_b, w_ffn_in, w_ffn_out, w_router, b_router, w_exp_in, w_exp_out, ln_ffn_g, ln_ffn_b,
    w_in_2, rwkv_mu_2, rwkv_w0_2, rwkv_w2_2, rwkv_a0_2, rwkv_a2_2, rwkv_g2_2, rwkv_k_k_2,
    rwkv_k_a_2, rwkv_r_k_2, rwkv_ln_w_2, rwkv_ln_b_2, ssm_a_re_2, ssm_a_im_2, ssm_b_re_2,
    ssm_b_im_2, ssm_c_re_2, ssm_c_im_2, ssm_d_2, ssm_log_dt_2, ssm_glu_w_2, ssm_glu_b_2,
    w_up_rwkv_2, w_up_moba_2, w_up_ssm_2, gate_b_2, w_out_2, ln1_w_2, ln1_b_2, router_group_w_2,
    router_group_b_2, router_expert_w_2, router_expert_b_2, expert_w_gate_2, expert_w_up_2,
    expert_w_down_2, ln2_w_2, ln2_b_2,
):
    x = first_block(
        x, mem, positions, w_in_swa, attn_sinks, w_in_fox, b_forget, w_mem_kv, w_out, ln_attn_g,
        ln_attn_b, w_ffn_in, w_ffn_out, w_router, b_router, w_exp_in, w_exp_out, ln_ffn_g,
        ln_ffn_b,
    )
    return second_block(
        x, w_in_2, rwkv_mu_2, rwkv_w0_2, rwkv_w2_2, rwkv_a0_2, rwkv_a2_2, rwkv_g2_2, rwkv_k_k_2,
        rwkv_k_a_2, rwkv_r_k_2, rwkv_ln_w_2, rwkv_ln_b_2, ssm_a_re_2, ssm_a_im_2, ssm_b_re_2,
        ssm_b_im_2, ssm_c_re_2, ssm_c_im_2, ssm_d_2, ssm_log_dt_2, ssm_glu_w_2, ssm_glu_b_2,
        w_up_rwkv_2, w_up_moba_2, w_up_ssm_2, gate_b_2, w_out_2, ln1_w_2, ln1_b_2,
        router_group_w_2, router_group_b_2, router_expert_w_2, router_expert_b_2,
        expert_w_gate_2, expert_w_up_2, expert_w_down_2, ln2_w_2, ln2_b_2,
    )


_drawn_inputs = setup_inputs


def setup_inputs(seed=0):
    import zlib

    import numpy as np

    out = dict(_drawn_inputs(seed))
    spreads = {}
    factors = {'attn_sinks': 8.0,
     'rwkv_w2_2': 4.504,
     'rwkv_a0_2': 5.219,
     'rwkv_k_k_2': 17.857,
     'rwkv_k_a_2': 3.344,
     'rwkv_ln_w_2': 4.49,
     'rwkv_ln_b_2': 16.306,
     'ssm_a_re_2': 200.0,
     'ssm_glu_b_2': 8.0,
     'gate_b_2': 5.072,
     'router_group_b_2': 12.861,
     'router_expert_b_2': 8.0,
     'ln2_b_2': 2.735,
     'ssm_a_im_2': 30.312,
     'ssm_b_re_2': 30.304,
     'ssm_b_im_2': 34.968,
     'ssm_c_re_2': 29.28,
     'ssm_c_im_2': 32.32,
     'ssm_log_dt_2': 27.4}
    for name, (base, spread) in spreads.items():
        noise = np.random.default_rng([zlib.crc32(name.encode()), seed]).standard_normal(out[name].shape)
        drawn = base * np.exp(spread * noise) if base else spread * noise
        out[name] = jnp.asarray(drawn.astype(out[name].dtype))
    for name, factor in factors.items():
        out[name] = (out[name] * factor).astype(out[name].dtype)
    return out
```

```python
from contextlib import ExitStack

import numpy as np
import concourse.bass as bass
from concourse import mybir

ALU = mybir.AluOpType
ACT = mybir.ActivationFunctionType
AX = mybir.AxisListType
F32 = mybir.dt.float32
I32 = mybir.dt.int32
U32 = mybir.dt.uint32

T = 256
D = 1024
DFF = 2816
NE1 = 8
NE2 = 32
ALPHA1 = 4.0 ** 0.25
ALPHA2 = 2.0 ** 0.25
LN_EPS = 1e-5
GN_EPS = 64e-5
NEG = -1e30
EH = float(np.exp(-0.5))
RING = 4
SLOT = 4096
TWO_PI = 2.0 * np.pi
PI_A = 6.28125
PI_B = float(np.float32(np.round((TWO_PI - PI_A) * 2.0 ** 24) / 2.0 ** 24 // 2.0 ** -20 * 2.0 ** -20))
PI_C = float(TWO_PI - PI_A - PI_B)
MAGIC = 12582912.0


def const_table():
    p = np.arange(128)
    parts = {}
    parts["ident"] = np.eye(128)
    parts["ones"] = np.ones((128, 128))
    same = lambda n: (p[:, None] // n) == (p[None, :] // n)
    parts["bones"] = same(64)
    parts["bmean"] = same(64) / 64.0
    rt = np.zeros((128, 128))
    for b in (0, 64):
        for m in range(8):
            rt[b + m + 8, b + m] = -1.0
            rt[b + m, b + m + 8] = 1.0
    parts["rot"] = rt
    inv = np.zeros(128)
    freq = np.float32(500000.0) ** (-np.arange(0, 16, 2, dtype=np.float32) / np.float32(16))
    for b in (0, 64):
        inv[b:b + 8] = freq
        inv[b + 8:b + 16] = freq
    parts["inv"] = inv[:, None]
    parts["eps"] = np.full((128, 1), LN_EPS)
    parts["epg"] = np.full((128, 1), GN_EPS)
    i = p[:, None]
    q = p[:, None]
    k1 = np.arange(128)[None, :]
    k2 = np.arange(256)[None, :]
    ok = lambda qq, kk: ((kk // 64) <= (qq // 64)) & ((kk // 64) >= (qq // 64) - 2)
    parts["swa"] = np.concatenate([np.where(ok(q, k1), 0, NEG), np.where(ok(q + 128, k2), 0, NEG)], 1)
    parts["caus"] = np.concatenate([np.where(k1 <= q, 0, NEG), np.where(k2 <= q + 128, 0, NEG)], 1)
    parts["dist"] = np.concatenate([np.where(k1 <= q, k1 - q, NEG), np.where(k2 <= q + 128, k2 - q - 128, NEG)], 1)
    j = p[None, :]
    ch = same(64)
    parts["mDl"] = (j < i) & same(16)
    parts["mDu"] = (i < j) & same(16)
    parts["mOu"] = (i < j) & ch & ~same(16)
    parts["mSu"] = (i < j) & ch
    parts["mIu"] = (i <= j) & ch
    parts["i64"] = np.concatenate([np.eye(64)] * 2, 0)
    parts["cmask"] = (j // 16 % 2) == (i // 64)
    parts["su"] = (i < j)
    parts["iota"] = np.broadcast_to(np.arange(128)[None, :], (128, 128))
    cols, at, off = [], 0, {}
    for n, a in parts.items():
        a = np.asarray(a, np.float32)
        off[n] = (at, a.shape[1])
        at += a.shape[1]
        cols.append(a)
    return np.ascontiguousarray(np.concatenate(cols, 1), np.float32), off


CT, COFF = const_table()

VEC = [("sink", 12), ("bf", 1), ("mu", 14), ("w0", 4), ("a0", 4), ("kk", 4), ("ka", 4), ("rk", 4),
       ("lnw", 4), ("lnb", 4), ("are", 16), ("aim", 16), ("ldt", 16), ("sd", 4), ("gb", 8),
       ("gateb", 24), ("br1", 8), ("br2", 36)]
VOFF = {}
_a = 0
for _n, _w in VEC:
    VOFF[_n] = (_a, _w)
    _a += _w
NVEC = _a


class Prog:

    def __init__(self, nc, ctx):
        self.nc, self.ctx = nc, ctx
        self.q = {e: [] for e in ("pe", "dve", "act", "pool", "sp")}
        self.sem = {e: ctx.enter_context(nc.semaphore("s_" + e)) for e in ("pe", "dve", "act", "pool")}
        self.n = {e: 0 for e in self.sem}
        self.seen = {e: {} for e in self.q}

    def wait(self, e, deps):
        for d in deps:
            if d is None:
                continue
            if isinstance(d, list):
                self.wait(e, d)
                continue
            s, v = d
            if self.seen[e].get(id(s), 0) < v:
                self.seen[e][id(s)] = v
                self.q[e].append(("w", s, v))

    def op(self, e, fn, *deps):
        if e in ("dve", "act") and self.n[e]:
            self.wait(e, [(self.sem[e], self.n[e])])
        self.wait(e, deps)
        self.n[e] += 1
        self.q[e].append(("i", fn, self.sem[e], 1))
        return (self.sem[e], self.n[e])

    def quiet(self, e, fn, *deps):
        self.wait(e, deps)
        self.q[e].append(("i", fn, None, 0))

    def dve(self, fn, *deps):
        return self.op("dve", fn, *deps)

    def act(self, fn, *deps):
        return self.op("act", fn, *deps)

    def pool(self, fn, *deps):
        return self.op("pool", fn, *deps)

    def mm(self, out, lhsT, rhs, start, stop, *deps):
        self.quiet("pe", lambda e: e.matmul(out, lhsT, rhs, start=start, stop=stop), *deps)

    def mml(self, out, lhsT, rhs, start, stop, *deps):
        return self.op("pe", lambda e: e.matmul(out, lhsT, rhs, start=start, stop=stop), *deps)

    def tr(self, out, in_, ident, *deps):
        return self.op("pe", lambda e: e.transpose(out, in_, ident), *deps)

    def dma(self, e, out, in_, sem, count, *deps):
        self.wait(e, deps)
        self.q[e].append(("i", lambda g: g.dma_start(out, in_), sem, 16))
        return (sem, count)

    def run(self, e):
        def go(g):
            for it in self.q[e]:
                if it[0] == "w":
                    g.wait_ge(it[1], it[2])
                else:
                    ins = it[1](g)
                    if it[2] is not None:
                        ins.then_inc(it[2], it[3])
        return go


class Ring:

    def __init__(self, P, buf, plan):
        self.P, self.buf, self.plan = P, buf, plan
        self.sems = [P.ctx.enter_context(P.nc.semaphore(f"s_w{i}")) for i in range(RING)]
        self.loaded = self.taken = 0
        for _ in range(RING):
            self.load(None)

    def load(self, after):
        i = self.loaded
        if i < len(self.plan):
            src, n = self.plan[i][1:]
            s = i % RING
            self.P.dma("sp", self.buf[:, s * SLOT:s * SLOT + n], src, self.sems[s], 16 * (i // RING + 1), after)
            self.loaded += 1

    def take(self, name):
        i = self.taken
        assert self.plan[i][0] == name, (self.plan[i][0], name)
        self.taken += 1
        s, n = i % RING, self.plan[i][2]
        return self.buf[:, s * SLOT:s * SLOT + n], (self.sems[s], 16 * (i // RING + 1))

    def release(self, tok):
        self.load(tok)


def build(nc, dr, out, dbg=None):
    ctx = ExitStack()
    with ctx:
        P = Prog(nc, ctx)
        dbg = dbg or {}

        def sb(name, n, dt=F32):
            return ctx.enter_context(nc.sbuf_tensor(name, [128, n], dt))

        def sem(name):
            return ctx.enter_context(nc.semaphore(name))

        ringbuf = sb("ringbuf", RING * SLOT)
        CST = sb("cst", CT.shape[1])
        VC = sb("vec", NVEC)
        X = sb("X", 2 * D)
        XT = sb("XT", 8 * T)
        Y = sb("Y", 2 * D)
        GB = sb("GB", 2 * D)
        AR = sb("arena", 23000)
        SM = sb("small", 1024)
        IX = sb("ix", 64, U32)
        POS = sb("pos", T, I32)
        PB = [ctx.enter_context(nc.psum_tensor(f"pb{i}", [128, 512], F32)) for i in range(8)]
        bfree = [None] * 8

        c = {n: CST[:, o:o + w] for n, (o, w) in COFF.items()}
        v = {n: VC[:, o:o + w] for n, (o, w) in VOFF.items()}
        ident = c["ident"]

        x3 = X[:, :].rearrange("p (t n) -> p t n", t=2)
        y3 = Y[:, :].rearrange("p (t n) -> p t n", t=2)
        xT = XT[:, :].rearrange("p (j t) -> p j t", j=8)

        def ar(at, *shape):
            n = int(np.prod(shape))
            assert at + n <= 23000, (at, n)
            a = AR[:, at:at + n]
            if len(shape) == 2:
                return a.rearrange("p (a b) -> p a b", a=shape[0])
            if len(shape) == 3:
                return a.rearrange("p (a b c) -> p a b c", a=shape[0], b=shape[1])
            return a

        dsem = sem("s_dbg") if dbg else None
        dcnt = [0]

        def dump(name, ap, *deps):
            if name in dbg:
                dcnt[0] += 16
                P.dma("sp", dbg[name], ap, dsem, dcnt[0], *deps)
                P.wait("sp", [(dsem, dcnt[0])])
                for e in ("pe", "dve", "act", "pool"):
                    P.wait(e, [(dsem, dcnt[0])])

        s_c, s_x, s_p, s_m = sem("s_c"), sem("s_x"), sem("s_p"), sem("s_m")
        t_x = P.dma("sp", x3, dr["x"].rearrange("a (t p) d -> p (a t) d", p=128), s_x, 16)
        t_c = P.dma("act", CST[:, :], dr["cst"], s_c, 16)
        s_v = sem("s_v")
        t_v = P.dma("act", VC[:, :], dr["vec"], s_v, 16)
        t_p = P.dma("act", POS[:, :], dr["pos"], s_p, 16)
        mem = ar(18900, 2, D)
        t_m = P.dma("act", mem, dr["mem"].rearrange("a (t p) d -> p (a t) d", p=128), s_m, 16)

        plan = []

        def add(name, n=None, order=None):
            a = dr[name]
            for i in (order if order is not None else range(a.shape[0])):
                plan.append((name, a[i], a.shape[2]))

        add("wkv", order=[0])
        add("swT")
        add("swk")
        add("swv")
        add("wo", order=[0, 1])
        add("fin")
        for i in range(6):
            n = SLOT if i < 5 else SLOT // 2
            plan.append(("fout", dr["fout"][i][:, 0:n], n))
        add("wkv", order=[1])
        add("foT")
        add("foqf")
        add("fov")
        add("fov2")
        add("wo", order=[2, 3])
        for e in range(NE1):
            for i in range(11):
                plan.append(("ein", dr["ein"][e, i], SLOT))
            for i in range(6):
                n = SLOT if i < 5 else SLOT // 2
                plan.append(("eout", dr["eout"][e, i][:, 0:n], n))
        add("u2")
        add("mqk2")
        add("mv2")
        add("z2")
        add("z2b")
        add("glu")
        for i in range(8):
            plan.append(("gate2", dr["gate2"][i], 3072))
            if i % 2 == 0:
                plan.append(("up2", dr["up2"][i // 2], 3072))
        add("wo2")
        for e in range(NE2):
            plan.append(("e2in", dr["e2in"][e], SLOT))
            plan.append(("e2out", dr["e2out"][e], 2048))
        ring = Ring(P, ringbuf, plan)

        s_g = sem("s_g")
        gcount = [0]

        def load_gb(i, after):
            gcount[0] += 16
            return P.dma("sp", GB[:, :], dr["gb"][i], s_g, gcount[0], after)

        def transpose_rows(dstT, src3, ready, banks, wait_dst=None, skip=0):
            toks = []
            for j2 in range(4):
                b = banks[j2 % len(banks)]
                for jj in range(2):
                    for tt in range(2):
                        j = 2 * j2 + jj
                        last = P.tr(PB[b][:, jj * 256 + tt * 128:jj * 256 + tt * 128 + 128],
                                    src3[:, tt, j * 128:(j + 1) * 128], ident, ready[tt], t_c, bfree[b])
                dst = dstT[:, 2 * j2:2 * j2 + 2, :]
                src = PB[b][:, :].rearrange("p (j t) -> p j t", j=2)
                if j2 % 2:
                    tk = P.act(lambda e, dst=dst, src=src: e.activation(dst, src, ACT.Copy), last, wait_dst)
                else:
                    tk = P.dve(lambda e, dst=dst, src=src: e.tensor_copy(dst, src), last, wait_dst)
                bfree[b] = tk
                toks.append(tk)
            return toks

        def tile_T(outp, w, kt, col, m, rT, *deps, kstride=None):
            for j in range(kt):
                f = P.mml if j == kt - 1 else P.mm
                tk = f(outp, w[:, j, col:col + m], rT[:, j, :], j == 0, j == kt - 1, *deps)
            return tk

        def rows(outp, aT, tt, w, kt, col, n, *deps):
            for j in range(kt):
                f = P.mml if j == kt - 1 else P.mm
                tk = f(outp, aT[:, j, tt * 128:(tt + 1) * 128], w[:, j, col:col + n], j == 0, j == kt - 1, *deps)
            return tk

        def evac(dst, src, tok, eng, scale=None, *deps):
            if eng == "act":
                return P.act(lambda e: e.activation(dst, src, ACT.Copy, scale=1.0 if scale is None else scale), tok, *deps)
            if scale is None:
                return P.dve(lambda e: e.tensor_copy(dst, src), tok, *deps)
            return P.dve(lambda e: e.tensor_scalar(dst, src, scale, None, ALU.mult), tok, *deps)

        def proj_T(name, w, kt, ncol, rT, rdeps, dsts, banks, scales=None):
            wap, wt = w
            w3 = wap.rearrange("p (j n) -> p j n", j=kt)
            toks = []
            for i, d in enumerate(dsts):
                b = banks[(i // 2) % len(banks)]
                o = (i % 2) * 256
                m = min(128, ncol - i * 128)
                tk = tile_T(PB[b][0:m, o:o + 256], w3, kt, i * 128, m, rT, wt, rdeps, bfree[b] if i % 2 == 0 else None)
                if i % 2 or i == len(dsts) - 1:
                    for k in range(i - i % 2, i + 1):
                        toks.append(evac(dsts[k], PB[b][0:m, (k % 2) * 256:(k % 2) * 256 + 256], tk,
                                         "act" if (i // 2) % 2 else "dve", scales[k] if scales else None))
                    bfree[b] = toks[-1]
            return toks, tk

        def layer_norm(alpha, acc, acc_toks, gbtok, final=False):
            st = SM[:, 0:24].rearrange("p (t h s) -> p t h s", t=2, h=2)
            mv = SM[:, 24:28].rearrange("p (t s) -> p t s", t=2)
            sd = SM[:, 28:30]
            nb = SM[:, 30:32]
            toks, bs = [], [[], []]
            for tt in range(2):
                for h in range(2):
                    a, at_ = acc(tt, h)
                    xs = x3[:, tt, h * 512:(h + 1) * 512]
                    ys = y3[:, tt, h * 512:(h + 1) * 512]
                    t1 = P.dve(lambda e, a=a, xs=xs, ys=ys: e.scalar_tensor_tensor(ys, xs, alpha, a, ALU.mult, ALU.add), at_)
                    acc_toks(tt, h, t1)
                    t2 = P.dve(lambda e, tt=tt, h=h, ys=ys: e.bn_stats(st[:, tt, h, :], ys), t1)
                    bs[tt].append(t2)
            for tt in range(2):
                t3 = P.dve(lambda e, tt=tt: e.bn_aggr(mv[:, tt, :], st[:, tt, :, :]), bs[tt])
                t4 = P.act(lambda e, tt=tt: e.activation(sd[:, tt:tt + 1], mv[:, tt, 1:2], ACT.Sqrt, bias=c["eps"]), t3, t_c)
                t5 = P.dve(lambda e, tt=tt: e.reciprocal(sd[:, tt:tt + 1], sd[:, tt:tt + 1]), t4)
                t6 = P.dve(lambda e, tt=tt: e.tensor_scalar(y3[:, tt, :], y3[:, tt, :], mv[:, tt, 0:1], sd[:, tt:tt + 1],
                                                            ALU.subtract, ALU.mult), t5, t3)
                t7 = P.dve(lambda e, tt=tt: e.tensor_tensor(y3[:, tt, :], y3[:, tt, :], GB[:, 0:D], ALU.mult), t6, gbtok)
                t8 = P.dve(lambda e, tt=tt: e.tensor_tensor(x3[:, tt, :], y3[:, tt, :], GB[:, D:2 * D], ALU.add), t7)
                toks.append(t8)
            return toks

        def attention(heads, wbuf):
            S = [ar(wbuf + 512 * i, 512) for i in range(3)]
            PT = [ar(wbuf + 1536 + 512 * i, 512) for i in range(2)]
            n = len(heads)
            st = [dict() for _ in heads]
            sfree, ptfree = [None] * 3, [None] * 2
            stat = SM[:, 64:64 + 8 * 16].rearrange("p (h s) -> p h s", h=16)
            fin = []

            def A(i):
                h, s = heads[i], st[i]
                b = i % 2
                full = h["kind"] == "mem"
                w0 = 256 if full else 128
                s["w0"], s["wd"] = w0, w0 + 256
                for qt in range(2):
                    o = PB[b][:, 0:w0] if qt == 0 else PB[b][:, w0:w0 + 256]
                    kw = w0 if qt == 0 else 256
                    more = "cq" in h
                    f = P.mm if more else P.mml
                    tk = f(o, h["q"][:, qt * 128:(qt + 1) * 128], h["k"][:, 0:kw], True, not more, h["deps"], bfree[b])
                    if more:
                        tk = P.mml(o, h["cq"][:, qt * 128:(qt + 1) * 128], h["ck"][:, 0:kw], False, True)
                s["A"] = tk

            def B(i):
                h, s = heads[i], st[i]
                b, w0, wd = i % 2, s["w0"], s["wd"]
                sb_, hs = S[i % 3], stat[:, i % 16, :]
                src = PB[b]
                if h["kind"] == "mem":
                    t1 = s["A"]
                    srcs = PB[b]
                else:
                    if h["kind"] == "moba":
                        t1 = P.dve(lambda e: e.scalar_tensor_tensor(sb_[:, 0:wd], c["dist"], h["slope"], src[:, 0:wd],
                                                                    ALU.mult, ALU.add), s["A"], sfree[i % 3], t_c)
                    else:
                        mk = c["swa"] if h["kind"] == "swa" else c["caus"]
                        t1 = P.dve(lambda e: e.tensor_tensor(sb_[:, 0:wd], src[:, 0:wd], mk, ALU.add), s["A"], sfree[i % 3], t_c)
                    bfree[b] = t1
                    srcs = sb_
                t2 = P.dve(lambda e: e.tensor_reduce(hs[:, 0:1], srcs[:, 0:w0], AX.X, ALU.max, negate=True), t1)
                t2 = P.dve(lambda e: e.tensor_reduce(hs[:, 1:2], srcs[:, w0:wd], AX.X, ALU.max, negate=True), t1)
                if "sink" in h:
                    sk = v["sink"][:, h["sink"]:h["sink"] + 1]
                    t2 = P.dve(lambda e: e.tensor_scalar(hs[:, 6:7], sk, -1.0, None, ALU.mult), t2, t_v)
                    t2 = P.dve(lambda e: e.tensor_scalar(hs[:, 0:2], hs[:, 0:2], hs[:, 6:7], None, ALU.min), t2)
                    t3 = P.dve(lambda e: e.tensor_scalar(hs[:, 4:6], hs[:, 0:2], sk, None, ALU.add), t2)
                    t4 = P.act(lambda e: e.activation(hs[:, 4:6], hs[:, 4:6], ACT.Exp), t3)
                    s["sk"] = t4
                ta = P.act(lambda e: e.activation(sb_[:, 0:w0], srcs[:, 0:w0], ACT.Exp, bias=hs[:, 0:1], accum_out=hs[:, 2:3]), t2, sfree[i % 3])
                tb = P.act(lambda e: e.activation(sb_[:, w0:wd], srcs[:, w0:wd], ACT.Exp, bias=hs[:, 1:2], accum_out=hs[:, 3:4]), t2)
                if h["kind"] == "mem":
                    bfree[b] = tb
                s["B"] = tb

            def C(i):
                h, s = heads[i], st[i]
                w0, wd = s["w0"], s["wd"]
                sb_, hs = S[i % 3], stat[:, i % 16, :]
                t = s["B"]
                if "sink" in h:
                    t = P.dve(lambda e: e.tensor_tensor(hs[:, 2:4], hs[:, 2:4], hs[:, 4:6], ALU.add), t, s["sk"])
                t = P.dve(lambda e: e.reciprocal(hs[:, 2:4], hs[:, 2:4]), t)
                P.dve(lambda e: e.tensor_scalar(sb_[:, 0:w0], sb_[:, 0:w0], hs[:, 2:3], None, ALU.mult), t)
                s["C"] = P.dve(lambda e: e.tensor_scalar(sb_[:, w0:wd], sb_[:, w0:wd], hs[:, 3:4], None, ALU.mult), t)

            def Dd(i):
                h, s = heads[i], st[i]
                w0, wd = s["w0"], s["wd"]
                sb_, b = S[i % 3], 2 + i % 2
                pt = PT[i % 2]
                P.tr(PB[b][:, 0:128], sb_[:, 0:128], ident, s["C"], bfree[b])
                P.tr(PB[b][:, 128:256], sb_[:, w0:w0 + 128], ident)
                if w0 == 256:
                    P.tr(PB[b][:, 256:384], sb_[:, 128:256], ident)
                tk = P.tr(PB[b][:, wd - 128:wd], sb_[:, w0 + 128:w0 + 256], ident)
                sfree[i % 3] = tk
                s["D"] = evac(pt[:, 0:wd], PB[b][:, 0:wd], tk, "act" if i % 2 else "dve", None, ptfree[i % 2])
                bfree[b] = s["D"]

            def Ee(i):
                h, s = heads[i], st[i]
                w0, wd = s["w0"], s["wd"]
                b, base = 4 + (i // 2) % 2, h["base"]
                pt = PT[i % 2]
                o = PB[b][base:base + 64, :]
                P.mm(o[:, 0:256], h["v"][0], pt[:, 0:256], True, False, s["D"], h["vdeps"], bfree[b] if i % 2 == 0 else None)
                q0 = 0 if w0 == 256 else 128
                tk = P.mml(o[:, q0:256], h["v"][1], pt[:, 256:wd], False, True)
                ptfree[i % 2] = tk
                if i % 2:
                    e = evac(h["out"], PB[b][:, 0:256], tk, "dve" if i % 4 == 1 else "act")
                    bfree[b] = e
                    fin.append(e)

            for i in range(n + 3):
                if i < n:
                    A(i)
                    B(i)
                if 0 <= i - 1 < n:
                    C(i - 1)
                if 0 <= i - 2 < n:
                    Dd(i - 2)
                if 0 <= i - 3 < n:
                    Ee(i - 3)
            return fin

        def sincos(ang, sn, cs, tmp, tok):
            t = P.dve(lambda e: e.tensor_scalar(tmp, ang, 1.0 / TWO_PI, MAGIC, ALU.mult, ALU.add), tok)
            t = P.dve(lambda e: e.tensor_scalar(tmp, tmp, MAGIC, None, ALU.subtract), t)
            for k in (PI_A, PI_B, PI_C):
                t = P.dve(lambda e, k=k: e.scalar_tensor_tensor(ang, tmp, -k, ang, ALU.mult, ALU.add), t)
            t = P.dve(lambda e: e.tensor_scalar(ang, ang, 3.1415925, -3.1415925, ALU.min, ALU.max), t)
            ts = P.act(lambda e: e.activation(sn, ang, ACT.Sin), t)
            tc = P.act(lambda e: e.activation(cs, ang, ACT.Sin, scale=0.5), t)
            tc = P.dve(lambda e: e.tensor_tensor(cs, cs, cs, ALU.mult), tc)
            tc = P.dve(lambda e: e.tensor_scalar(cs, cs, -2.0, 1.0, ALU.mult, ALU.add), tc)
            return [ts, tc]

        def w_out(name, mixT, deps):
            tk = {}
            for h in range(2):
                w = ring.take(name)
                w3 = w[0].rearrange("p (j n) -> p j n", j=8)
                for tt in range(2):
                    b = 2 * h + tt
                    tk[(tt, h)] = rows(PB[b][:, :], mixT, tt, w3, 8, 0, 512, w[1], deps, bfree[b])
                ring.release(tk[(1, h)])
            return tk

        def add_norm(alpha, tk, gb):
            def acc(tt, h):
                return PB[2 * h + tt][:, :], tk[(tt, h)]

            def done(tt, h, t):
                bfree[2 * h + tt] = t

            return layer_norm(alpha, acc, done, gb)

        def ffn(kin, kout, nf, hT, xdeps, nin, hfree, accb, obanks=(0, 1, 2, 3), between=None):
            npair = nin
            f = 0
            toks = []
            while f < nf:
                w = ring.take(kin)
                w3 = w[0].rearrange("p (j n) -> p j n", j=8)
                for i in range(npair):
                    b = accb[f % len(accb)]
                    ta = tile_T(PB[b][:, 0:256], w3, 8, i * 128, 128, xT, w[1], xdeps, bfree[b])
                    tb = tile_T(PB[b][:, 256:512], w3, 8, (npair + i) * 128, 128, xT)
                    dst = hT[:, f, :]
                    t1 = P.act(lambda e, dst=dst, b=b: e.activation(dst, PB[b][:, 0:256], ACT.Silu), tb, hfree)
                    t2 = P.dve(lambda e, dst=dst, b=b: e.tensor_tensor(dst, dst, PB[b][:, 256:512], ALU.mult), t1, tb)
                    bfree[b] = t2
                    toks.append(t2)
                    f += 1
                ring.release(tb)
            tk = {}
            f = 0
            while f < nf:
                w = ring.take(kout)
                nk = w[0].shape[1] // 1024
                w3 = w[0].rearrange("p (j n) -> p j n", j=nk)
                for j in range(nk):
                    for tt in range(2):
                        for h in range(2):
                            b = obanks[2 * h + tt]
                            g = P.mml if (f == nf - 1 or j == nk - 1) else P.mm
                            r = g(PB[b][:, :], hT[:, f, tt * 128:(tt + 1) * 128], w3[:, j, h * 512:(h + 1) * 512],
                                  f == 0, f == nf - 1, w[1], toks[f], bfree[b] if f == 0 else None)
                            if f == nf - 1:
                                tk[(tt, h)] = r
                    f += 1
                ring.release(r)
            return tk, r

        qT = ar(0, 6, T)
        kT = ar(1536, 6, T)
        qcT = ar(3072, 2, T)
        Vn = ar(3584, 2, 768)
        kmT = ar(5120, 2, T)
        vmn = ar(5632, 2, T)
        mixT = ar(6144, 8, T)
        memT = ar(8192, 8, T)
        WB = 10240
        rC, rS = ar(12800, T), ar(13056, T)
        rt1, rt2 = ar(13312, T), ar(13568, T)
        cumT, A2, B2 = ar(13824, T), ar(14080, 12, T), ar(17152, 12, T)

        tmT = transpose_rows(memT, mem, [t_m, t_m], [4, 5])
        txT = transpose_rows(xT, x3, [t_x, t_x], [4, 5])

        t = P.dve(lambda e: e.tensor_copy(rt1, POS[:, :]), t_p)
        t = P.dve(lambda e: e.tensor_scalar(rt1, rt1, c["inv"], None, ALU.mult), t, t_c)
        t_rope = sincos(rt1, rS, rC, rt2, t)

        def mem_kv():
            w = ring.take("wkv")
            w3 = w[0].rearrange("p (j n) -> p j n", j=8)
            tk, _ = [], None
            for i in range(2):
                b = 6
                p_ = tile_T(PB[b][:, i * 256:i * 256 + 256], w3, 8, i * 128, 128, memT, w[1], tmT, bfree[b] if i == 0 else None, wfree[0])
            for i in range(2):
                tk.append(evac(kmT[:, i, :], PB[b][:, i * 256:i * 256 + 256], p_, "act", None, wfree[0]))
            bfree[6] = tk[-1]
            for tt in range(2):
                b = 7
                p_ = rows(PB[b][:, tt * 256:tt * 256 + 256], memT, tt, w3, 8, 256, 256, bfree[b] if tt == 0 else None)
            for tt in range(2):
                tk.append(evac(vmn[:, tt, :], PB[b][:, tt * 256:tt * 256 + 256], p_, "dve"))
            bfree[7] = tk[-1]
            ring.release(p_)
            return tk

        wfree = [None]
        t_kv = mem_kv()

        def take_T(name, dsts, scales, ncol, banks, rdeps):
            w = ring.take(name)
            toks, last = proj_T(name, w, 8, ncol, xT, rdeps, dsts, banks, scales)
            ring.release(last)
            return toks

        tq = take_T("swT", [qT[:, i, :] for i in range(4)], [0.125] * 4, 512, [4, 5], txT)
        tq2 = take_T("swT", [qT[:, 4, :], qT[:, 5, :], qcT[:, 0, :], qcT[:, 1, :]], [0.125] * 4, 512, [4, 5], txT)
        w = ring.take("swk")
        tk_, last = proj_T("swk", w, 8, 384, xT, txT, [kT[:, i, :] for i in range(3)], [4, 5])
        ring.release(last)
        tq = tq + tq2[0:2]
        tqc = tq2[2:4]

        def rope(ap, tok, b):
            p_ = P.mml(PB[b][:, 0:256], c["rot"], ap, True, True, tok, t_c, bfree[b])
            i1 = P.dve(lambda e: e.tensor_tensor(rt1, PB[b][:, 0:256], rS, ALU.mult), p_, t_rope)
            bfree[b] = i1
            i2 = P.dve(lambda e: e.tensor_tensor(ap, ap, rC, ALU.mult), p_)
            return P.dve(lambda e: e.tensor_tensor(ap, ap, rt1, ALU.add), i1, i2)

        tq = [rope(qT[:, i, :], tq[i], 4 + i % 2) for i in range(6)]
        tk_ = [rope(kT[:, i, :], tk_[i], 4 + i % 2) for i in range(3)]
        w = ring.take("swv")
        w3 = w[0].rearrange("p (j n) -> p j n", j=8)
        tv = []
        for tt in range(2):
            p_ = rows(PB[6 + tt][:, 0:192], xT, tt, w3, 8, 0, 192, w[1], bfree[6 + tt])
            bfree[6 + tt] = evac(Vn[:, tt, 0:192], PB[6 + tt][:, 0:192], p_, "act" if tt else "dve")
            tv.append(bfree[6 + tt])
        ring.release(p_)
        heads = []
        for h in range(12):
            b = 64 * (h % 2)
            g = h // 4
            heads.append(dict(kind="swa", q=qT[b:b + 64, h // 2, :], k=kT[b:b + 64, g, :], base=b, sink=h,
                              deps=[tq[h // 2], tk_[g]], v=[Vn[:, 0, g * 64:g * 64 + 64], Vn[:, 1, g * 64:g * 64 + 64]],
                              vdeps=tv, out=mixT[:, h // 2, :]))

        def mem_heads():
            r = []
            for h in range(4):
                b = 64 * (h % 2)
                r.append(dict(kind="mem", q=qcT[b:b + 64, h // 2, :], k=kmT[b:b + 64, h // 2, :], base=b,
                              deps=[tqc[h // 2], t_kv[h // 2]], v=[vmn[:, 0, h * 64:h * 64 + 64], vmn[:, 1, h * 64:h * 64 + 64]],
                              vdeps=t_kv, out=mixT[:, 6 + h // 2, :]))
            return r

        t_gb = load_gb(0, None)
        fin = attention(heads + mem_heads(), WB)
        dump("mix0", mixT, fin)
        tk = w_out("wo", mixT, fin)
        tx = add_norm(ALPHA1, tk, t_gb)
        dump("ln0", x3, tx)
        t_gb = load_gb(1, tx)
        txT = transpose_rows(xT, x3, tx, [4, 5])
        hT = ar(10240, 22, T)
        ftk, _ = ffn("fin", "fout", 22, hT, txT, 2, fin, [4, 5, 6, 7])
        tx = add_norm(ALPHA1, ftk, t_gb)
        dump("ln1", x3, tx)
        t_gb = load_gb(2, tx)
        txT = transpose_rows(xT, x3, tx, [4, 5])
        hdone = [ftk[(1, 1)]]

        wfree[0] = tx
        t_kv = mem_kv()
        tq, tk_ = [], []
        for i in range(3):
            ds = [(qT[:, j, :] if j < 6 else kT[:, j - 6, :]) for j in range(4 * i, 4 * i + 4)]
            sc = [(0.125 if j < 6 else None) for j in range(4 * i, 4 * i + 4)]
            tq += take_T("foT", ds, sc, 512, [4, 5], txT)
        tk_ = tq[6:]
        w = ring.take("foqf")
        w3 = w[0].rearrange("p (j n) -> p j n", j=8)
        toks, last = proj_T("foqf", w, 8, 256, xT, txT, [qcT[:, 0, :], qcT[:, 1, :]], [4], [0.125] * 2)
        tqc = toks
        pf = tile_T(PB[5][0:12, 0:256], w3, 8, 256, 12, xT, bfree[5])
        ring.release(pf)
        f12, e12 = rt1[0:12, :], rt2[0:12, :]
        cum12, g12 = cumT[0:12, :], rC[0:12, :]
        t = P.dve(lambda e: e.tensor_scalar(f12, PB[5][0:12, 0:256], v["bf"][0:12, :], None, ALU.add), pf, hdone)
        bfree[5] = t
        ta = P.act(lambda e: e.activation(e12, f12, ACT.Abs), t)
        ta = P.act(lambda e: e.activation(e12, e12, ACT.Exp, scale=-1.0), ta)
        ta = P.dve(lambda e: e.tensor_scalar(e12, e12, 1.0, None, ALU.add), ta)
        ta = P.act(lambda e: e.activation(e12, e12, ACT.Ln), ta)
        t = P.dve(lambda e: e.tensor_scalar(f12, f12, 0.0, None, ALU.min), t)
        t = P.dve(lambda e: e.tensor_tensor(f12, f12, e12, ALU.subtract), t, ta)
        t1 = P.dve(lambda e: e.memset(g12, 1.0), hdone)
        t1 = P.dve(lambda e: e.tensor_tensor_scan(cum12, g12, f12, 0.0, ALU.mult, ALU.add), t, t1)
        t2 = P.dve(lambda e: e.tensor_scalar(f12, cum12, -1.0, None, ALU.mult), t1)
        m1 = P.dve(lambda e: e.memset(A2[0:2, :, :], 1.0), hdone)
        m2 = P.dve(lambda e: e.memset(B2[0:2, :, :], 1.0), hdone)
        s_ab = sem("s_ab")
        tab = P.dma("act", A2[0:1, :, :], cum12, s_ab, 16, t1, m1)
        s_ab2 = sem("s_ab2")
        tab2 = P.dma("act", B2[1:2, :, :], f12, s_ab2, 16, t2, m2)
        tv = []
        for ci, (n0, nn) in enumerate(((0, 512), (512, 256))):
            w = ring.take("fov" if ci == 0 else "fov2")
            w3 = w[0].rearrange("p (j n) -> p j n", j=8)
            for tt in range(2):
                b = 6 + tt
                p_ = rows(PB[b][:, 0:nn], xT, tt, w3, 8, 0, nn, w[1], bfree[b])
                bfree[b] = evac(Vn[:, tt, n0:n0 + nn], PB[b][:, 0:nn], p_, "act" if tt else "dve")
                tv.append(bfree[b])
            ring.release(p_)
        heads = []
        for h in range(12):
            b = 64 * (h % 2)
            heads.append(dict(kind="fox", q=qT[b:b + 64, h // 2, :], k=kT[b:b + 64, h // 2, :], base=b,
                              cq=A2[0:2, h, :], ck=B2[0:2, h, :], deps=[tq[h // 2], tk_[h // 2], tab, tab2],
                              v=[Vn[:, 0, h * 64:h * 64 + 64], Vn[:, 1, h * 64:h * 64 + 64]],
                              vdeps=tv, out=mixT[:, h // 2, :]))
        fin = attention(heads + mem_heads(), WB)
        dump("mix1", mixT, fin)
        tk = w_out("wo", mixT, fin)
        tx = add_norm(ALPHA1, tk, t_gb)
        dump("ln2", x3, tx)
        t_gb = load_gb(3, tx)
        txT = transpose_rows(xT, x3, tx, [4, 5])

        def top2(L, n, oh, g, tok, base):
            mx = SM[:, base:base + 8]
            ixf = SM[:, base + 8:base + 16]
            ix = IX[:, 0:8]
            df = SM[:, base + 16:base + 17]
            t = P.dve(lambda e: e.max(mx, L), tok)
            t = P.dve(lambda e: e.max_index(ix, mx, L), t)
            t = P.dve(lambda e: e.tensor_copy(ixf, ix), t)
            iota = c["iota"][:, 0:n]
            P.dve(lambda e: e.tensor_scalar(oh[0], iota, ixf[:, 0:1], None, ALU.is_equal), t)
            to = P.dve(lambda e: e.tensor_scalar(oh[1], iota, ixf[:, 1:2], None, ALU.is_equal), t)
            t = P.dve(lambda e: e.tensor_tensor(df, mx[:, 1:2], mx[:, 0:1], ALU.subtract), t)
            ta = P.act(lambda e: e.activation(df, df, ACT.Exp), t)
            tb = P.dve(lambda e: e.tensor_scalar(g[:, 0:1], df, 1.0, None, ALU.add), ta)
            tb = P.dve(lambda e: e.reciprocal(g[:, 0:1], g[:, 0:1]), tb)
            tb = P.dve(lambda e: e.tensor_tensor(g[:, 1:2], g[:, 0:1], df, ALU.mult), tb)
            return [to, tb]

        wr1 = dr["wr1"]
        s_r = sem("s_r")
        RW = ar(0, 8, 36)
        t_r = P.dma("act", RW[:, :, 0:8], dr["wr1"], s_r, 16, fin)
        G1 = ar(512, 2, 8)
        L1 = ar(544, 2, 8)
        O1 = ar(576, 2, 2, 8)
        gt = ar(640, 2, 2)
        tgate = []
        for tt in range(2):
            p_ = rows(PB[6 + tt][:, 0:8], xT, tt, RW[:, :, 0:8], 8, 0, 8, t_r, txT, bfree[6 + tt])
            t = P.dve(lambda e, tt=tt: e.tensor_tensor(L1[:, tt, :], PB[6 + tt][:, 0:8], v["br1"], ALU.add), p_)
            bfree[6 + tt] = t
            tt2 = top2(L1[:, tt, :], 8, [O1[:, tt, 0, :], O1[:, tt, 1, :]], gt[:, tt, :], t, 256 + 32 * tt)
            t = P.dve(lambda e, tt=tt: e.tensor_scalar(G1[:, tt, :], O1[:, tt, 0, :], gt[:, tt, 0:1], None, ALU.mult), tt2)
            t = P.dve(lambda e, tt=tt: e.scalar_tensor_tensor(G1[:, tt, :], O1[:, tt, 1, :], gt[:, tt, 1:2], G1[:, tt, :],
                                                              ALU.mult, ALU.add), t)
            tgate.append(t)
        dump("g1", G1, tgate)

        def moe_dense(kin, kout, ne, nf, G, gdeps, hTs, xd, ta0):
            acct = [[None, None], [None, None]]
            hfree = [None, None]
            for e_ in range(ne):
                tk, r = ffn(kin, kout, nf, hTs[e_ % 2], xd, 2, hfree[e_ % 2], [4, 5, 6, 7])
                hfree[e_ % 2] = r
                for tt in range(2):
                    for h in range(2):
                        ys = y3[:, tt, h * 512:(h + 1) * 512]
                        b = 2 * h + tt
                        gcol = G[:, tt, e_:e_ + 1]
                        if e_ == 0:
                            t = P.dve(lambda e, ys=ys, b=b, gcol=gcol: e.tensor_scalar(ys, PB[b][:, :], gcol, None, ALU.mult),
                                      tk[(tt, h)], gdeps, ta0)
                        else:
                            t = P.dve(lambda e, ys=ys, b=b, gcol=gcol: e.scalar_tensor_tensor(ys, PB[b][:, :], gcol, ys, ALU.mult, ALU.add),
                                      tk[(tt, h)], acct[tt][h])
                        bfree[b] = t
                        acct[tt][h] = t
            return acct

        hTs = [ar(1024, 22, T), ar(1024 + 5632, 22, T)]
        acct = moe_dense("ein", "eout", NE1, 22, G1, tgate, hTs, txT, tx)
        tx = layer_norm(ALPHA1, lambda tt, h: (y3[:, tt, h * 512:(h + 1) * 512], acct[tt][h]), lambda *a: None, t_gb)
        dump("ln3", x3, tx)
        t_gb = load_gb(4, tx)
        txT = transpose_rows(xT, x3, tx, [4, 5])
        free0 = tx

        yaT, ybT, ycT = ar(0, 4, T), ar(1024, 4, T), ar(2048, 4, T)
        uT = ar(3072, 4, T)
        tu = take_T("u2", [uT[:, i, :] for i in range(4)], None, 512, [4, 5], [txT, free0])

        def s5():
            B0 = 4096
            CS, SN = ar(B0, 16, T), ar(B0 + 4096, 16, T)
            bre, bim = ar(B0 + 8192, 16, 16), ar(B0 + 8448, 16, 16)
            cre, cim = ar(B0 + 8704, 4, 64), ar(B0 + 8960, 4, 64)
            Z = ar(B0 + 9216, 2, 512)
            BBt = ar(B0 + 10240, 2, 512)
            CTt = ar(B0 + 11264, 2, 512)
            s = SM[:, 320:320 + 16 * 14].rearrange("p (k g) -> p k g", k=14)
            dt, th, mag, co, si, t0, t1_, t2_, cr, ci, den, lr, li, x4 = [s[:, k, :] for k in range(14)]
            tmp = [ar(B0 + 12288 + 256 * i, T) for i in range(12)]
            s_b, s_cc = sem("s_b5"), sem("s_c5")
            tb_ = P.dma("act", ar(B0 + 8192, 512), dr["s5b"], s_b, 16, free0)
            tc_ = P.dma("act", ar(B0 + 8704, 512), dr["s5c"], s_cc, 16, free0)
            t = P.act(lambda e: e.activation(dt, v["ldt"], ACT.Exp), free0)
            tth = P.dve(lambda e: e.tensor_tensor(th, v["aim"], dt, ALU.mult), t)
            tm = P.dve(lambda e: e.tensor_tensor(mag, v["are"], dt, ALU.mult), t)
            tm = P.act(lambda e: e.activation(mag, mag, ACT.Exp), tm)
            tsc = sincos(th, si, co, t0, tth)
            t = P.dve(lambda e: e.tensor_tensor(lr, mag, co, ALU.mult), tm, tsc)
            tl = P.dve(lambda e: e.tensor_scalar(lr, lr, -1.0, None, ALU.add), t)
            tli = P.dve(lambda e: e.tensor_tensor(li, mag, si, ALU.mult), tm, tsc)
            ta = P.dve(lambda e: e.tensor_tensor(den, v["are"], v["are"], ALU.mult))
            tb = P.dve(lambda e: e.tensor_tensor(t0, v["aim"], v["aim"], ALU.mult), tsc)
            ta = P.dve(lambda e: e.tensor_tensor(den, den, t0, ALU.add), ta, tb)
            tden = P.dve(lambda e: e.reciprocal(den, den), ta)
            a = P.dve(lambda e: e.tensor_tensor(t0, lr, v["are"], ALU.mult), tl, ta)
            b = P.dve(lambda e: e.tensor_tensor(t1_, li, v["aim"], ALU.mult), tli)
            a = P.dve(lambda e: e.tensor_tensor(cr, t0, t1_, ALU.add), a, b)
            tcr = P.dve(lambda e: e.tensor_tensor(cr, cr, den, ALU.mult), a, tden)
            b = P.dve(lambda e: e.tensor_tensor(t2_, li, v["are"], ALU.mult), tli)
            d = P.dve(lambda e: e.tensor_tensor(x4, lr, v["aim"], ALU.mult), tl)
            b = P.dve(lambda e: e.tensor_tensor(ci, t2_, x4, ALU.subtract), b, d)
            tci = P.dve(lambda e: e.tensor_tensor(ci, ci, den, ALU.mult), b, tden)
            bc = lambda a_: a_.unsqueeze(2).to_broadcast([128, 16, 16])
            w1, w2 = ar(B0 + 12288, 16, 16), ar(B0 + 12544, 16, 16)
            tz = P.dve(lambda e: e.memset(Z, 0.0), free0)
            zt = []
            for k, (m1, m2, op) in enumerate(((cr, ci, ALU.subtract), (ci, cr, ALU.add))):
                t = P.dve(lambda e, m1=m1: e.tensor_tensor(w1, bre, bc(m1), ALU.mult), tb_, tcr, tci, zt)
                t2 = P.dve(lambda e, m2=m2: e.tensor_tensor(w2, bim, bc(m2), ALU.mult), tb_, zt)
                for g in range(2):
                    r = slice(64 * g, 64 * g + 64)
                    dst = Z[:, k, :].rearrange("p (t h) -> p t h", t=16)[r, :, 16 * g:16 * g + 16]
                    zt.append(P.dve(lambda e, dst=dst, r=r, op=op: e.tensor_tensor(dst, w1[r], w2[r], op), t, t2, tz))
            for k in range(2):
                for q in range(4):
                    tk = P.tr(PB[6 + k][:, q * 128:q * 128 + 128], Z[:, k, q * 128:q * 128 + 128], ident, zt, bfree[6 + k])
                bfree[6 + k] = evac(BBt[:, k, :], PB[6 + k][:, :], tk, "act")
            tbb = [bfree[6], bfree[7]]
            dup = ar(B0 + 12800, 128)
            tct = []
            last = None
            for k, src in enumerate((cre, cim)):
                for q in range(4):
                    d1 = P.dve(lambda e, q=q, src=src: e.tensor_copy(dup[:, 0:64], src[:, q, :]), tc_, last)
                    d2 = P.dve(lambda e, q=q, src=src: e.tensor_copy(dup[:, 64:128], src[:, q, :]), last)
                    last = P.tr(PB[6 + k][:, q * 128:q * 128 + 128], dup, ident, d1, d2, bfree[6 + k])
                mk = c["cmask"].unsqueeze(1).to_broadcast([128, 4, 128])
                t = P.dve(lambda e, k=k, mk=mk: e.scalar_tensor_tensor(
                    CTt[:, k, :].rearrange("p (q m) -> p q m", q=4), PB[6 + k][:, :].rearrange("p (q m) -> p q m", q=4),
                    1.0 if k == 0 else -1.0, mk, ALU.mult, ALU.mult), last)
                bfree[6 + k] = t
                tct.append(t)
            a = P.dve(lambda e: e.tensor_copy(CS[:, :, 0], co), tsc, free0)
            b = P.dve(lambda e: e.tensor_copy(SN[:, :, 0], si), tsc)
            tt_ = [a, b]
            n = 1
            p4 = [ar(B0 + 12288, 16, 128), ar(B0 + 14336, 16, 128)]
            while n < 256:
                cn = CS[:, :, n - 1:n].to_broadcast([128, 16, n])
                sn_ = SN[:, :, n - 1:n].to_broadcast([128, 16, n])
                m1, m2 = p4[0][:, :, 0:n], p4[1][:, :, 0:n]
                lo, hi = slice(0, n), slice(n, 2 * n)
                a = P.dve(lambda e, m1=m1, lo=lo, cn=cn: e.tensor_tensor(m1, CS[:, :, lo], cn, ALU.mult), tt_, zt, tbb, tct)
                b = P.dve(lambda e, m2=m2, lo=lo, sn_=sn_: e.tensor_tensor(m2, SN[:, :, lo], sn_, ALU.mult), tt_)
                a2 = P.dve(lambda e, m1=m1, m2=m2, hi=hi: e.tensor_tensor(CS[:, :, hi], m1, m2, ALU.subtract), a, b)
                a = P.dve(lambda e, m1=m1, lo=lo, sn_=sn_: e.tensor_tensor(m1, CS[:, :, lo], sn_, ALU.mult), a2)
                b = P.dve(lambda e, m2=m2, lo=lo, cn=cn: e.tensor_tensor(m2, SN[:, :, lo], cn, ALU.mult), a2)
                b2 = P.dve(lambda e, m1=m1, m2=m2, hi=hi: e.tensor_tensor(SN[:, :, hi], m1, m2, ALU.add), a, b)
                tt_ = [a2, b2]
                n *= 2
            hfree = [None, None]
            ydone = []
            mulg = lambda o, a_, b_, *d: P.dve(lambda e: e.tensor_tensor(o, a_, b_, ALU.mult), *d)
            addg = lambda o, a_, b_, op, *d: P.dve(lambda e: e.tensor_tensor(o, a_, b_, op), *d)
            for i in range(16):
                q, r = i // 4, 32 * (i % 4)
                b = 6 + i % 2
                k6 = i % 2
                m1, m2, zr, zi, hr, hi_ = tmp[6 * k6:6 * k6 + 6]
                ub = uT[r:r + 32, q, :]
                P.mm(PB[b][:, 0:256], BBt[r:r + 32, 0, q * 128:q * 128 + 128], ub, True, True, tbb, tu, bfree[b])
                tk = P.mml(PB[b][:, 256:512], BBt[r:r + 32, 1, q * 128:q * 128 + 128], ub, True, True)
                br_, bi_ = PB[b][:, 0:256], PB[b][:, 256:512]
                Ci, Si = CS[:, i, :], SN[:, i, :]
                a = mulg(m1, br_, Ci, tk, tt_, hfree[k6])
                d = mulg(m2, bi_, Si, tk)
                t1 = addg(zr, m1, m2, ALU.add, a, d)
                a = mulg(m1, bi_, Ci, t1)
                d = mulg(m2, br_, Si, t1)
                bfree[b] = [a, d]
                t2 = addg(zi, m1, m2, ALU.subtract, a, d)
                mg = mag[:, i:i + 1].to_broadcast([128, 256])
                t1 = P.dve(lambda e, zr=zr, mg=mg: e.tensor_tensor_scan(zr, mg, zr, 0.0, ALU.mult, ALU.add), t1, tm)
                t2 = P.dve(lambda e, zi=zi, mg=mg: e.tensor_tensor_scan(zi, mg, zi, 0.0, ALU.mult, ALU.add), t2)
                a = mulg(m1, zr, Ci, t1, t2)
                d = mulg(m2, zi, Si, t2)
                t3 = addg(hr, m1, m2, ALU.subtract, a, d)
                a = mulg(m1, zr, Si, t3)
                d = mulg(m2, zi, Ci, t3)
                t4 = addg(hi_, m1, m2, ALU.add, a, d)
                yb = 4 + q % 2
                o = PB[yb][r:r + 32, 0:256]
                col = q * 128 + r
                P.mm(o, CTt[:, 0, col:col + 32], hr, True, False, t3, tct, bfree[yb] if i % 4 == 0 else None)
                tk = P.mml(o, CTt[:, 1, col:col + 32], hi_, False, True, t4)
                hfree[k6] = tk
                if i % 4 == 3:
                    yq = ycT[:, q, :]
                    g1, g2 = ar(B0 + 15360, T), ar(B0 + 15616, T)
                    t = P.dve(lambda e, yq=yq, q=q, yb=yb: e.scalar_tensor_tensor(yq, uT[:, q, :], v["sd"][:, q:q + 1], PB[yb][:, 0:256],
                                                                           ALU.mult, ALU.add), tk, ydone)
                    bfree[yb] = t
                    t1 = P.dve(lambda e, yq=yq: e.tensor_tensor(g1, yq, yq, ALU.mult), t)
                    t1 = P.dve(lambda e: e.tensor_scalar(g1, g1, 0.044715, 1.0, ALU.mult, ALU.add), t1)
                    t1 = P.dve(lambda e, yq=yq: e.tensor_tensor(g1, g1, yq, ALU.mult), t1)
                    t1 = P.act(lambda e: e.activation(g1, g1, ACT.Tanh, scale=float(np.sqrt(2 / np.pi))), t1)
                    t1 = P.dve(lambda e: e.tensor_scalar(g1, g1, 0.5, 0.5, ALU.mult, ALU.add), t1)
                    ydone = [P.dve(lambda e, yq=yq: e.tensor_tensor(yq, yq, g1, ALU.mult), t1)]
            return ydone

        t_s5 = s5()
        dump("s5y", ycT, t_s5)

        mq, mk_, mv = ar(4096, 4, T), ar(5120, 4, T), ar(6144, 2, 512)
        tq = take_T("mqk2", [mq[:, i, :] for i in range(4)], [0.125] * 4, 512, [4, 5], [txT, t_s5])
        tk_ = take_T("mqk2", [mk_[:, i, :] for i in range(4)], None, 512, [4, 5], [txT, t_s5])
        w = ring.take("mv2")
        w3 = w[0].rearrange("p (j n) -> p j n", j=8)
        tv = []
        for tt in range(2):
            p_ = rows(PB[6 + tt][:, :], xT, tt, w3, 8, 0, 512, w[1], bfree[6 + tt])
            bfree[6 + tt] = evac(mv[:, tt, :], PB[6 + tt][:, :], p_, "act" if tt else "dve", None, t_s5)
            tv.append(bfree[6 + tt])
        ring.release(p_)
        heads = []
        for h in range(8):
            b = 64 * (h % 2)
            heads.append(dict(kind="moba", q=mq[b:b + 64, h // 2, :], k=mk_[b:b + 64, h // 2, :], base=b, slope=2.0 ** -(h + 1),
                              deps=[tq[h // 2], tk_[h // 2]], v=[mv[:, 0, h * 64:h * 64 + 64], mv[:, 1, h * 64:h * 64 + 64]],
                              vdeps=tv, out=ybT[:, h // 2, :]))
        t_mb = attention(heads, 7168)
        dump("mobay", ybT, t_mb)

        def rwkv():
            zT = ar(3072, 14 * 257).rearrange("p (i t) -> p i t", i=14)
            B0 = 3072 + 14 * 257
            fr = [t_mb, t_s5]
            tz0 = P.dve(lambda e: e.memset(zT[:, :, 0:1], 0.0), fr)
            tz = []
            for ci in range(4):
                n = 4 if ci < 3 else 2
                w = ring.take("z2" if ci < 3 else "z2b")
                toks, last = proj_T("z2", w, 8, n * 128, xT, [txT, fr], [zT[:, 4 * ci + i, 1:257] for i in range(n)], [4, 5])
                ring.release(last)
                tz += toks
            d = ar(B0, T)
            zs = []
            t = None
            for i in range(14):
                t = P.dve(lambda e, i=i: e.tensor_tensor(d, zT[:, i, 0:256], zT[:, i, 1:257], ALU.subtract), tz[i], tz0, t)
                t = P.dve(lambda e, i=i: e.scalar_tensor_tensor(zT[:, i, 1:257], d, v["mu"][:, i:i + 1], zT[:, i, 1:257], ALU.mult, ALU.add), t)
                zs.append(t)
            z = lambda i: zT[:, i, 1:257]
            LW = ar(B0 + 256, 2, 512)
            s_l = sem("s_l")
            t_l = P.dma("act", ar(B0 + 256, 1024), dr["lora"], s_l, 16, fr)
            txw = P.act(lambda e: e.activation(z(12)[0:64], z(12)[0:64], ACT.Tanh), zs[12])
            t = P.act(lambda e: e.activation(z(13), z(13), ACT.Tanh, scale=0.5), zs[13])
            txg = P.dve(lambda e: e.tensor_scalar(z(13), z(13), 0.5, 0.5, ALU.mult, ALU.add), t)
            hv = SM[:, 600:616].rearrange("p (k i) -> p k i", k=4)
            th = P.dve(lambda e: e.tensor_scalar(hv[:, 0, :], v["w0"], 0.5, None, ALU.mult))
            th = P.dve(lambda e: e.tensor_scalar(hv[:, 1, :], v["a0"], 0.5, None, ALU.mult))
            th = P.dve(lambda e: e.tensor_scalar(hv[:, 2, :], v["ka"], -1.0, 1.0, ALU.mult, ALU.add))
            at = [B0 + 1280]

            def al(*shape):
                n = int(np.prod(shape))
                r = ar(at[0], *shape)
                at[0] += n
                return r
            W, iW, Wm = al(T), al(T), al(T)
            q1, q2, q3, q4 = al(T), al(T), al(T), al(T)
            G = al(T)
            at_, bt_, kt_, rt_ = al(T), al(T), al(T), al(T)
            An, Bn, Kn, Vn_ = al(2, 128), al(2, 128), al(2, 128), al(2, 128)
            Dl, Du, Ou, LakT, LrbT, LrkT = [al(4, 128) for _ in range(6)]
            D2, D2t, N1, N1t = [al(4, 128) for _ in range(4)]
            P1 = al(4, 128)
            MT = al(4, 128)
            Uv, SAv, Apn = al(4, 64), al(4, 64), al(4, 64)
            ApT = al(T)
            PTI, QW = al(4, 64), al(4, 64)
            ST = al(4, 64)
            bons = al(T)
            F = lambda a_: a_.rearrange("p a b -> p (a b)")
            prev = fr
            res = []
            for i in range(4):
                pv = prev
                rr, kk_, vv = z(i), z(4 + i), z(8 + i)
                p_ = P.mml(PB[6][:, 0:256], LW[0:64, 0, i * 128:(i + 1) * 128], z(12)[0:64], True, True, t_l, txw, bfree[6])
                p2 = P.mml(PB[7][:, 0:256], LW[64:128, 0, i * 128:(i + 1) * 128], z(12)[64:128], True, True, zs[12], bfree[7])
                p3 = P.mml(PB[7][:, 256:512], LW[:, 1, i * 128:(i + 1) * 128], z(13), True, True, txg)
                t = P.act(lambda e, i=i: e.activation(q1, PB[6][:, 0:256], ACT.Tanh, bias=hv[:, 0, i:i + 1], scale=0.5), p_, th, pv)
                bfree[6] = t
                tlw = P.dve(lambda e: e.tensor_scalar(q1, q1, -EH / 2, -EH / 2, ALU.mult, ALU.add), t)
                on = c["ones"][:, 0:64]
                tcs = []
                for ch in range(4):
                    s_ = slice(64 * ch, 64 * ch + 64)
                    tcs.append(P.dve(lambda e, s_=s_: e.tensor_tensor_scan(q2[:, s_], on, q1[:, s_], 0.0, ALU.mult, ALU.add), tlw, pv))
                tW = P.act(lambda e: e.activation(W, q2, ACT.Exp), tcs, pv)
                tiW = P.act(lambda e: e.activation(iW, q2, ACT.Exp, scale=-1.0), tcs, pv)
                t = P.dve(lambda e: e.tensor_tensor(q3, q2, q1, ALU.subtract), tcs, pv)
                tWm = P.act(lambda e: e.activation(Wm, q3, ACT.Exp), t, pv)
                t = P.act(lambda e, i=i: e.activation(q4, PB[7][:, 0:256], ACT.Tanh, bias=hv[:, 1, i:i + 1], scale=0.5), p3, th, pv)
                ta = P.dve(lambda e: e.tensor_scalar(q4, q4, 0.5, 0.5, ALU.mult, ALU.add), t)
                tG = P.act(lambda e: e.activation(G, PB[7][:, 256:512], ACT.Copy), p3, pv)
                bfree[7] = [t, tG]
                t = P.dve(lambda e, i=i, kk_=kk_: e.tensor_scalar(q1, kk_, v["kk"][:, i:i + 1], None, ALU.mult), zs[4 + i], tcs, tWm)
                t = P.dve(lambda e: e.tensor_tensor(q2, q1, q1, ALU.mult), t, tW, tiW, tWm)
                p_ = P.mml(PB[6][:, 0:256], c["bones"], q2, True, True, t, bfree[6])
                t1 = P.dve(lambda e: e.tensor_scalar(q3, PB[6][:, 0:256], 1e-24, None, ALU.max), p_, tWm)
                bfree[6] = t1
                t1 = P.act(lambda e: e.activation(q3, q3, ACT.Sqrt), t1)
                t1 = P.dve(lambda e: e.reciprocal(q3, q3), t1)
                tkk = P.dve(lambda e: e.tensor_tensor(q1, q1, q3, ALU.mult), t1)
                tat = P.dve(lambda e: e.scalar_tensor_tensor(at_, q1, -1.0, Wm, ALU.mult, ALU.mult), tkk, tWm, pv)
                t = P.dve(lambda e: e.tensor_tensor(q2, q1, q4, ALU.mult), tkk, ta, p_)
                tbt = P.dve(lambda e: e.tensor_tensor(bt_, q2, iW, ALU.mult), t, tiW, pv)
                t = P.dve(lambda e, i=i: e.tensor_scalar(q3, q4, v["ka"][:, i:i + 1], hv[:, 2, i:i + 1], ALU.mult, ALU.add), ta, tkk)
                tkp = P.dve(lambda e, kk_=kk_: e.tensor_tensor(q3, q3, kk_, ALU.mult), t)
                tkt = P.dve(lambda e: e.tensor_tensor(kt_, q3, iW, ALU.mult), tkp, tiW, pv)
                trt = P.dve(lambda e, rr=rr: e.tensor_tensor(rt_, rr, W, ALU.mult), zs[i], tW, pv)
                t = P.dve(lambda e, i=i, rr=rr: e.scalar_tensor_tensor(q2, rr, v["rk"][:, i:i + 1], q3, ALU.mult, ALU.mult), tkp, tbt)
                p_ = P.mml(PB[6][:, 0:256], c["bones"], q2, True, True, t, bfree[6])
                tbo = P.dve(lambda e, vv=vv: e.tensor_tensor(bons, PB[6][:, 0:256], vv, ALU.mult), p_, zs[8 + i], pv)
                bfree[6] = tbo
                for k, (src, dst, tk) in enumerate(((at_, An, tat), (bt_, Bn, tbt), (kt_, Kn, tkt), (vv, Vn_, zs[8 + i]))):
                    b = 6 + k // 2
                    for tt in range(2):
                        o = (k % 2) * 256 + tt * 128
                        tr_ = P.tr(PB[b][:, o:o + 128], src[:, tt * 128:(tt + 1) * 128], ident, tk, bfree[b] if k % 2 == 0 else None)
                    if k % 2:
                        for kk2, d2_ in ((0, (An, Kn)[k // 2]), (1, dst)):
                            e_ = evac(F(d2_), PB[b][:, kk2 * 256:kk2 * 256 + 256], tr_, "act", None, pv)
                        bfree[b] = e_
                tn = e_
                inst = [(p, tt) for p in range(2) for tt in range(2)]

                def pairs(l, r, deps, b):
                    tk = None
                    for n_, (p, tt) in enumerate(inst):
                        rs, cs_ = slice(64 * p, 64 * p + 64), slice(128 * tt, 128 * tt + 128)
                        tk = P.mml(PB[b][:, n_ * 128:n_ * 128 + 128], l[rs, cs_], r[rs, cs_], True, True, deps, bfree[b],
                                   tk if n_ == 2 else None)
                    return tk

                def masked(dst, b, mask, tk, eng="dve"):
                    m = c[mask].unsqueeze(1).to_broadcast([128, 4, 128])
                    src = PB[b][:, :].rearrange("p (n t) -> p n t", n=4)
                    return P.dve(lambda e: e.tensor_tensor(dst, src, m, ALU.mult), tk, pv)

                tk = pairs(bt_, at_, [tat, tbt], 0)
                tDu = masked(Du, 0, "mDu", tk)
                tOu = masked(Ou, 0, "mOu", tk)
                bfree[0] = tOu
                tk = pairs(at_, bt_, [], 1)
                tDl = masked(Dl, 1, "mDl", tk)
                bfree[1] = tDl
                tk = pairs(kt_, at_, [tkt], 2)
                tLak = masked(LakT, 2, "mSu", tk)
                bfree[2] = tLak
                tk = pairs(bt_, rt_, [trt], 3)
                tLrb = masked(LrbT, 3, "mIu", tk)
                bfree[3] = tLrb
                tk = pairs(kt_, rt_, [], 0)
                tLrk = masked(LrkT, 0, "mIu", tk)
                bfree[0] = tLrk

                def prod(b, l, r, deps):
                    for n_ in range(4):
                        tk = P.mml(PB[b][:, n_ * 128:n_ * 128 + 128], l[:, n_, :], r[:, n_, :], True, True, deps, bfree[b])
                    return tk

                def take(dst, b, tk, eng, *deps):
                    e_ = evac(F(dst), PB[b][:, :], tk, eng, None, pv, *deps)
                    bfree[b] = e_
                    return e_

                def plus(dst, b, other, tk, *deps):
                    e_ = P.dve(lambda e: e.tensor_tensor(F(dst), F(other), PB[b][:, :], ALU.add), tk, pv, *deps)
                    bfree[b] = e_
                    return e_

                idb = ident.unsqueeze(1).to_broadcast([128, 4, 128])
                tP = P.dve(lambda e: e.tensor_tensor(P1, Dl, idb, ALU.add), tDl, pv)
                a = prod(1, Du, Dl, [tDu, tDl])
                t2 = take(D2, 1, a, "act")
                b = prod(2, Dl, Du, [])
                t2t = take(D2t, 2, b, "dve")
                a = prod(3, D2t, P1, [t2t, tP])
                tP = plus(P1, 3, P1, a)
                a = prod(1, D2t, D2, [t2])
                b = prod(2, D2, D2t, [])
                t4 = take(Dl, 1, a, "act", b)
                t4t = take(Du, 2, b, "dve", a)
                a = prod(3, Du, P1, [t4t, tP])
                tP = plus(P1, 3, P1, a)
                b = prod(2, Dl, Du, [t4])
                t8t = take(D2t, 2, b, "dve")
                a = prod(3, D2t, P1, [t8t, tP])
                tP = plus(P1, 3, P1, a)
                for n_ in range(4):
                    tk = P.tr(PB[1][:, n_ * 128:n_ * 128 + 128], P1[:, n_, :], ident, tP, bfree[1])
                tMt = take(D2, 1, tk, "act", b)
                a = prod(0, P1, Ou, [tOu, tP])
                tN = take(N1, 0, a, "act")
                b = prod(2, Ou, P1, [])
                tNt = take(N1t, 2, b, "dve")
                a = prod(3, N1, N1t, [tN, tNt])
                tN2 = take(Dl, 3, a, "act")
                a = prod(1, Dl, D2, [tN2, tMt])
                tR = plus(Du, 1, D2, a)
                a = prod(2, N1t, Du, [tR])
                tMT = plus(MT, 2, Du, a)
                for n_, (p, tt) in enumerate(inst):
                    tk = P.mml(PB[3][:, n_ * 64:n_ * 64 + 64], LakT[:, n_, :], Vn_[:, tt, 64 * p:64 * p + 64], True, True, tLak, tn, bfree[3])
                tU = evac(F(Uv), PB[3][:, 0:256], tk, "act", None, pv)
                bfree[3] = tU
                for n_, (p, tt) in enumerate(inst):
                    P.mml(PB[0][:, n_ * 64:n_ * 64 + 64], MT[:, n_, :], Uv[:, n_, :], True, True, tMT, tU, bfree[0])
                for n_, (p, tt) in enumerate(inst):
                    tk = P.mml(PB[0][:, 256 + n_ * 64:256 + n_ * 64 + 64], MT[:, n_, :], An[:, tt, 64 * p:64 * p + 64], True, True, tn)
                tSA = evac(F(SAv), PB[0][:, 0:256], tk, "dve", None, pv)
                tAn = evac(F(Apn), PB[0][:, 256:512], tk, "dve", None, pv)
                bfree[0] = tAn
                for n_, (p, tt) in enumerate(inst):
                    tk = P.mml(PB[1][64 * p:64 * p + 64, tt * 128:tt * 128 + 128], An[:, tt, 64 * p:64 * p + 64], MT[:, n_, :], True, True, bfree[1])
                tAp = evac(ApT, PB[1][:, 0:256], tk, "dve", None, pv)
                bfree[1] = tAp
                tk = None
                for p, ch in ((0, 0), (0, 2), (1, 0), (1, 2), (0, 1), (1, 1)):
                        ps_ = slice(64 * p, 64 * p + 64)
                        sw = tk if (p, ch) == (0, 1) else None
                        tt, hs = ch // 2, slice(64 * (ch % 2), 64 * (ch % 2) + 64)
                        n_ = 2 * p + tt
                        P.mml(PB[2][ps_, ch * 64:ch * 64 + 64], Apn[hs, n_, :], Bn[hs, tt, ps_], True, True, tAn, tn, bfree[2], sw)
                        P.mm(PB[3][ps_, ch * 64:ch * 64 + 64], Bn[hs, tt, ps_], SAv[hs, n_, :], True, False, tSA, bfree[3])
                        tk = P.mml(PB[3][ps_, ch * 64:ch * 64 + 64], Kn[hs, tt, ps_], Vn_[hs, tt, ps_], False, True)
                i64 = c["i64"].unsqueeze(1).to_broadcast([128, 3, 64])
                tPT = P.dve(lambda e: e.tensor_tensor(PTI[:, 0:3, :], PB[2][:, 0:192].rearrange("p (c n) -> p c n", c=3), i64, ALU.add), tk, pv)
                bfree[2] = tPT
                tQ = []
                for ch in range(3):
                    wc = W[:, 64 * ch + 63:64 * ch + 64]
                    dst = ST[:, 1, :] if ch == 0 else QW[:, ch, :]
                    tQ.append(P.dve(lambda e, wc=wc, dst=dst, ch=ch: e.tensor_scalar(dst, PB[3][:, ch * 64:ch * 64 + 64], wc, None, ALU.mult), tk, pv))
                bfree[3] = tQ[-1]
                tS = [None, tQ[0]]
                for ch in (1, 2):
                    for p in range(2):
                        ps_ = slice(64 * p, 64 * p + 64)
                        tk = P.mml(PB[0][ps_, ch * 64:ch * 64 + 64], PTI[ps_, ch, :], ST[ps_, ch, :], True, True, tPT, tS[ch], bfree[0])
                    wc = W[:, 64 * ch + 63:64 * ch + 64]
                    tS.append(P.dve(lambda e, wc=wc, ch=ch: e.scalar_tensor_tensor(ST[:, ch + 1, :], PB[0][:, ch * 64:ch * 64 + 64], wc, QW[:, ch, :],
                                                                                    ALU.mult, ALU.add), tk, tQ[ch]))
                    bfree[0] = tS[-1]
                tk = None
                for p in range(2):
                    sw = tk
                    for ch in (1, 2, 3):
                        tt, hs = ch // 2, slice(64 * (ch % 2), 64 * (ch % 2) + 64)
                        ps_ = slice(64 * p, 64 * p + 64)
                        n_ = 2 * p + tt
                        tk = P.mml(PB[1][hs, n_ * 64:n_ * 64 + 64], ApT[ps_, 64 * ch:64 * ch + 64], ST[ps_, ch, :], True, True, tAp, tS[ch], bfree[1], sw)
                saq = SAv.rearrange("p (a t) n -> p a t n", t=2)
                paq = PB[1][:, 0:256].rearrange("p (a t n) -> p a t n", t=2, n=64)
                t1 = P.dve(lambda e: e.tensor_tensor(saq[64:128, :, 0, :], saq[64:128, :, 0, :], paq[64:128, :, 0, :], ALU.add), tk)
                t2 = P.dve(lambda e: e.tensor_tensor(saq[:, :, 1, :], saq[:, :, 1, :], paq[:, :, 1, :], ALU.add), tk)
                bfree[1] = t2
                for p in range(2):
                    ps_ = slice(64 * p, 64 * p + 64)
                    for tt in range(2):
                        n_ = 2 * p + tt
                        o = PB[2][ps_, tt * 128:tt * 128 + 128]
                        P.mm(o, SAv[:, n_, :], LrbT[:, n_, :], True, False, t1, t2, tLrb, bfree[2])
                        P.mm(o, Vn_[:, tt, ps_], LrkT[:, n_, :], False, False, tLrk)
                        chs = [ch for ch in (2 * tt, 2 * tt + 1) if ch > 0]
                        for ch in chs:
                            tk = P.mml(PB[2][ps_, 64 * ch:64 * ch + 64], ST[ps_, ch, :], rt_[ps_, 64 * ch:64 * ch + 64], False, ch == chs[-1], trt, tS[ch])
                tY = evac(q1, PB[2][:, 0:256], tk, "dve", None, tat, tbt)
                bfree[2] = tY
                p_ = P.mml(PB[3][:, 0:256], c["bmean"], q1, True, True, tY, bfree[3])
                t = P.dve(lambda e: e.tensor_tensor(q1, q1, PB[3][:, 0:256], ALU.subtract), p_)
                t2 = P.dve(lambda e: e.tensor_tensor(q2, q1, q1, ALU.mult), t, tbo)
                p_ = P.mml(PB[3][:, 256:512], c["bmean"], q2, True, True, t2)
                t3 = P.act(lambda e: e.activation(q3, PB[3][:, 256:512], ACT.Sqrt, bias=c["epg"]), p_, tkt)
                bfree[3] = t3
                t3 = P.dve(lambda e: e.reciprocal(q3, q3), t3)
                t = P.dve(lambda e: e.tensor_tensor(q1, q1, q3, ALU.mult), t3)
                t = P.dve(lambda e, i=i: e.tensor_scalar(q1, q1, v["lnw"][:, i:i + 1], v["lnb"][:, i:i + 1], ALU.mult, ALU.add), t)
                t = P.dve(lambda e: e.tensor_tensor(q1, q1, bons, ALU.add), t, tbo)
                ya = yaT[:, i, :]
                t = P.dve(lambda e, ya=ya: e.tensor_tensor(ya, q1, G, ALU.mult), t, tG)
                res.append(t)
                prev = [t, tk]
            return res

        t_rw = rwkv()
        dump("rwy", yaT, t_rw)

        zA, zB = ar(4096, 4, T), ar(5120, 4, T)
        w = ring.take("glu")
        w3 = w[0].rearrange("p (j n) -> p j n", j=4)
        gh = SM[:, 620:628]
        gh2 = SM[:, 628:652]
        th1 = P.dve(lambda e: e.tensor_scalar(gh, v["gb"], 0.5, None, ALU.mult))
        th2 = P.dve(lambda e: e.tensor_scalar(gh2, v["gateb"], 0.5, None, ALU.mult))
        tz = []
        for i in range(4):
            b = 4 + i % 4
            p_ = tile_T(PB[b][:, 0:256], w3, 4, i * 128, 128, ycT, w[1], t_s5, bfree[b])
            p2 = tile_T(PB[b][:, 256:512], w3, 4, (4 + i) * 128, 128, ycT)
            ta = P.act(lambda e, i=i, b=b: e.activation(zB[:, i, :], PB[b][:, 256:512], ACT.Tanh, scale=0.5, bias=gh[:, 4 + i:5 + i]), p2, th1, t_rw)
            tb = P.dve(lambda e, i=i: e.tensor_scalar(zB[:, i, :], zB[:, i, :], 0.5, 0.5, ALU.mult, ALU.add), ta)
            tb = P.dve(lambda e, i=i, b=b: e.scalar_tensor_tensor(zA[:, i, :], PB[b][:, 0:256], v["gb"][:, i:i + 1], zB[:, i, :],
                                                           ALU.add, ALU.mult), tb, p_, t_rw)
            bfree[b] = tb
            tz.append(tb)
        ring.release(p2)
        dump("s5", zA, tz)
        mT = ar(6144, 8, T)
        gtile, mtile = [ar(8192 + 256 * i, T) for i in range(4)], [ar(9216 + 256 * i, T) for i in range(4)]
        ydeps = [t_rw, t_mb, tz]
        tm = []
        gfree = [None] * 4
        wu = None
        n = 0
        for dt_ in range(8):
            wg = ring.take("gate2")
            g3 = wg[0].rearrange("p (j n) -> p j n", j=8)
            if dt_ % 2 == 0:
                wu = ring.take("up2")
            u5 = wu[0].rearrange("p (d b j n) -> p d b j n", d=2, b=3, j=4)
            acc = mT[:, dt_, :]
            tprev = None
            for br in range(3):
                b = 4 + n % 4
                yT = (yaT, ybT, zA)[br]
                p_ = tile_T(PB[b][:, 0:256], g3, 8, br * 128, 128, xT, wg[1], bfree[b])
                for j in range(4):
                    f = P.mml if j == 3 else P.mm
                    p2 = f(PB[b][:, 256:512], u5[:, dt_ % 2, br, j, :], yT[:, j, :], j == 0, j == 3, wu[1], ydeps)
                gs = gtile[n % 4]
                t = P.act(lambda e, gs=gs, b=b, br=br, dt_=dt_: e.activation(gs, PB[b][:, 0:256], ACT.Tanh, scale=0.5,
                                                            bias=gh2[:, br * 8 + dt_:br * 8 + dt_ + 1]), p2, th2, gfree[n % 4], t_rw)
                t = P.dve(lambda e, gs=gs: e.tensor_scalar(gs, gs, 0.5, 0.5, ALU.mult, ALU.add), t)
                if br == 0:
                    t = P.dve(lambda e, gs=gs, b=b, acc=acc: e.tensor_tensor(acc, gs, PB[b][:, 256:512], ALU.mult), t, p2, t_rw)
                    bfree[b] = t
                else:
                    t = P.dve(lambda e, gs=gs, b=b: e.tensor_tensor(gs, gs, PB[b][:, 256:512], ALU.mult), t, p2)
                    bfree[b] = t
                    t = P.dve(lambda e, gs=gs, acc=acc: e.tensor_tensor(acc, acc, gs, ALU.add), t, tprev)
                gfree[n % 4] = t
                tprev = t
                n += 1
            tm.append(tprev)
            if dt_ % 2 == 0:
                ring.release(p2)
            else:
                ring.release(p2)
                ring.release(p2)
        dump("merged", mT, tm)
        tk = w_out("wo2", mT, tm)
        tx = add_norm(ALPHA2, tk, t_gb)
        dump("ln4", x3, tx)
        t_gb = load_gb(5, tx)
        txT = transpose_rows(xT, x3, tx, [4, 5])

        s_r2 = sem("s_r2")
        t_r = P.dma("act", RW, dr["wr2"], s_r2, 16, tk[(1, 1)])
        G2 = ar(512, 2, 32)
        Lg = ar(1024, 2, 36)
        E2 = ar(1152, 2, 32)
        O2 = ar(1280, 2, 2, 32)
        gt2 = ar(1408, 2, 2)
        Lp = ar(1420, 2, 8)
        OG = ar(1440, 2, 8)
        tgate = []
        fr = tm
        for tt in range(2):
            p_ = rows(PB[6 + tt][:, 0:36], xT, tt, RW, 8, 0, 36, t_r, txT, bfree[6 + tt])
            t = P.dve(lambda e, tt=tt: e.tensor_tensor(Lg[:, tt, :], PB[6 + tt][:, 0:36], v["br2"], ALU.add), p_, fr, tk[(1, 1)])
            bfree[6 + tt] = t
            m_ = P.dve(lambda e, tt=tt: e.memset(Lp[:, tt, :], -3e38), tk[(1, 1)])
            m_ = P.dve(lambda e, tt=tt: e.tensor_copy(Lp[:, tt, 0:4], Lg[:, tt, 0:4]), t, m_)
            mx, ixf = SM[:, 700:708], SM[:, 708:716]
            a = P.dve(lambda e, tt=tt: e.max(mx, Lp[:, tt, :]), m_)
            b = P.dve(lambda e, tt=tt: e.max_index(IX[:, 8:16], mx, Lp[:, tt, :]), a)
            b = P.dve(lambda e: e.tensor_copy(ixf, IX[:, 8:16]), b)
            oh = P.dve(lambda e, tt=tt: e.tensor_scalar(OG[:, tt, :], c["iota"][:, 0:8], ixf[:, 0:1], None, ALU.is_equal), b)
            ng = SM[:, 716:717]
            eg = SM[:, 720:724]
            pg = SM[:, 717 + tt:718 + tt]
            a = P.dve(lambda e: e.tensor_scalar(ng, mx[:, 0:1], -1.0, None, ALU.mult), a, tgate)
            a = P.act(lambda e, tt=tt, pg=pg: e.activation(eg, Lg[:, tt, 0:4], ACT.Exp, bias=ng, accum_out=pg), a)
            tpg = P.dve(lambda e, pg=pg: e.reciprocal(pg, pg), a)
            e4 = E2[:, tt, :].rearrange("p (g k) -> p g k", g=4)
            l4 = Lg[:, tt, 4:36].rearrange("p (g k) -> p g k", g=4)
            o4 = OG[:, tt, 0:4].unsqueeze(2).to_broadcast([128, 4, 8])
            pen = SM[:, 724:728]
            pb4 = pen.unsqueeze(2).to_broadcast([128, 4, 8])
            a = P.dve(lambda e, tt=tt, pen=pen: e.tensor_scalar(pen, OG[:, tt, 0:4], 3e38, -3e38, ALU.mult, ALU.add), oh)
            b = P.dve(lambda e, e4=e4, l4=l4, o4=o4: e.tensor_tensor(e4, l4, o4, ALU.mult), oh)
            t = P.dve(lambda e, e4=e4, pb4=pb4: e.tensor_tensor(e4, e4, pb4, ALU.add), a, b)
            tt2 = top2(E2[:, tt, :], 32, [O2[:, tt, 0, :], O2[:, tt, 1, :]], gt2[:, tt, :], t, 740 + 32 * tt)
            t = P.dve(lambda e, tt=tt, pg=pg: e.tensor_scalar(gt2[:, tt, :], gt2[:, tt, :], pg, None, ALU.mult), tt2, tpg)
            t = P.dve(lambda e, tt=tt: e.tensor_scalar(G2[:, tt, :], O2[:, tt, 0, :], gt2[:, tt, 0:1], None, ALU.mult), t)
            t = P.dve(lambda e, tt=tt: e.scalar_tensor_tensor(G2[:, tt, :], O2[:, tt, 1, :], gt2[:, tt, 1:2], G2[:, tt, :],
                                                              ALU.mult, ALU.add), t)
            tgate.append(t)
        dump("g2", G2, tgate)
        hTs = [ar(2048, 2, T), ar(2560, 2, T)]
        acct = moe_dense("e2in", "e2out", NE2, 2, G2, tgate, hTs, txT, tx)
        tx = layer_norm(ALPHA2, lambda tt, h: (y3[:, tt, h * 512:(h + 1) * 512], acct[tt][h]), lambda *a: None, t_gb)
        s_o = sem("s_o")
        to = P.dma("sp", out.rearrange("a (t p) d -> p (a t) d", p=128), x3, s_o, 16, tx)
        P.wait("sp", [to])

        block = ctx.enter_context(nc.Block())
        block.sync(P.run("sp"))
        block.scalar(P.run("act"))
        block.vector(P.run("dve"))
        block.gpsimd(P.run("pool"))
        block.tensor(P.run("pe"))


def cols(w, groups, kt=8):
    out = []
    for g in groups:
        a = w[:, g]
        out.append(a.reshape(kt, 128, a.shape[1]).transpose(1, 0, 2).reshape(128, -1))
    return np.ascontiguousarray(np.stack(out))


def rowsk(w, nk=4):
    k = w.shape[0] // 128
    a = w.reshape(k, 128, 1024).transpose(1, 0, 2)
    n = -(-k // nk)
    o = np.zeros((n, 128, nk * 1024), w.dtype)
    for i in range(n):
        b = a[:, i * nk:(i + 1) * nk]
        o[i, :, :b.shape[1] * 1024] = b.reshape(128, -1)
    return o


def pairs(n):
    return [np.r_[i:i + 256, n + i:n + i + 256] for i in range(0, n, 256)]


def col4(a):
    return a.reshape(-1, 128).T


def layout(I):
    I = {k: np.asarray(a) for k, a in I.items()}
    r = lambda a, b: np.arange(a, b)
    A = {}
    A["x"], A["mem"] = I["x"], I["mem"]
    A["cst"] = CT
    A["pos"] = np.ascontiguousarray(np.broadcast_to(I["positions"].reshape(1, T), (128, T)))
    sw, fo = I["w_in_swa"][0], I["w_in_fox"][0]
    A["wkv"] = np.concatenate([cols(I["w_mem_kv"][i], [r(0, 512)]) for i in range(2)])
    k0 = 768
    kd = np.concatenate([np.r_[k0 + 64 * g:k0 + 64 * g + 64, k0 + 64 * g:k0 + 64 * g + 64] for g in range(3)])
    A["swT"] = cols(sw, [r(0, 512), np.r_[512:768, 1152:1408]])
    A["swk"] = cols(sw, [kd])
    A["swv"] = cols(sw, [r(960, 1152)])
    A["wo"] = np.concatenate([cols(I["w_out"][i], [r(0, 512), r(512, 1024)]) for i in range(2)])
    A["fin"] = cols(I["w_ffn_in"][0], pairs(DFF))
    A["fout"] = rowsk(I["w_ffn_out"][0])
    A["foT"] = cols(fo, [r(512 * i, 512 * i + 512) for i in range(3)])
    A["foqf"] = cols(fo, [r(2304, 2572)])
    A["fov"] = cols(fo, [r(1536, 2048)])
    A["fov2"] = cols(fo, [r(2048, 2304)])
    A["ein"] = np.stack([cols(w, pairs(DFF)) for w in I["w_exp_in"][0]])
    A["eout"] = np.stack([rowsk(w) for w in I["w_exp_out"][0]])
    w2 = I["w_in_2"][0]
    A["z2"] = cols(w2, [r(0, 512), r(512, 1024), r(1024, 1536)])
    A["z2b"] = cols(w2, [r(1536, 1792)])
    A["mqk2"] = cols(w2, [r(1792, 2304), r(2304, 2816)])
    A["mv2"] = cols(w2, [r(2816, 3328)])
    A["u2"] = cols(w2, [r(3328, 3840)])
    A["gate2"] = cols(w2, [np.concatenate([3840 + 1024 * b + r(128 * d, 128 * d + 128) for b in range(3)]) for d in range(8)])
    up = np.stack([I["w_up_rwkv_2"][0], I["w_up_moba_2"][0], I["w_up_ssm_2"][0]])
    A["up2"] = np.ascontiguousarray(up.reshape(3, 4, 128, 4, 2, 128).transpose(3, 2, 4, 0, 1, 5).reshape(4, 128, 3072))
    A["glu"] = cols(I["ssm_glu_w_2"][0], [r(0, 1024)], 4)
    A["wo2"] = cols(I["w_out_2"][0], [r(0, 512), r(512, 1024)])
    A["e2in"] = np.stack([cols(np.concatenate([g, u], 1), [r(0, 512)])[0]
                          for g, u in zip(I["expert_w_gate_2"][0], I["expert_w_up_2"][0])])
    A["e2out"] = np.stack([rowsk(w, 2)[0] for w in I["expert_w_down_2"][0]])
    gb = [np.concatenate([I["ln_attn_g"][0], I["ln_attn_b"][0]]), np.concatenate([I["ln_ffn_g"][0], I["ln_ffn_b"][0]]),
          np.concatenate([I["ln_attn_g"][1], I["ln_attn_b"][1]]), np.concatenate([I["ln_ffn_g"][1], I["ln_ffn_b"][1]]),
          np.concatenate([I["ln1_w_2"][0], I["ln1_b_2"][0]]), np.concatenate([I["ln2_w_2"][0], I["ln2_b_2"][0]])]
    A["gb"] = np.ascontiguousarray(np.broadcast_to(np.stack(gb)[:, None, :], (6, 128, 2048)))
    kp = lambda w: np.ascontiguousarray(w.reshape(8, 128, -1).transpose(1, 0, 2))
    A["wr1"] = kp(I["w_router"][0])
    A["wr2"] = kp(np.concatenate([I["router_group_w_2"][0], I["router_expert_w_2"][0]], 1))
    A["lora"] = np.ascontiguousarray(np.concatenate([np.concatenate([I["rwkv_w2_2"][0], I["rwkv_a2_2"][0]], 0), I["rwkv_g2_2"][0]], 1))
    V = np.zeros((128, NVEC), np.float32)

    def put(n, a):
        o, w = VOFF[n]
        V[0:a.shape[0], o:o + w] = a
    bc = lambda a: np.broadcast_to(a[None, :], (128, a.shape[0]))
    put("sink", bc(I["attn_sinks"][0]))
    put("bf", I["b_forget"][0][:, None])
    put("mu", col4(I["rwkv_mu_2"][0]))
    for n, k in (("w0", "rwkv_w0_2"), ("a0", "rwkv_a0_2"), ("kk", "rwkv_k_k_2"), ("ka", "rwkv_k_a_2"), ("rk", "rwkv_r_k_2"),
                 ("lnw", "rwkv_ln_w_2"), ("lnb", "rwkv_ln_b_2"), ("are", "ssm_a_re_2"), ("aim", "ssm_a_im_2"), ("sd", "ssm_d_2"),
                 ("gb", "ssm_glu_b_2"), ("gateb", "gate_b_2")):
        put(n, col4(I[k][0].reshape(-1)))
    put("ldt", np.repeat(I["ssm_log_dt_2"][0], 64).reshape(16, 128).T)
    put("br1", bc(I["b_router"][0]))
    put("br2", bc(np.concatenate([I["router_group_b_2"][0], I["router_expert_b_2"][0]])))
    A["vec"] = V
    b5 = [I[k][0].reshape(16, 128, 16).transpose(1, 0, 2).reshape(128, 256) for k in ("ssm_b_re_2", "ssm_b_im_2")]
    A["s5b"] = np.ascontiguousarray(np.concatenate(b5, 1))
    c5 = [I[k][0].reshape(4, 128, 64).transpose(1, 0, 2).reshape(128, 256) for k in ("ssm_c_re_2", "ssm_c_im_2")]
    A["s5c"] = np.ascontiguousarray(np.concatenate(c5, 1))
    return A


def program(nc, arrays, dbg=()):
    dr = {n: nc.dram_tensor("in_" + n, a.shape, mybir.dt.from_np(a.dtype), kind="ExternalInput").ap() for n, a in arrays.items()}
    out = nc.dram_tensor("out_0", (1, T, D), F32, kind="ExternalOutput").ap()
    d = {n: nc.dram_tensor("dbg_" + n, s, F32, kind="ExternalOutput").ap() for n, s in dbg}
    build(nc, dr, out, d)


def kernel(**inputs):
    import concourse.bacc as _bacc
    from concourse.bass_utils import run_bass_kernel_spmd as _run

    arrays = layout(inputs)
    nc = _bacc.Bacc("TRN2", target_bir_lowering=False, num_devices=1)
    program(nc, arrays)
    r = _run(nc, [{"in_" + n: a for n, a in arrays.items()}], core_ids=[0])
    return r.results[0]["out_0"]
```

```python
from contextlib import ExitStack

import numpy as np
import concourse.bass as bass
from concourse import mybir

ALU = mybir.AluOpType
ACT = mybir.ActivationFunctionType
AX = mybir.AxisListType
F32 = mybir.dt.float32
I32 = mybir.dt.int32
U32 = mybir.dt.uint32

T = 256
D = 1024
DFF = 2816
NE1 = 8
NE2 = 32
ALPHA1 = 4.0 ** 0.25
ALPHA2 = 2.0 ** 0.25
LN_EPS = 1e-5
GN_EPS = 64e-5
NEG = -1e30
EH = float(np.exp(-0.5))
RING = 4
EARLY = 4
SLOT = 4096
TWO_PI = 2.0 * np.pi
PI_A = 6.28125
PI_B = float(np.float32(np.round((TWO_PI - PI_A) * 2.0 ** 24) / 2.0 ** 24 // 2.0 ** -20 * 2.0 ** -20))
PI_C = float(TWO_PI - PI_A - PI_B)
MAGIC = 12582912.0


def const_table():
    p = np.arange(128)
    parts = {}
    parts["ident"] = np.eye(128)
    parts["ones"] = np.ones((128, 128))
    same = lambda n: (p[:, None] // n) == (p[None, :] // n)
    parts["bones"] = same(64)
    parts["bmean"] = same(64) / 64.0
    rt = np.zeros((128, 128))
    for b in (0, 64):
        for m in range(8):
            rt[b + m + 8, b + m] = -1.0
            rt[b + m, b + m + 8] = 1.0
    parts["rot"] = rt
    inv = np.zeros(128)
    freq = np.float32(500000.0) ** (-np.arange(0, 16, 2, dtype=np.float32) / np.float32(16))
    for b in (0, 64):
        inv[b:b + 8] = freq
        inv[b + 8:b + 16] = freq
    parts["inv"] = inv[:, None]
    parts["eps"] = np.full((128, 1), LN_EPS)
    parts["epg"] = np.full((128, 1), GN_EPS)
    i = p[:, None]
    q = p[:, None]
    k1 = np.arange(128)[None, :]
    k2 = np.arange(256)[None, :]
    ok = lambda qq, kk: ((kk // 64) <= (qq // 64)) & ((kk // 64) >= (qq // 64) - 2)
    parts["swa"] = np.concatenate([np.where(ok(q, k1), 0, NEG), np.where(ok(q + 128, k2), 0, NEG)], 1)
    parts["caus"] = np.concatenate([np.where(k1 <= q, 0, NEG), np.where(k2 <= q + 128, 0, NEG)], 1)
    parts["dist"] = np.concatenate([np.where(k1 <= q, k1 - q, NEG), np.where(k2 <= q + 128, k2 - q - 128, NEG)], 1)
    j = p[None, :]
    i6, j6 = i % 64, np.arange(64)[None, :]
    b6 = (i6 // 16) == (j6 // 16)
    parts["mDl"] = (j6 < i6) & b6
    parts["mDu"] = (i6 < j6) & b6
    parts["mOu"] = (i6 < j6) & ~b6
    parts["mSu"] = (i6 < j6)
    parts["mIu"] = (i6 <= j6)
    parts["i64"] = np.concatenate([np.eye(64)] * 2, 0)
    parts["cmask"] = (j // 16 % 2) == (i // 64)
    parts["su"] = (i < j)
    parts["iota"] = np.broadcast_to(np.arange(128)[None, :], (128, 128))
    cols, at, off = [], 0, {}
    for n, a in parts.items():
        a = np.asarray(a, np.float32)
        off[n] = (at, a.shape[1])
        at += a.shape[1]
        cols.append(a)
    return np.ascontiguousarray(np.concatenate(cols, 1), np.float32), off


CT, COFF = const_table()

VEC = [("sink", 12), ("bf", 1), ("mu", 14), ("w0", 4), ("a0", 4), ("kk", 4), ("ka", 4), ("rk", 4),
       ("lnw", 4), ("lnb", 4), ("are", 16), ("aim", 16), ("ldt", 16), ("sd", 4), ("gb", 8),
       ("gateb", 24), ("br1", 8), ("br2", 36)]
VOFF = {}
_a = 0
for _n, _w in VEC:
    VOFF[_n] = (_a, _w)
    _a += _w
NVEC = _a


class Prog:

    def __init__(self, nc, ctx):
        self.nc, self.ctx = nc, ctx
        self.q = {e: [] for e in ("pe", "dve", "act", "pool", "sp")}
        self.sem = {e: ctx.enter_context(nc.semaphore("s_" + e)) for e in ("pe", "dve", "act", "pool")}
        self.n = {e: 0 for e in self.sem}
        self.seen = {e: {} for e in self.q}

    def wait(self, e, deps):
        for d in deps:
            if d is None:
                continue
            if isinstance(d, list):
                self.wait(e, d)
                continue
            s, v = d
            if self.seen[e].get(id(s), 0) < v:
                self.seen[e][id(s)] = v
                self.q[e].append(("w", s, v))

    def op(self, e, fn, *deps, par=False):
        if e != "pe" and self.n[e] and not par:
            self.wait(e, [(self.sem[e], self.n[e])])
        self.wait(e, deps)
        self.n[e] += 1
        self.q[e].append(("i", fn, self.sem[e], 1))
        return (self.sem[e], self.n[e])

    def quiet(self, e, fn, *deps):
        self.wait(e, deps)
        self.q[e].append(("i", fn, None, 0))

    def dve(self, fn, *deps, par=False):
        return self.op("dve", fn, *deps, par=par)

    def act(self, fn, *deps, par=False):
        return self.op("act", fn, *deps, par=par)

    def pool(self, fn, *deps, par=False):
        return self.op("pool", fn, *deps, par=par)

    def mm(self, out, lhsT, rhs, start, stop, *deps):
        self.quiet("pe", lambda e: e.matmul(out, lhsT, rhs, start=start, stop=stop), *deps)

    def mml(self, out, lhsT, rhs, start, stop, *deps):
        return self.op("pe", lambda e: e.matmul(out, lhsT, rhs, start=start, stop=stop), *deps)

    def tr(self, out, in_, ident, *deps):
        return self.op("pe", lambda e: e.transpose(out, in_, ident), *deps)

    def dma(self, e, out, in_, sem, count, *deps):
        self.wait(e, deps)
        self.q[e].append(("i", lambda g: g.dma_start(out, in_), sem, 16))
        return (sem, count)

    def open(self, tag):
        self.wait_all("before the section")
        self.tag = tag
        self.saved = (self.q, self.sem, self.n, self.seen)
        self.q = {e: [] for e in self.q}
        self.sem = {e: self.ctx.enter_context(self.nc.semaphore(f"{tag}_{e}")) for e in self.sem}
        self.n = {e: 0 for e in self.n}
        self.seen = {e: {} for e in self.seen}

    def close(self, flag):
        self.wait_all("the end of the section")
        sub = self.q
        self.q, self.sem, self.n, self.seen = self.saved
        for e in self.q:
            self.q[e].append(("if", flag, sub[e], self.tag))

    def wait_all(self, _):
        every = [(self.sem[e], self.n[e]) for e in self.n if self.n[e]]
        for e in self.q:
            self.wait(e, every)

    def run(self, e):
        def go(g, queue=None):
            for it in self.q[e] if queue is None else queue:
                if it[0] == "w":
                    g.wait_ge(it[1], it[2])
                elif it[0] == "if":
                    with g.register(f"flag_{e}_{it[3]}") as reg:
                        g.reg_load(reg, it[1])
                        with g.If_ne(reg, 0):
                            go(g, it[2])
                else:
                    ins = it[1](g)
                    if it[2] is not None:
                        ins.then_inc(it[2], it[3])
        return go


class Ring:

    def __init__(self, P, slots, plan, tag="s_w", start=None):
        self.P, self.slots, self.plan, self.size = P, slots, plan, len(slots)
        self.sems = [P.ctx.enter_context(P.nc.semaphore(f"{tag}{i}")) for i in range(self.size)]
        self.count = [0] * self.size
        self.landed = []
        self.taken = 0
        self.heir = None
        self.released = 0
        for _ in range(self.size if start is None else start):
            self.load(None)

    def load(self, after):
        i = len(self.landed)
        if i < len(self.plan):
            src, n = self.plan[i][1:]
            s = i % self.size
            dst = self.slots[s][:, 0:n]
            parts = [(dst, src)]
            if len(src.shape) == 4:
                d4 = dst.rearrange("p (a b n) -> p a b n", a=src.shape[1], b=src.shape[2])
                parts = [(d4[:, k], src[:, k]) for k in range(src.shape[1])]
            elif len(src.shape) == 3:
                parts = [(dst.rearrange("p (a n) -> p a n", a=src.shape[1]), src)]
            for d, a in parts:
                self.count[s] += 16
                self.P.dma("sp", d, a, self.sems[s], self.count[s], after)
            self.landed.append((self.sems[s], self.count[s]))
        elif self.heir:
            self.heir.slots[self.heir.own + self.released - len(self.plan) + self.size] = self.slots[self.released % self.size]
            self.heir.load(after)

    def take(self, name):
        i = self.taken
        assert self.plan[i][0] == name, (self.plan[i][0], name)
        self.taken += 1
        s, n = i % self.size, self.plan[i][2]
        return self.slots[s][:, 0:n], self.landed[i]

    def release(self, tok):
        self.load(tok)
        self.released += 1


def build(nc, dr, out, dbg=None):
    ctx = ExitStack()
    with ctx:
        P = Prog(nc, ctx)
        dbg = dbg or {}

        def sb(name, n, dt=F32):
            return ctx.enter_context(nc.sbuf_tensor(name, [128, n], dt))

        def sem(name):
            return ctx.enter_context(nc.semaphore(name))

        ringbuf = sb("ringbuf", RING * SLOT)
        CST = sb("cst", CT.shape[1])
        VC = sb("vec", NVEC)
        X = sb("X", 2 * D)
        XT = sb("XT", 8 * T)
        Y = sb("Y", 2 * D)
        GB = sb("GB", 2 * D)
        AR = sb("arena", 23500)
        SM = sb("small", 1024)
        IX = sb("ix", 64, U32)
        POS = sb("pos", T, I32)
        PB = [ctx.enter_context(nc.psum_tensor(f"pb{i}", [128, 512], F32)) for i in range(8)]
        bfree = [None] * 8

        c = {n: CST[:, o:o + w] for n, (o, w) in COFF.items()}
        v = {n: VC[:, o:o + w] for n, (o, w) in VOFF.items()}
        ident = c["ident"]

        x3 = X[:, :].rearrange("p (t n) -> p t n", t=2)
        y3 = Y[:, :].rearrange("p (t n) -> p t n", t=2)
        xT = XT[:, :].rearrange("p (j t) -> p j t", j=8)

        def ar(at, *shape):
            n = int(np.prod(shape))
            assert at + n <= 23500, (at, n)
            a = AR[:, at:at + n]
            if len(shape) == 2:
                return a.rearrange("p (a b) -> p a b", a=shape[0])
            if len(shape) == 3:
                return a.rearrange("p (a b c) -> p a b c", a=shape[0], b=shape[1])
            return a

        dsem = sem("s_dbg") if dbg else None
        dcnt = [0]

        def dump(name, ap, *deps):
            if name in dbg:
                dcnt[0] += 16
                P.dma("sp", dbg[name], ap, dsem, dcnt[0], *deps)
                P.wait("sp", [(dsem, dcnt[0])])
                for e in ("pe", "dve", "act", "pool"):
                    P.wait(e, [(dsem, dcnt[0])])

        s_c, s_x, s_p, s_m = sem("s_c"), sem("s_x"), sem("s_p"), sem("s_m")
        plan = []

        def add(name, n=None, order=None):
            a = dr[name]
            for i in (order if order is not None else range(a.shape[0])):
                plan.append((name, a[i], a.shape[2]))

        add("wkv", order=[0])
        add("swT")
        add("swk")
        add("swv")
        add("wo", order=[0, 1])
        add("fin")
        for i in range(6):
            n = SLOT if i < 5 else SLOT // 2
            plan.append(("fout", dr["fout"][i][:, 0:n], n))
        add("wkv", order=[1])
        add("foT")
        add("foqf")
        add("fov")
        add("fov2")
        add("wo", order=[2, 3])
        for e in range(NE1):
            for i in range(11):
                plan.append(("ein", dr["ein"][e, i], SLOT))
            for i in range(6):
                n = SLOT if i < 5 else SLOT // 2
                plan.append(("eout", dr["eout"][e, i][:, 0:n], n))
        add("u2")
        add("mqk2")
        add("mv2")
        add("z2")
        add("z2b")
        for i in range(EARLY):
            plan.append(("gate2", dr["gate2"][i], 3072))
        add("glu")
        for i in range(8):
            if i >= EARLY:
                plan.append(("gate2", dr["gate2"][i], 3072))
            if i % 2 == 0:
                plan.append(("up2", dr["up2"][i // 2], 3072))
        add("wo2")
        for q in range(NE2 // 4):
            for i in range(4):
                plan.append(("e2in", dr["e2in"][q, i], SLOT))
            for i in range(2):
                plan.append(("e2out", dr["e2out"][q, i], SLOT))
        n1 = [k for k, pl in enumerate(plan) if pl[0] == "e2in"][0]
        ring = Ring(P, [ringbuf[:, i * SLOT:(i + 1) * SLOT] for i in range(RING)], plan[:n1], start=0)

        mem = ar(18900, 2, D)
        s_i = sem("s_i")
        t_i = P.dma("sp", CST[:, 0:128], dr["cst"][:, 0:128], s_i, 16)
        t_m = P.dma("sp", mem, dr["mem"].rearrange("a (t p) d -> p (a t) d", p=128), s_m, 16)
        ring.load(None)
        t_x = P.dma("sp", x3, dr["x"].rearrange("a (t p) d -> p (a t) d", p=128), s_x, 16)
        ring.load(None)
        t_p = P.dma("sp", POS[:, :], dr["pos"], s_p, 16)
        t_c = P.dma("sp", CST[:, 128:], dr["cst"][:, 128:], s_c, 16)
        s_v = sem("s_v")
        t_v = P.dma("sp", VC[:, :], dr["vec"], s_v, 16)
        ring.load(None)
        ring.load(None)

        s_g = sem("s_g")
        gcount = [0]

        def load_gb(i, after):
            gcount[0] += 16
            return P.dma("sp", GB[:, :], dr["gb"][i], s_g, gcount[0], after)

        def transpose_rows(dstT, src3, ready, banks):
            toks = []
            for tt in range(2):
                for h in range(2):
                    b = banks[(2 * tt + h) % len(banks)]
                    for jj in range(4):
                        j = 4 * h + jj
                        last = P.tr(PB[b][:, jj * 128:jj * 128 + 128], src3[:, tt, j * 128:(j + 1) * 128], ident, ready[tt], t_i, bfree[b])
                    dst = dstT[:, 4 * h:4 * h + 4, tt * 128:tt * 128 + 128]
                    src = PB[b][:, :].rearrange("p (j t) -> p j t", j=4)
                    if h:
                        tk = P.act(lambda e, dst=dst, src=src: e.activation(dst, src, ACT.Copy), last)
                    else:
                        tk = P.dve(lambda e, dst=dst, src=src: e.tensor_copy(dst, src), last)
                    bfree[b] = tk
                    toks.append(tk)
            return toks

        def tile_T(outp, w, kt, col, m, rT, *deps, kstride=None):
            for j in range(kt):
                f = P.mml if j == kt - 1 else P.mm
                tk = f(outp, w[:, j, col:col + m], rT[:, j, :], j == 0, j == kt - 1, *deps)
            return tk

        def rows(outp, aT, tt, w, kt, col, n, *deps):
            for j in range(kt):
                f = P.mml if j == kt - 1 else P.mm
                tk = f(outp, aT[:, j, tt * 128:(tt + 1) * 128], w[:, j, col:col + n], j == 0, j == kt - 1, *deps)
            return tk

        def evac(dst, src, tok, eng, scale=None, *deps, par=False):
            if eng == "act":
                return P.act(lambda e: e.activation(dst, src, ACT.Copy, scale=1.0 if scale is None else scale), tok, *deps, par=par)
            if scale is None:
                return P.dve(lambda e: e.tensor_copy(dst, src), tok, *deps, par=par)
            return P.dve(lambda e: e.tensor_scalar(dst, src, scale, None, ALU.mult), tok, *deps, par=par)

        def proj_T(name, w, kt, ncol, rT, rdeps, dsts, banks, scales=None, eng=None):
            wap, wt = w
            w3 = wap.rearrange("p (j n) -> p j n", j=kt)
            toks = []
            for i, d in enumerate(dsts):
                b = banks[(i // 2) % len(banks)]
                o = (i % 2) * 256
                m = min(128, ncol - i * 128)
                tk = tile_T(PB[b][0:m, o:o + 256], w3, kt, i * 128, m, rT, wt, rdeps, bfree[b] if i % 2 == 0 else None)
                if i % 2 or i == len(dsts) - 1:
                    for k in range(i - i % 2, i + 1):
                        toks.append(evac(dsts[k], PB[b][0:m, (k % 2) * 256:(k % 2) * 256 + 256], tk,
                                         eng or ("act" if (i // 2) % 2 else "dve"), scales[k] if scales else None))
                    bfree[b] = toks[-1]
            return toks, tk

        def layer_norm(alpha, acc, acc_toks, gbtok, final=False):
            st = SM[:, 0:24].rearrange("p (t h s) -> p t h s", t=2, h=2)
            mv = SM[:, 24:28].rearrange("p (t s) -> p t s", t=2)
            sd = SM[:, 28:30]
            nb = SM[:, 30:32]
            toks, t3, t4 = [], [], []
            P.act(lambda e: e.activation(SM[:, 32:33], c["eps"], ACT.Sqrt), t_c)
            t5 = [None, None]

            def scale(tt):
                t = P.dve(lambda e: e.reciprocal(sd[:, tt:tt + 1], sd[:, tt:tt + 1]), t4[tt])
                t = P.dve(lambda e: e.scalar_tensor_tensor(nb[:, tt:tt + 1], mv[:, tt, 0:1], -1.0, sd[:, tt:tt + 1], ALU.mult, ALU.mult), t)
                t5[tt] = P.act(lambda e: e.activation(y3[:, tt, :], y3[:, tt, :], ACT.Identity, scale=sd[:, tt:tt + 1], bias=nb[:, tt:tt + 1]), t)

            for tt in range(2):
                bs = []
                for h in range(2):
                    a, at_ = acc(tt, h)
                    xs = x3[:, tt, h * 512:(h + 1) * 512]
                    ys = y3[:, tt, h * 512:(h + 1) * 512]
                    t1 = at_
                    if alpha is not None:
                        t1 = P.dve(lambda e, a=a, xs=xs, ys=ys: e.scalar_tensor_tensor(ys, xs, alpha, a, ALU.mult, ALU.add), at_, par=h == 1)
                    acc_toks(tt, h, t1)
                    bs.append(t1)
                for h in range(2):
                    ys = y3[:, tt, h * 512:(h + 1) * 512]
                    bs[h] = P.dve(lambda e, tt=tt, h=h, ys=ys: e.bn_stats(st[:, tt, h, :], ys), bs[h], par=True)
                    if tt and not h:
                        scale(0)
                t3.append(P.dve(lambda e, tt=tt: e.bn_aggr(mv[:, tt, :], st[:, tt, :, :]), bs))
                t4.append(P.act(lambda e, tt=tt: e.activation(sd[:, tt:tt + 1], mv[:, tt, 1:2], ACT.Sqrt, bias=c["eps"]), t3[tt], t_c))
            t7 = P.dve(lambda e: e.tensor_tensor(y3[:, 0, :], y3[:, 0, :], GB[:, 0:D], ALU.mult), t5[0], gbtok)
            toks.append(P.pool(lambda e: e.tensor_tensor(x3[:, 0, :], y3[:, 0, :], GB[:, D:2 * D], ALU.add), t7))
            scale(1)
            t7 = P.dve(lambda e: e.tensor_tensor(y3[:, 1, :], y3[:, 1, :], GB[:, 0:D], ALU.mult), t5[1])
            toks.append(P.dve(lambda e: e.tensor_tensor(x3[:, 1, :], y3[:, 1, :], GB[:, D:2 * D], ALU.add), t7))
            return toks

        def attention(heads, wbuf):
            fin = []
            for _ in attention_steps(heads, wbuf, fin):
                pass
            return fin

        def attention_steps(heads, wbuf, fin, ob=(4, 5)):
            S = [ar(wbuf + 512 * i, 512) for i in range(3)]
            PT = [ar(wbuf + 1536 + 512 * i, 512) for i in range(2)]
            n = len(heads)
            st = [dict() for _ in heads]
            sfree, ptfree = [None] * 3, [None] * 2
            stat = SM[:, 64:64 + 8 * 16].rearrange("p (h s) -> p h s", h=16)

            def A(i):
                h, s = heads[i], st[i]
                b = i % 2
                full = h["kind"] == "mem"
                w0 = 256 if full else 128
                s["w0"], s["wd"] = w0, w0 + 256
                for qt in range(2):
                    o = PB[b][:, 0:w0] if qt == 0 else PB[b][:, w0:w0 + 256]
                    kw = w0 if qt == 0 else 256
                    more = "cq" in h
                    f = P.mm if more else P.mml
                    tk = f(o, h["q"][:, qt * 128:(qt + 1) * 128], h["k"][:, 0:kw], True, not more, h["deps"], bfree[b])
                    if more:
                        tk = P.mml(o, h["cq"][:, qt * 128:(qt + 1) * 128], h["ck"][:, 0:kw], False, True)
                s["A"] = tk

            def B(i):
                h, s = heads[i], st[i]
                b, w0, wd = i % 2, s["w0"], s["wd"]
                sb_, hs = S[i % 3], stat[:, i % 16, :]
                src = PB[b]
                if h["kind"] == "mem":
                    t1 = s["A"]
                    srcs = PB[b]
                else:
                    if h["kind"] == "moba":
                        t1 = P.dve(lambda e: e.scalar_tensor_tensor(sb_[:, 0:wd], c["dist"], h["slope"], src[:, 0:wd],
                                                                    ALU.mult, ALU.add), s["A"], sfree[i % 3], t_c)
                    else:
                        mk = c["swa"] if h["kind"] == "swa" else c["caus"]
                        t1 = P.dve(lambda e: e.tensor_tensor(sb_[:, 0:wd], src[:, 0:wd], mk, ALU.add), s["A"], sfree[i % 3], t_c)
                    bfree[b] = t1
                    srcs = sb_
                t2 = P.dve(lambda e: e.tensor_reduce(hs[:, 0:1], srcs[:, 0:w0], AX.X, ALU.max, negate=True), t1)
                t2 = P.dve(lambda e: e.tensor_reduce(hs[:, 1:2], srcs[:, w0:wd], AX.X, ALU.max, negate=True), t1, par=True)
                if "sink" in h:
                    sk = v["sink"][:, h["sink"]:h["sink"] + 1]
                    t2 = P.dve(lambda e: e.tensor_scalar(hs[:, 0:2], hs[:, 0:2], nsink[:, h["sink"]:h["sink"] + 1], None, ALU.min), t2)
                    t3 = P.dve(lambda e: e.tensor_scalar(hs[:, 4:6], hs[:, 0:2], sk, None, ALU.add), t2)
                    t4 = P.act(lambda e: e.activation(hs[:, 4:6], hs[:, 4:6], ACT.Exp), t3)
                    s["sk"] = t4
                ta = P.act(lambda e: e.activation(sb_[:, 0:w0], srcs[:, 0:w0], ACT.Exp, bias=hs[:, 0:1], accum_out=hs[:, 2:3]), t2, sfree[i % 3])
                tb = P.act(lambda e: e.activation(sb_[:, w0:wd], srcs[:, w0:wd], ACT.Exp, bias=hs[:, 1:2], accum_out=hs[:, 3:4]), t2, par=True)
                if h["kind"] == "mem":
                    bfree[b] = tb
                s["B"] = tb

            def C(i):
                h, s = heads[i], st[i]
                w0, wd = s["w0"], s["wd"]
                sb_, hs = S[i % 3], stat[:, i % 16, :]
                t = s["B"]
                if "sink" in h:
                    t = P.dve(lambda e: e.tensor_tensor(hs[:, 2:4], hs[:, 2:4], hs[:, 4:6], ALU.add), t, s["sk"])
                t = P.dve(lambda e: e.reciprocal(hs[:, 2:4], hs[:, 2:4]), t)
                tc0 = P.dve(lambda e: e.tensor_scalar(sb_[:, 0:w0], sb_[:, 0:w0], hs[:, 2:3], None, ALU.mult), t)
                s["C"] = [tc0, P.dve(lambda e: e.tensor_scalar(sb_[:, w0:wd], sb_[:, w0:wd], hs[:, 3:4], None, ALU.mult), t, par=True)]

            def Dd(i):
                h, s = heads[i], st[i]
                w0, wd = s["w0"], s["wd"]
                sb_, b = S[i % 3], 2 + i % 2
                pt = PT[i % 2]
                P.tr(PB[b][:, 0:128], sb_[:, 0:128], ident, s["C"], bfree[b])
                P.tr(PB[b][:, 128:256], sb_[:, w0:w0 + 128], ident)
                if w0 == 256:
                    P.tr(PB[b][:, 256:384], sb_[:, 128:256], ident)
                tk = P.tr(PB[b][:, wd - 128:wd], sb_[:, w0 + 128:w0 + 256], ident)
                sfree[i % 3] = tk
                s["D"] = evac(pt[:, 0:wd], PB[b][:, 0:wd], tk, "act" if i % 2 else "dve", None, ptfree[i % 2])
                bfree[b] = s["D"]

            def Ee(i):
                h, s = heads[i], st[i]
                w0, wd = s["w0"], s["wd"]
                b, base = ob[(i // 2) % len(ob)], h["base"]
                pt = PT[i % 2]
                o = PB[b][base:base + 64, :]
                P.mm(o[:, 0:256], h["v"][0], pt[:, 0:256], True, False, s["D"], h["vdeps"], bfree[b] if i % 2 == 0 else None)
                q0 = 0 if w0 == 256 else 128
                tk = P.mml(o[:, q0:256], h["v"][1], pt[:, 256:wd], False, True)
                ptfree[i % 2] = tk
                if i % 2:
                    e = evac(h["out"], PB[b][:, 0:256], tk, "dve" if i % 4 == 1 else "act")
                    bfree[b] = e
                    fin.append(e)

            for i in range(n + 3):
                if i < n:
                    A(i)
                    B(i)
                yield
                if 0 <= i - 1 < n:
                    C(i - 1)
                if 0 <= i - 2 < n:
                    Dd(i - 2)
                yield
                if 0 <= i - 3 < n:
                    Ee(i - 3)

        def sincos(ang, sn, cs, tmp, tok):
            t = P.dve(lambda e: e.tensor_scalar(tmp, ang, 1.0 / TWO_PI, MAGIC, ALU.mult, ALU.add), tok)
            t = P.dve(lambda e: e.tensor_scalar(tmp, tmp, MAGIC, None, ALU.subtract), t)
            for k in (PI_A, PI_B, PI_C):
                t = P.dve(lambda e, k=k: e.scalar_tensor_tensor(ang, tmp, -k, ang, ALU.mult, ALU.add), t)
            t = P.dve(lambda e: e.tensor_scalar(ang, ang, 3.1415925, -3.1415925, ALU.min, ALU.max), t)
            ts = P.act(lambda e: e.activation(sn, ang, ACT.Sin), t)
            tc = P.act(lambda e: e.activation(cs, ang, ACT.Sin, scale=0.5), t)
            tc = P.dve(lambda e: e.tensor_tensor(cs, cs, cs, ALU.mult), tc)
            tc = P.dve(lambda e: e.tensor_scalar(cs, cs, -2.0, 1.0, ALU.mult, ALU.add), tc)
            return [ts, tc]

        def w_out(name, mixT, deps):
            tk = {}
            for h in range(2):
                w = ring.take(name)
                w3 = w[0].rearrange("p (j n) -> p j n", j=8)
                for tt in range(2):
                    b = 2 * h + tt
                    tk[(tt, h)] = rows(PB[b][:, :], mixT, tt, w3, 8, 0, 512, w[1], deps, bfree[b])
                ring.release(tk[(1, h)])
            return tk

        def add_norm(alpha, tk, gb):
            def acc(tt, h):
                return PB[2 * h + tt][:, :], tk[(tt, h)]

            def done(tt, h, t):
                bfree[2 * h + tt] = t

            return layer_norm(alpha, acc, done, gb)

        def ffn(kin, kout, nf, hT, xdeps, nin, hfree, accb, obanks=(0, 1, 2, 3), ring=ring):
            npair = nin
            f = 0
            toks = []
            while f < nf:
                w = ring.take(kin)
                w3 = w[0].rearrange("p (j n) -> p j n", j=8)
                for i in range(npair):
                    b = accb[f % len(accb)]
                    ta = tile_T(PB[b][:, 0:256], w3, 8, i * 128, 128, xT, w[1], xdeps, bfree[b])
                    tb = tile_T(PB[b][:, 256:512], w3, 8, (npair + i) * 128, 128, xT)
                    dst = hT[:, f, :]
                    t1 = P.act(lambda e, dst=dst, b=b: e.activation(dst, PB[b][:, 0:256], ACT.Silu), tb, hfree)
                    t2 = P.dve(lambda e, dst=dst, b=b: e.tensor_tensor(dst, dst, PB[b][:, 256:512], ALU.mult), t1, tb)
                    bfree[b] = t2
                    toks.append(t2)
                    f += 1
                ring.release(tb)
            tk = {}
            f = 0
            while f < nf:
                w = ring.take(kout)
                nk = w[0].shape[1] // 1024
                w3 = w[0].rearrange("p (j n) -> p j n", j=nk)
                jt = [(j, tt) for j in range(nk) for tt in range(2)]
                if f + nk == nf:
                    jt = [(j, tt) for tt in range(2) for j in range(nk)]
                for j, tt in jt:
                    for h in range(2):
                        b = obanks[2 * h + tt]
                        g = P.mml if (f + j == nf - 1 or j == nk - 1) else P.mm
                        r = g(PB[b][:, :], hT[:, f + j, tt * 128:(tt + 1) * 128], w3[:, j, h * 512:(h + 1) * 512],
                              f + j == 0, f + j == nf - 1, w[1], toks[f + j], bfree[b] if f + j == 0 else None)
                        if f + j == nf - 1:
                            tk[(tt, h)] = r
                f += nk
                ring.release(r)
            return tk, r

        qT = ar(0, 6, T)
        kT = ar(1536, 6, T)
        qcT = ar(3072, 2, T)
        Vn = ar(3584, 2, 768)
        kmT = ar(5120, 2, T)
        vmn = ar(5632, 2, T)
        mixT = ar(6144, 8, T)
        memT = ar(8192, 8, T)
        WB = 10240
        rC, rS = ar(12800, T), ar(13056, T)
        rt1, rt2 = ar(13312, T), ar(13568, T)
        cumT, A2, B2 = ar(13824, T), ar(14080, 12, T), ar(17152, 12, T)

        tmT = transpose_rows(memT, mem, [t_m, t_m], [4, 5, 6, 7])
        txT = transpose_rows(xT, x3, [t_x, t_x], [4, 5, 6, 7])

        t = P.dve(lambda e: e.tensor_copy(rt1, POS[:, :]), t_p)
        t = P.dve(lambda e: e.tensor_scalar(rt1, rt1, c["inv"], None, ALU.mult), t, t_c)
        t_rope = sincos(rt1, rS, rC, rt2, t)

        def mem_kv():
            w = ring.take("wkv")
            w3 = w[0].rearrange("p (j n) -> p j n", j=8)
            tk, _ = [], None
            for i in range(2):
                b = 6
                p_ = tile_T(PB[b][:, i * 256:i * 256 + 256], w3, 8, i * 128, 128, memT, w[1], tmT, bfree[b] if i == 0 else None, wfree[0])
            for i in range(2):
                tk.append(evac(kmT[:, i, :], PB[b][:, i * 256:i * 256 + 256], p_, "act", None, wfree[0]))
            bfree[6] = tk[-1]
            for tt in range(2):
                b = 7
                p_ = rows(PB[b][:, tt * 256:tt * 256 + 256], memT, tt, w3, 8, 256, 256, bfree[b] if tt == 0 else None)
            for tt in range(2):
                tk.append(evac(vmn[:, tt, :], PB[b][:, tt * 256:tt * 256 + 256], p_, "dve"))
            bfree[7] = tk[-1]
            ring.release(p_)
            return tk

        wfree = [None]
        t_kv = mem_kv()

        def take_T(name, dsts, scales, ncol, banks, rdeps, eng=None):
            w = ring.take(name)
            toks, last = proj_T(name, w, 8, ncol, xT, rdeps, dsts, banks, scales, eng)
            ring.release(last)
            return toks

        tq = take_T("swT", [qT[:, i, :] for i in range(4)], [0.125] * 4, 512, [4, 5], txT)
        tq2 = take_T("swT", [qT[:, 4, :], qT[:, 5, :], qcT[:, 0, :], qcT[:, 1, :]], [0.125] * 4, 512, [4, 5], txT)
        w = ring.take("swk")
        tk_, last = proj_T("swk", w, 8, 384, xT, txT, [kT[:, i, :] for i in range(3)], [4, 5])
        ring.release(last)
        tq = tq + tq2[0:2]
        tqc = tq2[2:4]

        def rope(ap, tok, b):
            p_ = P.mml(PB[b][:, 0:256], c["rot"], ap, True, True, tok, t_c, bfree[b])
            i1 = P.dve(lambda e: e.tensor_tensor(rt1, PB[b][:, 0:256], rS, ALU.mult), p_, t_rope)
            bfree[b] = i1
            i2 = P.dve(lambda e: e.tensor_tensor(ap, ap, rC, ALU.mult), p_)
            return P.dve(lambda e: e.tensor_tensor(ap, ap, rt1, ALU.add), i1, i2)

        tq = [rope(qT[:, i, :], tq[i], 4 + i % 2) for i in range(6)]
        tk_ = [rope(kT[:, i, :], tk_[i], 4 + i % 2) for i in range(3)]
        w = ring.take("swv")
        w3 = w[0].rearrange("p (j n) -> p j n", j=8)
        tv = []
        for tt in range(2):
            p_ = rows(PB[6 + tt][:, 0:192], xT, tt, w3, 8, 0, 192, w[1], bfree[6 + tt])
            bfree[6 + tt] = evac(Vn[:, tt, 0:192], PB[6 + tt][:, 0:192], p_, "act" if tt else "dve")
            tv.append(bfree[6 + tt])
        ring.release(p_)
        heads = []
        for h in range(12):
            b = 64 * (h % 2)
            g = h // 4
            heads.append(dict(kind="swa", q=qT[b:b + 64, h // 2, :], k=kT[b:b + 64, g, :], base=b, sink=h,
                              deps=[tq[h // 2], tk_[g]], v=[Vn[:, 0, g * 64:g * 64 + 64], Vn[:, 1, g * 64:g * 64 + 64]],
                              vdeps=tv, out=mixT[:, h // 2, :]))

        def mem_heads():
            r = []
            for h in range(4):
                b = 64 * (h % 2)
                r.append(dict(kind="mem", q=qcT[b:b + 64, h // 2, :], k=kmT[b:b + 64, h // 2, :], base=b,
                              deps=[tqc[h // 2], t_kv[h // 2]], v=[vmn[:, 0, h * 64:h * 64 + 64], vmn[:, 1, h * 64:h * 64 + 64]],
                              vdeps=t_kv, out=mixT[:, 6 + h // 2, :]))
            return r

        nsink = SM[:, 34:46]
        P.dve(lambda e: e.tensor_scalar(nsink, v["sink"], -1.0, None, ALU.mult), t_v)
        t_gb = load_gb(0, None)
        fin = attention(heads + mem_heads(), WB)
        dump("mix0", mixT, fin)
        tk = w_out("wo", mixT, fin)
        tx = add_norm(ALPHA1, tk, t_gb)
        dump("ln0", x3, tx)
        t_gb = load_gb(1, tx)
        txT = transpose_rows(xT, x3, tx, [4, 5, 6, 7])
        hT = ar(10240, 22, T)
        ftk, _ = ffn("fin", "fout", 22, hT, txT, 2, fin, [4, 5, 6, 7])
        wfree[0] = fin
        t_kv = mem_kv()
        tx = add_norm(ALPHA1, ftk, t_gb)
        dump("ln1", x3, tx)
        t_gb = load_gb(2, tx)
        txT = transpose_rows(xT, x3, tx, [4, 5, 6, 7])
        hdone = [ftk[(1, 1)]]

        tq, tk_ = [], []
        for i in range(3):
            ds = [(qT[:, j, :] if j < 6 else kT[:, j - 6, :]) for j in range(4 * i, 4 * i + 4)]
            sc = [(0.125 if j < 6 else None) for j in range(4 * i, 4 * i + 4)]
            tq += take_T("foT", ds, sc, 512, [4, 5], txT)
        tk_ = tq[6:]
        w = ring.take("foqf")
        w3 = w[0].rearrange("p (j n) -> p j n", j=8)
        toks, last = proj_T("foqf", w, 8, 256, xT, txT, [qcT[:, 0, :], qcT[:, 1, :]], [4], [0.125] * 2)
        tqc = toks
        pf = tile_T(PB[5][0:12, 0:256], w3, 8, 256, 12, xT, bfree[5])
        ring.release(pf)
        f12, e12 = rt1[0:12, :], rt2[0:12, :]
        cum12, g12 = cumT[0:12, :], rC[0:12, :]
        t = P.dve(lambda e: e.tensor_scalar(f12, PB[5][0:12, 0:256], v["bf"][0:12, :], None, ALU.add), pf, hdone)
        bfree[5] = t
        ta = P.act(lambda e: e.activation(e12, f12, ACT.Abs), t)
        ta = P.act(lambda e: e.activation(e12, e12, ACT.Exp, scale=-1.0), ta)
        ta = P.dve(lambda e: e.tensor_scalar(e12, e12, 1.0, None, ALU.add), ta)
        ta = P.act(lambda e: e.activation(e12, e12, ACT.Ln), ta)
        t = P.dve(lambda e: e.tensor_scalar(f12, f12, 0.0, None, ALU.min), t)
        t = P.dve(lambda e: e.tensor_tensor(f12, f12, e12, ALU.subtract), t, ta)
        t1 = P.dve(lambda e: e.memset(g12, 1.0), hdone)
        t1 = P.dve(lambda e: e.tensor_tensor_scan(cum12, g12, f12, 0.0, ALU.mult, ALU.add), t, t1)
        t2 = P.dve(lambda e: e.tensor_scalar(f12, cum12, -1.0, None, ALU.mult), t1)
        m1 = P.dve(lambda e: e.memset(A2[0:2, :, :], 1.0), hdone)
        m2 = P.dve(lambda e: e.memset(B2[0:2, :, :], 1.0), hdone)
        s_ab = sem("s_ab")
        tab = P.dma("act", A2[0:1, :, :], cum12, s_ab, 16, t1, m1)
        s_ab2 = sem("s_ab2")
        tab2 = P.dma("act", B2[1:2, :, :], f12, s_ab2, 16, t2, m2)
        tv = []
        for ci, (n0, nn) in enumerate(((0, 512), (512, 256))):
            w = ring.take("fov" if ci == 0 else "fov2")
            w3 = w[0].rearrange("p (j n) -> p j n", j=8)
            for tt in range(2):
                b = 6 + tt
                p_ = rows(PB[b][:, 0:nn], xT, tt, w3, 8, 0, nn, w[1], bfree[b])
                bfree[b] = evac(Vn[:, tt, n0:n0 + nn], PB[b][:, 0:nn], p_, "act" if tt else "dve")
                tv.append(bfree[b])
            ring.release(p_)
        heads = []
        for h in range(12):
            b = 64 * (h % 2)
            heads.append(dict(kind="fox", q=qT[b:b + 64, h // 2, :], k=kT[b:b + 64, h // 2, :], base=b,
                              cq=A2[0:2, h, :], ck=B2[0:2, h, :], deps=[tq[h // 2], tk_[h // 2], tab, tab2],
                              v=[Vn[:, 0, h * 64:h * 64 + 64], Vn[:, 1, h * 64:h * 64 + 64]],
                              vdeps=tv, out=mixT[:, h // 2, :]))
        fin = attention(heads + mem_heads(), WB)
        dump("mix1", mixT, fin)
        s_r = sem("s_r")
        RW = ar(0, 8, 36)
        t_r = P.dma("act", RW[:, :, 0:8], dr["wr1"], s_r, 16, fin)
        tk = w_out("wo", mixT, fin)
        tx = add_norm(ALPHA1, tk, t_gb)
        dump("ln2", x3, tx)
        t_gb = load_gb(3, tx)
        txT = transpose_rows(xT, x3, tx, [4, 5, 6, 7])

        def warm(func):
            P.act(lambda e: e.activation(SM[:, 33:34], c["eps"], func), t_c)

        def top2(L, n, O, g, tok, base, scale=None):
            mx = SM[:, base:base + 16].rearrange("p (t k) -> p t k", t=2)
            ixf = SM[:, base + 16:base + 32].rearrange("p (t k) -> p t k", t=2)
            ix = IX[:, 0:16].rearrange("p (t k) -> p t k", t=2)
            df = SM[:, base + 32:base + 34].unsqueeze(2)
            t0 = P.dve(lambda e: e.max(mx[:, 0, :], L[:, 0, :]), tok)
            t1 = P.dve(lambda e: e.max(mx[:, 1, :], L[:, 1, :]), tok, par=True)
            td = P.dve(lambda e: e.tensor_tensor(df, mx[:, :, 1:2], mx[:, :, 0:1], ALU.subtract), t0, t1)
            ta = P.act(lambda e: e.activation(df, df, ACT.Exp), td)
            t0 = P.dve(lambda e: e.max_index(ix[:, 0, :], mx[:, 0, :], L[:, 0, :]), t0, par=True)
            t1 = P.dve(lambda e: e.max_index(ix[:, 1, :], mx[:, 1, :], L[:, 1, :]), t1, par=True)
            t = P.dve(lambda e: e.tensor_copy(ixf, ix), t0, t1)
            io = c["iota"][:, 0:n].unsqueeze(1).to_broadcast([128, 2, n])
            to = []
            for tt in range(2):
                i2 = ixf[:, tt, 0:2].unsqueeze(2).to_broadcast([128, 2, n])
                to.append(P.dve(lambda e, tt=tt, i2=i2: e.tensor_tensor(O[:, tt, :, :], io, i2, ALU.is_equal), t, par=tt == 1))
            g0, g1 = g[:, :, 0:1], g[:, :, 1:2]
            tb = P.dve(lambda e: e.tensor_scalar(g0, df, 1.0, None, ALU.add), ta, par=True)
            tb = P.dve(lambda e: e.reciprocal(g0, g0), tb)
            if scale is not None:
                tb = P.dve(lambda e: e.tensor_tensor(g0, g0, scale[0], ALU.mult), tb, scale[1])
            tb = P.dve(lambda e: e.tensor_tensor(g1, g0, df, ALU.mult), tb)
            return to, tb

        def gates(G, O, g, n, deps):
            for tt in range(2):
                t = P.dve(lambda e, tt=tt: e.tensor_scalar(G[:, tt, :], O[:, tt, 0, :], g[:, tt, 0:1], None, ALU.mult), deps, par=tt == 1)
            for tt in range(2):
                t = P.dve(lambda e, tt=tt: e.scalar_tensor_tensor(G[:, tt, :], O[:, tt, 1, :], g[:, tt, 1:2], G[:, tt, :],
                                                                  ALU.mult, ALU.add), t, par=tt == 1)
            return t

        G1 = ar(512, 2, 8)
        L1 = ar(544, 2, 8)
        O1 = ar(576, 2, 2, 8)
        gt = ar(640, 2, 2)
        warm(ACT.Exp)
        for tt in range(2):
            p_ = rows(PB[3][:, tt * 8:tt * 8 + 8], xT, tt, RW[:, :, 0:8], 8, 0, 8, t_r, txT, bfree[3] if tt == 0 else None)
        b2 = v["br1"].unsqueeze(1).to_broadcast([128, 2, 8])
        t = P.dve(lambda e: e.tensor_tensor(L1, PB[3][:, 0:16].rearrange("p (t k) -> p t k", t=2), b2, ALU.add), p_)
        bfree[3] = t
        toh, tg_ = top2(L1, 8, O1, gt, t, 256)

        def tgate1():
            return gates(G1, O1, gt, 8, [toh, tg_])


        def moe_dense(kin, kout, ne, nf, G, gdeps, hTs, xd, ta0, ring):
            acct = [[None, None], [None, None]]
            hfree = [None, None]
            for e_ in range(ne):
                tk, r = ffn(kin, kout, nf, hTs[e_ % len(hTs)], xd, 2, hfree[e_ % len(hTs)], [4, 5, 6, 7], ring=ring)
                hfree[e_ % len(hTs)] = r
                for tt in range(2):
                    for h in range(2):
                        ys = y3[:, tt, h * 512:(h + 1) * 512]
                        b = 2 * h + tt
                        gcol = G[:, tt, e_:e_ + 1]
                        t = P.dve(lambda e, ys=ys, b=b, gcol=gcol: e.scalar_tensor_tensor(ys, PB[b][:, :], gcol, ys, ALU.mult, ALU.add),
                                  tk[(tt, h)], acct[tt][h])
                        bfree[b] = t
                        acct[tt][h] = t
            return acct

        def overflow(tag, plan_, kin, kout, ne, nf, G, flag):
            keep = list(bfree)
            P.open(tag)
            for i in range(8):
                bfree[i] = None
            r2 = Ring(P, [ar(1024 + i * SLOT, SLOT) for i in range(3)], plan_, tag + "_w")
            moe_dense(kin, kout, ne, nf, G, None, [ar(1024 + 3 * SLOT, nf, T)], None, None, r2)
            P.close(flag)
            for i in range(8):
                bfree[i] = keep[i]

        def slots(ne, cap, O, G, pos, over, cnt, flag, flagf, deps, gates_of):
            M = cnt
            t = P.dve(lambda e: e.tensor_tensor(M, O[:, :, 0, :], O[:, :, 1, :], ALU.add), deps)
            b = 3
            P.mm(PB[b][:, 0:ne], c["su"], M[:, 0, :], True, True, t, bfree[b])
            P.mm(PB[b][:, ne:2 * ne], c["su"], M[:, 1, :], True, False)
            P.mml(PB[b][:, ne:2 * ne], c["ones"], M[:, 0, :], False, True)
            P.mm(PB[b][:, 2 * ne:3 * ne], c["ones"], M[:, 0, :], True, False)
            p1 = P.mml(PB[b][:, 2 * ne:3 * ne], c["ones"], M[:, 1, :], False, True)
            tg = gates_of()
            rank = PB[b][:, 0:2 * ne].rearrange("p (t k) -> p t k", t=2)
            t = P.dve(lambda e: e.scalar_tensor_tensor(pos, rank, 1.0, M, ALU.add, ALU.mult), p1)
            tpos = P.dve(lambda e: e.tensor_scalar(pos, pos, -1.0, None, ALU.add), t)

            def rest():
                t = P.dve(lambda e: e.scalar_tensor_tensor(over, rank, float(cap), G, ALU.is_ge, ALU.mult), tg)
                t = P.dve(lambda e: e.tensor_reduce(flagf, PB[b][:, 2 * ne:3 * ne], AX.X, ALU.max), par=True)
                bfree[b] = t
                t = P.dve(lambda e: e.tensor_scalar(flagf, flagf, float(cap), None, ALU.is_gt), t)
                P.dve(lambda e: e.tensor_copy(flag, flagf), t)
            return [tpos, tg], rest

        def moe1():
            pos, over, cnt = ar(672, 2, 8), ar(688, 2, 8), ar(704, 2, 8)
            flag, flagf = IX[:, 32:33], SM[:, 850:851]
            tpos, rest = slots(NE1, 128, O1, G1, pos, over, cnt, flag, flagf, toh, tgate1)
            PS, PG = [ar(1024 + 256 * i, 2, 128) for i in range(2)], [ar(1536 + 256 * i, 2, 128) for i in range(2)]
            PGT = [ar(2048 + 256 * i, 256) for i in range(2)]
            XG = [ar(2560 + 1024 * i, 8, 128) for i in range(2)]
            HN = [ar(4608 + 256 * i, 256) for i in range(3)]
            HT = [ar(5376 + 2816 * i, 22, 128) for i in range(2)]
            YS = [ar(11008 + 1024 * i, 1024) for i in range(2)]
            acc = {}
            st = [dict() for _ in range(NE1)]

            def select(e_):
                i, d = e_ % 2, st[e_]
                for tt in range(2):
                    t = P.dve(lambda e, tt=tt, i=i: e.tensor_scalar(PS[i][:, tt, :], c["iota"], pos[:, tt, e_:e_ + 1], None, ALU.is_equal),
                              tpos, st[e_ - 2]["gath"] if e_ >= 2 else None)
                    t = P.dve(lambda e, tt=tt, i=i: e.tensor_scalar(PG[i][:, tt, :], PS[i][:, tt, :], G1[:, tt, e_:e_ + 1], None, ALU.mult),
                              st[e_ - 2]["pgt"] if e_ >= 2 else None)
                d["sel"] = t

            def gather(e_):
                i, d = e_ % 2, st[e_]
                d["xg"] = []
                for q in range(2):
                    b = 6 + q
                    for k in range(4):
                        for tt in range(2):
                            dt_ = 4 * q + k
                            tk = (P.mml if tt else P.mm)(PB[b][:, k * 128:(k + 1) * 128], x3[:, tt, dt_ * 128:(dt_ + 1) * 128], PS[i][:, tt, :],
                                                         tt == 0, tt == 1, d["sel"], tx, bfree[b])
                    bfree[b] = evac(XG[i][:, 4 * q:4 * q + 4, :].rearrange("p a b -> p (a b)"), PB[b][:, :], tk, "dve", None,
                                    st[e_ - 2]["in"] if e_ >= 2 else None)
                    d["xg"].append(bfree[b])
                d["gath"] = tk
                for tt in range(2):
                    tk = P.tr(PB[6][:, tt * 128:(tt + 1) * 128], PG[i][:, tt, :], ident, bfree[6])
                d["pgt"] = tk
                bfree[6] = evac(PGT[i], PB[6][:, 0:256], tk, "act", None, st[e_ - 2]["scat"] if e_ >= 2 else None)
                d["pg"] = bfree[6]

            def turn(e_, f2, th_, hn):
                i, b = e_ % 2, 6 + f2 % 2
                for k in range(2):
                    tk = P.tr(PB[b][:, k * 128:(k + 1) * 128], hn[:, k * 128:(k + 1) * 128], ident, th_, bfree[b])
                hnfree[f2 % 3] = tk
                bfree[b] = evac(HT[i][:, 2 * f2:2 * f2 + 2, :].rearrange("p a b -> p (a b)"), PB[b][:, 0:256], tk,
                                "act" if f2 % 2 else "dve", None, st[e_ - 2]["down"] if e_ >= 2 else None)
                st[e_].setdefault("ht", []).append(bfree[b])

            def scatter(e_):
                i, d = e_ % 2, st[e_]
                for tt in range(2):
                    for h in range(2):
                        b = 2 + h
                        tk = P.mml(PB[b][:, :], PGT[i][:, tt * 128:(tt + 1) * 128], YS[i][:, h * 512:(h + 1) * 512], True, True,
                                   d["pg"], d["ys"], bfree[b])
                        ys = y3[:, tt, h * 512:(h + 1) * 512]
                        bfree[b] = P.dve(lambda e, ys=ys, b=b: e.tensor_tensor(ys, ys, PB[b][:, :], ALU.add), tk, acc[(tt, h)])
                        acc[(tt, h)] = bfree[b]
                d["scat"] = tk

            hnfree = [None] * 3
            select(0)
            gather(0)
            rest()
            tz = P.dve(lambda e: e.tensor_scalar(Y[:, :], X[:, :], ALPHA1, None, ALU.mult), tx)
            for tt in range(2):
                for h in range(2):
                    acc[(tt, h)] = tz
            for e_ in range(NE1):
                i, d = e_ % 2, st[e_]
                pend = None
                for f2 in range(11):
                    w = ring.take("ein")
                    w3 = w[0].rearrange("p (j n) -> p j n", j=8)
                    b = 4 + f2 % 2
                    for k in range(8):
                        tk = (P.mml if k == 7 else P.mm)(PB[b][:, :], XG[i][:, k, :], w3[:, k, :], k == 0, k == 7, w[1], d["xg"], bfree[b])
                    ring.release(tk)
                    hn = HN[f2 % 3]
                    t1 = P.act(lambda e, hn=hn, b=b: e.activation(hn, PB[b][:, 0:256], ACT.Silu), tk, hnfree[f2 % 3])
                    t2 = P.dve(lambda e, hn=hn, b=b: e.tensor_tensor(hn, hn, PB[b][:, 256:512], ALU.mult), t1)
                    bfree[b] = t2
                    if pend:
                        turn(*pend)
                    pend = (e_, f2, t2, hn)
                    if f2 == 1 and e_:
                        scatter(e_ - 1)
                    if f2 == 4 and e_ + 1 < NE1:
                        select(e_ + 1)
                    if f2 == 7 and e_ == 0:
                        s5_coefficients()
                d["in"] = tk
                if e_ + 1 < NE1:
                    gather(e_ + 1)
                turn(*pend)
                f = 0
                for ci in range(6):
                    w = ring.take("eout")
                    nk = w[0].shape[1] // 1024
                    w3 = w[0].rearrange("p (j n) -> p j n", j=nk)
                    for j in range(nk):
                        for h in range(2):
                            tk = (P.mml if j == nk - 1 else P.mm)(PB[h][:, :], HT[i][:, f, :], w3[:, j, h * 512:(h + 1) * 512], f == 0, f == 21,
                                                                  w[1], d["ht"][f // 2], bfree[h] if f == 0 else None)
                        f += 1
                    ring.release(tk)
                d["down"] = tk
                fr = st[e_ - 2]["scat"] if e_ >= 2 else None
                bfree[0] = evac(YS[i][:, 0:512], PB[0][:, :], tk, "act", None, fr)
                bfree[1] = evac(YS[i][:, 512:1024], PB[1][:, :], tk, "dve", None, fr)
                d["ys"] = [bfree[0], bfree[1]]
            scatter(NE1 - 1)
            pl = []
            for e_ in range(NE1):
                pl += [("ein", dr["ein"][e_, i], SLOT) for i in range(11)]
                pl += [("eout", dr["eout"][e_, i][:, 0:(SLOT if i < 5 else SLOT // 2)], SLOT if i < 5 else SLOT // 2) for i in range(6)]
            overflow("o1", pl, "ein", "eout", NE1, 22, over, flag[0:1, :])
            return [[acc[(tt, h)] for h in range(2)] for tt in range(2)]

        s5v = SM[:, 320:320 + 16 * 14].rearrange("p (k g) -> p k g", k=14)
        dt5, th5, mag, co, si, t0, t1_, t2_, cr, ci5, den, lr, li, x4 = [s5v[:, k, :] for k in range(14)]
        s5t = {}

        def s5_coefficients():
            t = P.act(lambda e: e.activation(dt5, v["ldt"], ACT.Exp), t_v)
            tth = P.dve(lambda e: e.tensor_tensor(th5, v["aim"], dt5, ALU.mult), t, t_v)
            tm = P.dve(lambda e: e.tensor_tensor(mag, v["are"], dt5, ALU.mult), t)
            tm = P.act(lambda e: e.activation(mag, mag, ACT.Exp), tm)
            tsc = sincos(th5, si, co, t0, tth)
            t = P.dve(lambda e: e.tensor_tensor(lr, mag, co, ALU.mult), tm, tsc)
            tl = P.dve(lambda e: e.tensor_scalar(lr, lr, -1.0, None, ALU.add), t)
            tli = P.dve(lambda e: e.tensor_tensor(li, mag, si, ALU.mult), tm, tsc)
            ta = P.dve(lambda e: e.tensor_tensor(den, v["are"], v["are"], ALU.mult))
            tb = P.dve(lambda e: e.tensor_tensor(t0, v["aim"], v["aim"], ALU.mult), tsc)
            ta = P.dve(lambda e: e.tensor_tensor(den, den, t0, ALU.add), ta, tb)
            tden = P.dve(lambda e: e.reciprocal(den, den), ta)
            a = P.dve(lambda e: e.tensor_tensor(t0, lr, v["are"], ALU.mult), tl, ta)
            b = P.dve(lambda e: e.tensor_tensor(t1_, li, v["aim"], ALU.mult), tli)
            a = P.dve(lambda e: e.tensor_tensor(cr, t0, t1_, ALU.add), a, b)
            tcr = P.dve(lambda e: e.tensor_tensor(cr, cr, den, ALU.mult), a, tden)
            b = P.dve(lambda e: e.tensor_tensor(t2_, li, v["are"], ALU.mult), tli)
            d = P.dve(lambda e: e.tensor_tensor(x4, lr, v["aim"], ALU.mult), tl)
            b = P.dve(lambda e: e.tensor_tensor(ci5, t2_, x4, ALU.subtract), b, d)
            tci = P.dve(lambda e: e.tensor_tensor(ci5, ci5, den, ALU.mult), b, tden)
            s5t.update(mag=tm, sc=tsc, c=[tcr, tci])

        acct = moe1()
        tx = layer_norm(None, lambda tt, h: (y3[:, tt, h * 512:(h + 1) * 512], acct[tt][h]), lambda *a: None, t_gb)
        dump("ln3", x3, tx)
        txT = transpose_rows(xT, x3, tx, [4, 5, 6, 7])
        free0 = tx

        yaT, ybT, ycT = ar(0, 4, T), ar(1024, 4, T), ar(2048, 4, T)
        GT = ar(3072, EARLY, 3, T)
        zT = ar(6144, 14 * 257).rearrange("p (i t) -> p i t", i=14)
        W0 = 6144 + 14 * 257
        S0 = W0 + 10496
        LW = ar(S0 + 2048, 2, 512)
        s_l = sem("s_l")
        t_l = P.dma("act", ar(S0 + 2048, 1024), dr["lora"], s_l, 16, free0)
        BBt = Y[:, 0:1024].rearrange("p (k n) -> p k n", k=2)
        CTt = Y[:, 1024:2048].rearrange("p (k n) -> p k n", k=2)
        CS = GB[:, 0:1024].rearrange("p (i t) -> p i t", i=4)
        SN = GB[:, 1024:2048].rearrange("p (i t) -> p i t", i=4)
        E0 = W0 + 5700
        Z = ar(E0, 2, 512)
        b5, c5 = ar(E0 + 1024, 512), ar(E0 + 1536, 512)
        w1, w2 = ar(E0 + 2048, 16, 16), ar(E0 + 2304, 16, 16)
        dup = ar(E0 + 2560, 8, 128)
        s_b, s_cc = sem("s_b5"), sem("s_c5")
        tb_ = P.dma("act", b5, dr["s5b"], s_b, 16, free0)
        tc_ = P.dma("act", c5, dr["s5c"], s_cc, 16, free0)

        def s5_b():
            bre = b5[:, 0:256].rearrange("p (a b) -> p a b", a=16)
            bim = b5[:, 256:512].rearrange("p (a b) -> p a b", a=16)
            bc = lambda a_: a_.unsqueeze(2).to_broadcast([128, 16, 16])
            tz = P.dve(lambda e: e.memset(Z, 0.0), free0)
            zt = []
            for k, (m1, m2, op) in enumerate(((cr, ci5, ALU.subtract), (ci5, cr, ALU.add))):
                t = P.dve(lambda e, m1=m1: e.tensor_tensor(w1, bre, bc(m1), ALU.mult), tb_, s5t["c"], zt)
                t2 = P.dve(lambda e, m2=m2: e.tensor_tensor(w2, bim, bc(m2), ALU.mult), tb_, zt)
                for g in range(2):
                    r = slice(64 * g, 64 * g + 64)
                    dst = Z[:, k, :].rearrange("p (t h) -> p t h", t=16)[r, :, 16 * g:16 * g + 16]
                    zt.append(P.dve(lambda e, dst=dst, r=r, op=op: e.tensor_tensor(dst, w1[r], w2[r], op), t, t2, tz))
            td = []
            for k in range(2):
                src = c5[:, 256 * k:256 * k + 256].rearrange("p (q n) -> p q n", q=4)
                for h in range(2):
                    td.append(P.dve(lambda e, k=k, h=h, src=src: e.tensor_copy(dup[:, 4 * k:4 * k + 4, 64 * h:64 * h + 64], src), tc_))
            return zt, td

        def s5_bt(zt):
            for k in range(2):
                for q in range(4):
                    tk = P.tr(PB[6 + k][:, q * 128:q * 128 + 128], Z[:, k, q * 128:q * 128 + 128], ident, zt, bfree[6 + k])
                bfree[6 + k] = evac(BBt[:, k, :], PB[6 + k][:, :], tk, "act", None, free0)
            return [bfree[6], bfree[7]]

        def s5_ct(td):
            tct = []
            mk = c["cmask"].unsqueeze(1).to_broadcast([128, 4, 128])
            for k in range(2):
                for q in range(4):
                    last = P.tr(PB[6 + k][:, q * 128:q * 128 + 128], dup[:, 4 * k + q, :], ident, td, bfree[6 + k])
                t = P.dve(lambda e, k=k, mk=mk: e.scalar_tensor_tensor(
                    CTt[:, k, :].rearrange("p (q m) -> p q m", q=4), PB[6 + k][:, :].rearrange("p (q m) -> p q m", q=4),
                    1.0 if k == 0 else -1.0, mk, ALU.mult, ALU.mult), last)
                bfree[6 + k] = t
                tct.append(t)
            return tct

        mq, mk_, mv = ar(W0, 4, T), ar(W0 + 1024, 4, T), ar(W0 + 2048, 2, 512)
        tu = take_T("u2", [ycT[:, i, :] for i in range(4)], None, 512, [4, 5], [txT, free0], "act")
        zt, td = s5_b()
        tq = take_T("mqk2", [mq[:, i, :] for i in range(4)], [0.125] * 4, 512, [4, 5], [txT, free0], "act")
        tbb = s5_bt(zt)
        tk_ = take_T("mqk2", [mk_[:, i, :] for i in range(4)], None, 512, [4, 5], [txT, free0], "act")
        tct = s5_ct(td)
        w = ring.take("mv2")
        w3 = w[0].rearrange("p (j n) -> p j n", j=8)
        tv = []
        for tt in range(2):
            p_ = rows(PB[6 + tt][:, :], xT, tt, w3, 8, 0, 512, w[1], bfree[6 + tt])
            bfree[6 + tt] = evac(mv[:, tt, :], PB[6 + tt][:, :], p_, "act", None, free0)
            tv.append(bfree[6 + tt])
        ring.release(p_)
        tz0 = P.dve(lambda e: e.memset(zT[:, :, 0:1], 0.0), free0)
        tzp = []

        def z_steps():
            for ci in range(4):
                w = ring.take("z2" if ci < 3 else "z2b")
                w3 = w[0].rearrange("p (j n) -> p j n", j=8)
                for k in range(4 if ci < 3 else 2):
                    for j in range(8):
                        p_ = (P.mml if j == 7 else P.mm)(PB[5][:, 0:256], w3[:, j, k * 128:(k + 1) * 128], xT[:, j, :], j == 0, j == 7,
                                                         w[1], txT, bfree[5] if j == 0 else None)
                        if j % 2 and j < 7:
                            yield
                    bfree[5] = evac(zT[:, 4 * ci + k, 1:257], PB[5][:, 0:256], p_, "act", None, free0)
                    tzp.append(bfree[5])
                    if k == (3 if ci < 3 else 1):
                        ring.release(p_)
                    yield

        def s5_steps(ydone):
            m1, m2, zr, zi = [ar(S0 + 256 * i, T) for i in range(4)]
            hh = [(ar(S0 + 1024 + 512 * i, T), ar(S0 + 1280 + 512 * i, T)) for i in range(2)]
            bu = [ar(S0 + 1024 + 512 * i, 512) for i in range(2)]
            pm = [ar(S0, 4, 128), ar(S0 + 512, 4, 128)]
            hfree = [None, None]
            mulg = lambda o, a_, b_, *d, par=False: P.pool(lambda e: e.tensor_tensor(o, a_, b_, ALU.mult), *d, par=par)
            addg = lambda o, a_, b_, op, *d: P.pool(lambda e: e.tensor_tensor(o, a_, b_, op), *d)
            tbu = {}

            def enter(i):
                q, r = i // 4, 32 * (i % 4)
                ub = ycT[:, q, :][r:r + 32, :]
                P.mm(PB[6][:, 0:256], BBt[r:r + 32, 0, q * 128:q * 128 + 128], ub, True, True, tbb, tu, bfree[6])
                tk = P.mml(PB[6][:, 256:512], BBt[r:r + 32, 1, q * 128:q * 128 + 128], ub, True, True)
                tbu[i] = bfree[6] = evac(bu[i % 2], PB[6][:, :], tk, "act", None, hfree[i % 2], zt, td, tbb, tct)

            tdone = None
            for q in range(4):
                g4 = slice(4 * q, 4 * q + 4)
                a = P.pool(lambda e, g4=g4: e.tensor_copy(CS[:, :, 0], co[:, g4]), s5t["sc"], free0, tdone)
                b = P.pool(lambda e, g4=g4: e.tensor_copy(SN[:, :, 0], si[:, g4]), s5t["sc"], par=True)
                tt_ = [a, b]
                n = 1
                while n < 256:
                    cn = CS[:, :, n - 1:n].to_broadcast([128, 4, n])
                    sn_ = SN[:, :, n - 1:n].to_broadcast([128, 4, n])
                    p1, p2 = pm[0][:, :, 0:n], pm[1][:, :, 0:n]
                    lo, hi = slice(0, n), slice(n, 2 * n)
                    a = mulg(p1, CS[:, :, lo], cn, tt_)
                    b = mulg(p2, SN[:, :, lo], sn_, par=True)
                    a2 = addg(CS[:, :, hi], p1, p2, ALU.subtract, a, b)
                    a = mulg(p1, CS[:, :, lo], sn_, a2)
                    b = mulg(p2, SN[:, :, lo], cn, par=True)
                    b2 = addg(SN[:, :, hi], p1, p2, ALU.add, a, b)
                    tt_ = [a2, b2]
                    n *= 2
                    if n in (16, 64, 128, 256):
                        yield
                if q == 0:
                    enter(0)
                uq = ycT[:, q, :]
                for k in range(4):
                    i, r = 4 * q + k, 32 * k
                    if i < 15:
                        enter(i + 1)
                    hr, hi_ = hh[k % 2]
                    Ci, Si = CS[:, k, :], SN[:, k, :]
                    a = mulg(m1, hr, Ci, tbu[i], tt_)
                    d = mulg(m2, hi_, Si, par=True)
                    t1 = addg(zr, m1, m2, ALU.add, a, d)
                    a = mulg(m1, hi_, Ci, t1)
                    d = mulg(m2, hr, Si, par=True)
                    t2 = addg(zi, m1, m2, ALU.subtract, a, d)
                    yield
                    mg = mag[:, i:i + 1].to_broadcast([128, 256])
                    t1 = P.dve(lambda e, mg=mg: e.tensor_tensor_scan(zr, mg, zr, 0.0, ALU.mult, ALU.add), t1, s5t["mag"])
                    t2 = P.dve(lambda e, mg=mg: e.tensor_tensor_scan(zi, mg, zi, 0.0, ALU.mult, ALU.add), t2, par=True)
                    a = mulg(m1, zr, Ci, t1, t2)
                    d = mulg(m2, zi, Si, t2, par=True)
                    t3 = addg(hr, m1, m2, ALU.subtract, a, d)
                    a = mulg(m1, zr, Si, t3)
                    d = mulg(m2, zi, Ci, par=True)
                    t4 = addg(hi_, m1, m2, ALU.add, a, d)
                    tdone = t4
                    yield
                    o = PB[7][r:r + 32, 0:256]
                    col = q * 128 + r
                    P.mm(o, CTt[:, 0, col:col + 32], hr, True, False, t3, tct, bfree[7] if k == 0 else None)
                    tk = P.mml(o, CTt[:, 1, col:col + 32], hi_, False, True, t4)
                    hfree[k % 2] = tk
                yield
                t = P.dve(lambda e, uq=uq, q=q: e.scalar_tensor_tensor(uq, uq, v["sd"][:, q:q + 1], PB[7][:, 0:256], ALU.mult, ALU.add), tk, tbu[i])
                bfree[7] = t
                t1 = P.pool(lambda e, uq=uq: e.tensor_tensor(m1, uq, uq, ALU.mult), t)
                t1 = P.dve(lambda e: e.tensor_scalar(m1, m1, 0.044715, 1.0, ALU.mult, ALU.add), t1)
                t1 = P.dve(lambda e, uq=uq: e.tensor_tensor(m1, m1, uq, ALU.mult), t1)
                t1 = P.act(lambda e: e.activation(m1, m1, ACT.Tanh, scale=float(np.sqrt(2 / np.pi))), t1)
                t1 = P.dve(lambda e: e.tensor_scalar(m1, m1, 0.5, 0.5, ALU.mult, ALU.add), t1)
                ydone.append(P.dve(lambda e, uq=uq: e.tensor_tensor(uq, uq, m1, ALU.mult), t1))
                tdone = ydone[-1]

        heads = []
        for h in range(8):
            b = 64 * (h % 2)
            heads.append(dict(kind="moba", q=mq[b:b + 64, h // 2, :], k=mk_[b:b + 64, h // 2, :], base=b, slope=2.0 ** -(h + 1),
                              deps=[tq[h // 2], tk_[h // 2]], v=[mv[:, 0, h * 64:h * 64 + 64], mv[:, 1, h * 64:h * 64 + 64]],
                              vdeps=tv, out=ybT[:, h // 2, :]))
        t_mb = []
        moba = attention_steps(heads, W0 + 3072, t_mb, (4,))

        def weave_steps(a, b, na, nb):
            live = [a, b]
            while live:
                for g, n_ in ((a, na), (b, nb)):
                    for _ in range(n_ if g in live else 0):
                        try:
                            next(g)
                        except StopIteration:
                            live.remove(g)
                            break
                        yield

        def rwkv_steps(res):
            B0 = W0
            fr = [t_mb, zt, td, tbb, tct]
            zs = []
            dz = [ar(S0 - 256 - 256 * k, T) for k in range(2)]

            def shift(i):
                d = dz[i % 2]
                return P.dve(lambda e: e.tensor_tensor(d, zT[:, i, 0:256], zT[:, i, 1:257], ALU.subtract), tzp[i], tz0, fr,
                             zs[i - 2] if i > 1 else None, par=i > 0)

            td_ = shift(0)
            for i in range(14):
                d, t = dz[i % 2], td_
                if i < 13:
                    td_ = shift(i + 1)
                zs.append(P.dve(lambda e, i=i, d=d: e.scalar_tensor_tensor(zT[:, i, 1:257], d, v["mu"][:, i:i + 1], zT[:, i, 1:257],
                                                                           ALU.mult, ALU.add), t, par=True))
                if i % 3 == 2:
                    yield
            fr = [fr, zs]
            z = lambda i: zT[:, i, 1:257]
            txw = P.act(lambda e: e.activation(z(12)[0:64], z(12)[0:64], ACT.Tanh), zs[12])
            t = P.act(lambda e: e.activation(z(13), z(13), ACT.Tanh, scale=0.5), zs[13])
            txg = P.dve(lambda e: e.tensor_scalar(z(13), z(13), 0.5, 0.5, ALU.mult, ALU.add), t)
            hv = SM[:, 600:616].rearrange("p (k i) -> p k i", k=4)
            th = P.dve(lambda e: e.tensor_scalar(hv[:, 0, :], v["w0"], 0.5, None, ALU.mult))
            th = P.dve(lambda e: e.tensor_scalar(hv[:, 1, :], v["a0"], 0.5, None, ALU.mult))
            th = P.dve(lambda e: e.tensor_scalar(hv[:, 2, :], v["ka"], -1.0, 1.0, ALU.mult, ALU.add))
            at = [B0]

            def al(*shape):
                n = int(np.prod(shape))
                r = ar(at[0], *shape)
                at[0] += n
                return r
            iW, Wm = al(T), al(T)
            q1, q2, q3, q4 = al(T), al(T), al(T), al(T)
            two = [[al(T), al(T), al(T), al(T), al(2, 128), al(2, 128), al(2, 128), al(2, 128)] for _ in range(2)]
            Dl, Du, Ou, LakT, LrbT, LrkT = [al(4, 64) for _ in range(6)]
            D2, D2t, N1, N1t = [al(4, 64) for _ in range(4)]
            P1 = al(4, 64)
            MT = al(4, 64)
            Uv, SAv, Apn = al(4, 64), al(4, 64), al(4, 64)
            ApT = al(T)
            PTI, QW = al(4, 64), al(4, 64)
            ST = al(4, 64)
            F = lambda a_: a_.rearrange("p a b -> p (a b)")
            assert at[0] <= S0
            dd = [dict() for _ in range(4)]

            def names(i):
                return two[i % 2] + [z(4 + i), z(i), z(8 + i)]

            def first(i):
                W, G, at_, bt_, An, Bn, Kn, Vn_, kt_, rt_, bons = names(i)
                out_ = dd[i]
                pv = [fr, dd[i - 1]["first"] if i else None, dd[i - 2]["end"] if i > 1 else None]
                rr, kk_, vv = z(i), z(4 + i), z(8 + i)
                p_ = P.mml(PB[4][:, 0:256], LW[0:64, 0, i * 128:(i + 1) * 128], z(12)[0:64], True, True, t_l, txw, bfree[4])
                p2 = P.mml(PB[4][:, 256:512], LW[64:128, 0, i * 128:(i + 1) * 128], z(12)[64:128], True, True, zs[12], p_)
                t = P.act(lambda e, i=i: e.activation(q1, PB[4][:, 0:256], ACT.Tanh, bias=hv[:, 0, i:i + 1], scale=0.5), p_, p2, th, pv)
                tq4 = P.act(lambda e, i=i: e.activation(q4, PB[4][:, 256:512], ACT.Tanh, bias=hv[:, 1, i:i + 1], scale=0.5), p2, th, pv)
                bfree[4] = tq4
                yield
                p3 = P.mml(PB[4][:, 0:256], LW[:, 1, i * 128:(i + 1) * 128], z(13), True, True, txg, bfree[4])
                tG = P.act(lambda e: e.activation(G, PB[4][:, 0:256], ACT.Copy), p3, pv)
                bfree[4] = tG
                tlw = P.dve(lambda e: e.tensor_scalar(q1, q1, -EH / 2, -EH / 2, ALU.mult, ALU.add), t)
                on = c["ones"][:, 0:64]
                tcs = []
                for ch in range(4):
                    s_ = slice(64 * ch, 64 * ch + 64)
                    tcs.append(P.dve(lambda e, s_=s_: e.tensor_tensor_scan(q2[:, s_], on, q1[:, s_], 0.0, ALU.mult, ALU.add), tlw, pv, par=ch > 0))
                yield
                tW = P.act(lambda e: e.activation(W, q2, ACT.Exp), tcs, pv)
                tiW = P.act(lambda e: e.activation(iW, q2, ACT.Exp, scale=-1.0), tcs, pv)
                t = P.dve(lambda e: e.tensor_tensor(q3, q2, q1, ALU.subtract), tcs, pv)
                tWm = P.act(lambda e: e.activation(Wm, q3, ACT.Exp), t, pv)
                yield
                ta = P.dve(lambda e: e.tensor_scalar(q4, q4, 0.5, 0.5, ALU.mult, ALU.add), tq4, par=True)
                t = P.dve(lambda e, i=i, kk_=kk_: e.tensor_scalar(q1, kk_, v["kk"][:, i:i + 1], None, ALU.mult), zs[4 + i], tcs, tWm)
                t = P.dve(lambda e: e.tensor_tensor(q2, q1, q1, ALU.mult), t, tW, tiW, tWm)
                p_ = P.mml(PB[4][:, 0:256], c["bones"], q2, True, True, t, bfree[4])
                yield
                t1 = P.dve(lambda e: e.tensor_scalar(q3, PB[4][:, 0:256], 1e-24, None, ALU.max), p_, tWm)
                bfree[4] = t1
                t1 = P.act(lambda e: e.activation(q3, q3, ACT.Sqrt), t1)
                t1 = P.dve(lambda e: e.reciprocal(q3, q3), t1)
                yield
                tkk = P.dve(lambda e: e.tensor_tensor(q1, q1, q3, ALU.mult), t1)
                tat = P.dve(lambda e: e.scalar_tensor_tensor(at_, q1, -1.0, Wm, ALU.mult, ALU.mult), tkk, tWm, pv)
                t = P.dve(lambda e: e.tensor_tensor(q2, q1, q4, ALU.mult), tkk, ta, p_, par=True)
                tbt = P.dve(lambda e: e.tensor_tensor(bt_, q2, iW, ALU.mult), t, tiW, pv)
                yield
                t = P.dve(lambda e, i=i: e.tensor_scalar(q3, q4, v["ka"][:, i:i + 1], hv[:, 2, i:i + 1], ALU.mult, ALU.add), ta, tkk)
                tkp = P.dve(lambda e, kk_=kk_: e.tensor_tensor(q3, q3, kk_, ALU.mult), t)
                tkt = P.dve(lambda e: e.tensor_tensor(kt_, q3, iW, ALU.mult), tkp, tiW, pv)
                yield
                t = P.dve(lambda e, i=i, rr=rr: e.scalar_tensor_tensor(q2, rr, v["rk"][:, i:i + 1], q3, ALU.mult, ALU.mult), tkp, tbt)
                trt = P.dve(lambda e, rr=rr: e.tensor_tensor(rt_, rr, W, ALU.mult), zs[i], tW, pv, t)
                p_ = P.mml(PB[4][:, 0:256], c["bones"], q2, True, True, t, bfree[4])
                yield
                tbc = P.dve(lambda e: e.tensor_copy(q2, PB[4][:, 0:256]), p_)
                bfree[4] = tbc
                yield
                for k, (src, dst, tk) in enumerate(((at_, An, tat), (bt_, Bn, tbt), (kt_, Kn, tkt), (vv, Vn_, zs[8 + i]))):
                    b = 4
                    for tt in range(2):
                        o = (k % 2) * 256 + tt * 128
                        tr_ = P.tr(PB[b][:, o:o + 128], src[:, tt * 128:(tt + 1) * 128], ident, tk, bfree[b] if k % 2 == 0 else None)
                    if k % 2:
                        for kk2, d2_ in ((0, (An, Kn)[k // 2]), (1, dst)):
                            e_ = evac(F(d2_), PB[b][:, kk2 * 256:kk2 * 256 + 256], tr_, "act", None, pv)
                        bfree[b] = e_
                tn = e_
                tbo = P.dve(lambda e, vv=vv: e.tensor_tensor(bons, q2, vv, ALU.mult), tr_, tbc)
                out_.update(tat=tat, tbt=tbt, tkt=tkt, trt=trt, tbo=tbo, tn=tn, tG=tG, tW=tW)
                out_["first"] = [tn, tbo, tG]
                yield
                yield
            def second(i):
                W, G, at_, bt_, An, Bn, Kn, Vn_, kt_, rt_, bons = names(i)
                tat, tbt, tkt, trt, tbo, tn, tG, tW = [dd[i][k] for k in ("tat", "tbt", "tkt", "trt", "tbo", "tn", "tG", "tW")]
                q1, q2, q3 = at_, bt_, ApT
                pv = [fr, dd[i - 1]["core"] if i else None]
                inst = [(p, tt) for p in range(2) for tt in range(2)]

                def blocks(b):
                    return PB[b][:, 0:256]

                def pairs(l, r, deps, b):
                    tk = None
                    for n_, (p, tt) in enumerate(inst):
                        for c_ in range(2):
                            rs, cs_ = slice(64 * p, 64 * p + 64), slice(128 * tt + 64 * c_, 128 * tt + 64 * c_ + 64)
                            tk = P.mml(PB[b][64 * c_:64 * c_ + 64, n_ * 64:n_ * 64 + 64], l[rs, cs_], r[rs, cs_], True, True, deps, bfree[b],
                                       tk if (n_, c_) == (2, 0) else None)
                    return tk

                def masked(dst, b, mask, tk, eng="dve"):
                    m = c[mask].unsqueeze(1).to_broadcast([128, 4, 64])
                    src = blocks(b).rearrange("p (n t) -> p n t", n=4)
                    return P.dve(lambda e: e.tensor_tensor(dst, src, m, ALU.mult), tk, pv, par=True)

                tk = pairs(bt_, at_, [tat, tbt, pv], 0)
                tDu = masked(Du, 0, "mDu", tk)
                tOu = masked(Ou, 0, "mOu", tk)
                bfree[0] = tOu
                tk = pairs(at_, bt_, [], 1)
                tDl = masked(Dl, 1, "mDl", tk)
                bfree[1] = tDl
                yield
                tk = pairs(kt_, at_, [tkt], 2)
                tLak = masked(LakT, 2, "mSu", tk)
                bfree[2] = tLak
                tk = pairs(bt_, rt_, [trt], 3)
                tLrb = masked(LrbT, 3, "mIu", tk)
                bfree[3] = tLrb
                yield
                tk = pairs(kt_, rt_, [], 0)
                tLrk = masked(LrkT, 0, "mIu", tk)
                bfree[0] = tLrk

                def prod(b, l, r, deps):
                    for n_ in range(4):
                        for h_ in (slice(0, 64), slice(64, 128)):
                            rr_ = r[h_, n_, :] if r is not None else c["i64"][h_, :]
                            tk = P.mml(PB[b][h_, n_ * 64:n_ * 64 + 64], l[h_, n_, :], rr_, True, True, deps, bfree[b])
                    return tk

                def take(dst, b, tk, eng, *deps):
                    e_ = evac(F(dst), blocks(b), tk, eng, None, pv, *deps)
                    bfree[b] = e_
                    return e_

                def plus(dst, b, other, tk, *deps):
                    e_ = P.dve(lambda e: e.tensor_tensor(F(dst), F(other), blocks(b), ALU.add), tk, pv, *deps)
                    bfree[b] = e_
                    return e_

                idb = c["i64"].unsqueeze(1).to_broadcast([128, 4, 64])
                yield
                tP = P.dve(lambda e: e.tensor_tensor(P1, Dl, idb, ALU.add), tDl, pv)
                a = prod(1, Du, Dl, [tDu, tDl])
                t2 = take(D2, 1, a, "act")
                b = prod(2, Dl, Du, [])
                t2t = take(D2t, 2, b, "dve")
                yield
                a = prod(3, D2t, P1, [t2t, tP])
                tP = plus(P1, 3, P1, a)
                a = prod(1, D2t, D2, [t2])
                b = prod(2, D2, D2t, [])
                t4 = take(Dl, 1, a, "act", b)
                t4t = take(Du, 2, b, "dve", a)
                yield
                a = prod(3, Du, P1, [t4t, tP])
                tP = plus(P1, 3, P1, a)
                b = prod(2, Dl, Du, [t4])
                yield
                t8t = take(D2t, 2, b, "dve")
                a = prod(3, D2t, P1, [t8t, tP])
                tP = plus(P1, 3, P1, a)
                yield
                tk = prod(1, P1, None, [tP])
                yield
                tMt = take(D2, 1, tk, "act", b)
                a = prod(0, P1, Ou, [tOu, tP])
                tN = take(N1, 0, a, "act")
                b = prod(2, Ou, P1, [])
                yield
                tNt = take(N1t, 2, b, "dve")
                a = prod(3, N1, N1t, [tN, tNt])
                yield
                tN2 = take(Dl, 3, a, "act")
                a = prod(1, Dl, D2, [tN2, tMt])
                yield
                tR = plus(Du, 1, D2, a)
                a = prod(2, N1t, Du, [tR])
                yield
                tMT = plus(MT, 2, Du, a)
                yield
                h2 = (slice(0, 64), slice(64, 128))
                for n_, (p, tt) in enumerate(inst):
                    for h_ in h2:
                        tk = P.mml(PB[3][h_, n_ * 64:n_ * 64 + 64], LakT[h_, n_, :], Vn_[h_, tt, 64 * p:64 * p + 64], True, True, tLak, tn, bfree[3])
                yield
                tU = evac(F(Uv), PB[3][:, 0:256], tk, "act", None, pv)
                bfree[3] = tU
                for n_, (p, tt) in enumerate(inst):
                    for h_ in h2:
                        tk = P.mml(PB[0][h_, 256 + n_ * 64:256 + n_ * 64 + 64], MT[h_, n_, :], An[h_, tt, 64 * p:64 * p + 64], True, True, tMT, tn, bfree[0])
                for n_, (p, tt) in enumerate(inst):
                    for h_ in h2:
                        tk = P.mml(PB[0][h_, n_ * 64:n_ * 64 + 64], MT[h_, n_, :], Uv[h_, n_, :], True, True, tU)
                tk2 = None
                for c_ in range(2):
                    for n_, (p, tt) in enumerate(inst):
                        tk2 = P.mml(PB[1][64 * p:64 * p + 64, tt * 128 + 64 * c_:tt * 128 + 64 * c_ + 64], An[h2[c_], tt, 64 * p:64 * p + 64],
                                    MT[h2[c_], n_, :], True, True, bfree[1], tk2 if (c_, n_) == (1, 0) else None)
                yield
                tSA = evac(F(SAv), PB[0][:, 0:256], tk, "dve", None, pv)
                tAn = evac(F(Apn), PB[0][:, 256:512], tk, "dve", None, pv, par=True)
                bfree[0] = tAn
                tAp = evac(ApT, PB[1][:, 0:256], tk2, "act", None, pv)
                bfree[1] = tAp
                yield
                tk = None
                for p, ch in ((0, 0), (0, 2), (1, 0), (1, 2), (0, 1), (1, 1)):
                        ps_ = slice(64 * p, 64 * p + 64)
                        sw = tk if (p, ch) == (0, 1) else None
                        tt, hs = ch // 2, slice(64 * (ch % 2), 64 * (ch % 2) + 64)
                        n_ = 2 * p + tt
                        P.mml(PB[2][ps_, ch * 64:ch * 64 + 64], Apn[hs, n_, :], Bn[hs, tt, ps_], True, True, tAn, tn, bfree[2], sw)
                        P.mm(PB[3][ps_, ch * 64:ch * 64 + 64], Bn[hs, tt, ps_], SAv[hs, n_, :], True, False, tSA, bfree[3])
                        tk = P.mml(PB[3][ps_, ch * 64:ch * 64 + 64], Kn[hs, tt, ps_], Vn_[hs, tt, ps_], False, True)
                yield
                i64 = c["i64"].unsqueeze(1).to_broadcast([128, 3, 64])
                tPT = P.dve(lambda e: e.tensor_tensor(PTI[:, 0:3, :], PB[2][:, 0:192].rearrange("p (c n) -> p c n", c=3), i64, ALU.add), tk, pv)
                bfree[2] = tPT
                tQ = []
                for ch in range(3):
                    wc = W[:, 64 * ch + 63:64 * ch + 64]
                    dst = ST[:, 1, :] if ch == 0 else QW[:, ch, :]
                    tQ.append(P.dve(lambda e, wc=wc, dst=dst, ch=ch: e.tensor_scalar(dst, PB[3][:, ch * 64:ch * 64 + 64], wc, None, ALU.mult), tk, pv, par=True))
                bfree[3] = tQ[-1]
                tS = [None, tQ[0]]
                for ch in (1, 2):
                    for p in range(2):
                        ps_ = slice(64 * p, 64 * p + 64)
                        tk = P.mml(PB[0][ps_, ch * 64:ch * 64 + 64], PTI[ps_, ch, :], ST[ps_, ch, :], True, True, tPT, tS[ch], bfree[0])
                    yield
                    wc = W[:, 64 * ch + 63:64 * ch + 64]
                    tS.append(P.dve(lambda e, wc=wc, ch=ch: e.scalar_tensor_tensor(ST[:, ch + 1, :], PB[0][:, ch * 64:ch * 64 + 64], wc, QW[:, ch, :],
                                                                                    ALU.mult, ALU.add), tk, tQ[ch]))
                    bfree[0] = tS[-1]
                yield
                tk = None
                for p in range(2):
                    sw = tk
                    for ch in (1, 2, 3):
                        tt, hs = ch // 2, slice(64 * (ch % 2), 64 * (ch % 2) + 64)
                        ps_ = slice(64 * p, 64 * p + 64)
                        n_ = 2 * p + tt
                        tk = P.mml(PB[1][hs, n_ * 64:n_ * 64 + 64], ApT[ps_, 64 * ch:64 * ch + 64], ST[ps_, ch, :], True, True, tAp, tS[ch], bfree[1], sw)
                yield
                saq = SAv.rearrange("p (a t) n -> p a t n", t=2)
                paq = PB[1][:, 0:256].rearrange("p (a t n) -> p a t n", t=2, n=64)
                t1 = P.dve(lambda e: e.tensor_tensor(saq[64:128, :, 0, :], saq[64:128, :, 0, :], paq[64:128, :, 0, :], ALU.add), tk)
                t2 = P.dve(lambda e: e.tensor_tensor(saq[:, :, 1, :], saq[:, :, 1, :], paq[:, :, 1, :], ALU.add), tk, par=True)
                bfree[1] = t2
                yield
                tk = None
                for c_ in range(2):
                    for n_, (p, tt) in enumerate(inst):
                        ps_ = slice(64 * p, 64 * p + 64)
                        o = PB[2][ps_, tt * 128 + 64 * c_:tt * 128 + 64 * c_ + 64]
                        P.mm(o, Vn_[h2[c_], tt, ps_], LrkT[h2[c_], n_, :], True, False, tLrk, tLrb, bfree[2], tk if (n_, c_) == (0, 1) else None)
                        tk = P.mml(o, SAv[h2[c_], n_, :], LrbT[h2[c_], n_, :], False, True, t1, t2)
                for p in range(2):
                    ps_ = slice(64 * p, 64 * p + 64)
                    for ch in (1, 2, 3):
                        tk = P.mml(PB[0][ps_, 64 * ch:64 * ch + 64], ST[ps_, ch, :], rt_[ps_, 64 * ch:64 * ch + 64], True, True, trt, tS[ch], bfree[0])
                yield
                tY = evac(q1, PB[2][:, 0:256], tk, "dve", None, tat, tbt)
                bfree[2] = tY
                tY = P.dve(lambda e, q1=q1: e.tensor_tensor(q1[:, 64:256], q1[:, 64:256], PB[0][:, 64:256], ALU.add), tY)
                bfree[0] = tY
                dd[i].update(tY=tY, core=[tY, tk])

            def third(i):
                W, G, at_, bt_, An, Bn, Kn, Vn_, kt_, rt_, bons = names(i)
                q1, q2, q3 = at_, bt_, W
                tY, tbo, tG = [dd[i][k] for k in ("tY", "tbo", "tG")]
                p_ = P.mml(PB[4][:, 0:256], c["bmean"], q1, True, True, tY, bfree[4])
                yield
                t = P.dve(lambda e: e.tensor_tensor(q1, q1, PB[4][:, 0:256], ALU.subtract), p_)
                t2 = P.dve(lambda e: e.tensor_tensor(q2, q1, q1, ALU.mult), t, tbo)
                p_ = P.mml(PB[4][:, 256:512], c["bmean"], q2, True, True, t2)
                yield
                t3 = P.act(lambda e: e.activation(q3, PB[4][:, 256:512], ACT.Sqrt, bias=c["epg"]), p_, dd[i]["core"])
                bfree[4] = t3
                yield
                t3 = P.dve(lambda e: e.reciprocal(q3, q3), t3)
                yield
                t = P.dve(lambda e: e.tensor_tensor(q1, q1, q3, ALU.mult), t3)
                t = P.dve(lambda e, i=i: e.tensor_scalar(q1, q1, v["lnw"][:, i:i + 1], v["lnb"][:, i:i + 1], ALU.mult, ALU.add), t)
                yield
                t = P.dve(lambda e: e.tensor_tensor(q1, q1, bons, ALU.add), t, tbo)
                ya = yaT[:, i, :]
                t = P.dve(lambda e, ya=ya: e.tensor_tensor(ya, q1, G, ALU.mult), t, tG)
                res.append(t)
                dd[i]["end"] = [t, dd[i]["core"]]

            def beside(i):
                if i > 0:
                    yield from third(i - 1)
                if i < 3:
                    yield from first(i + 1)

            yield from first(0)
            for i in range(4):
                yield from weave_steps(second(i), beside(i), 2, 1)
            yield from third(3)

        tgl = {}

        def early_gates():
            for dt_ in range(EARLY):
                wg = ring.take("gate2")
                g3 = wg[0].rearrange("p (j n) -> p j n", j=8)
                for br in range(3):
                    for j in range(8):
                        f = P.mml if j == 7 else P.mm
                        p_ = f(PB[5][:, 0:256], g3[:, j, br * 128:(br + 1) * 128], xT[:, j, :], j == 0, j == 7, wg[1], txT, bfree[5] if j == 0 else None)
                        if j < 7:
                            yield
                    bfree[5] = evac(GT[:, dt_, br, :], PB[5][:, 0:256], p_, "act", None, free0)
                    tgl[(dt_, br)] = bfree[5]
                    if br == 2:
                        ring.release(p_)
                    yield

        def mixers(res):
            yield from weave_steps(moba, z_steps(), 1, 3)
            yield from weave_steps(rwkv_steps(res), early_gates(), 2, 1)

        t_rw, t_s5 = [], []
        s5 = s5_steps(t_s5)
        for _ in range(4):
            next(s5)
        for _ in weave_steps(s5, mixers(t_rw), 1, 6):
            pass
        t_gb = load_gb(4, t_s5)
        ring2 = Ring(P, [ar(23500 - (i + 1) * SLOT, SLOT) for i in range(3)] + [None] * RING, plan[n1:], "s_u", start=0)
        ring2.own = 3
        for _ in range(3):
            ring2.load([t_rw, t_s5])
        ring.heir = ring2
        dump("mobay", ybT, t_mb)
        dump("rwy", yaT, t_rw)

        zA, zB = ar(6144, 4, T), ar(9216, 4, T)
        w = ring.take("glu")
        w3 = w[0].rearrange("p (j n) -> p j n", j=4)
        gh = SM[:, 620:628]
        gh2 = SM[:, 628:652]
        th1 = P.dve(lambda e: e.tensor_scalar(gh, v["gb"], 0.5, None, ALU.mult))
        th2 = P.dve(lambda e: e.tensor_scalar(gh2, v["gateb"], 0.5, None, ALU.mult))
        tz = []
        for i in range(4):
            b = 4 + i % 4
            p_ = tile_T(PB[b][:, 0:256], w3, 4, i * 128, 128, ycT, w[1], t_s5, bfree[b])
            p2 = tile_T(PB[b][:, 256:512], w3, 4, (4 + i) * 128, 128, ycT)
            ta = P.act(lambda e, i=i, b=b: e.activation(zB[:, i, :], PB[b][:, 256:512], ACT.Tanh, scale=0.5, bias=gh[:, 4 + i:5 + i]), p2, th1, t_rw)
            tb = P.dve(lambda e, i=i: e.tensor_scalar(zB[:, i, :], zB[:, i, :], 0.5, 0.5, ALU.mult, ALU.add), ta)
            tb = P.dve(lambda e, i=i, b=b: e.scalar_tensor_tensor(zA[:, i, :], PB[b][:, 0:256], v["gb"][:, i:i + 1], zB[:, i, :],
                                                           ALU.add, ALU.mult), tb, p_, t_rw)
            bfree[b] = tb
            tz.append(tb)
        ring.release(p2)
        dump("s5", zA, tz)
        mT = ar(7168, 8, T)
        gtile = [ar(9216 + 256 * i, T) for i in range(4)]
        ydeps = [t_rw, t_mb, tz]
        tm = []
        gfree = [None] * 4
        wu = None
        n = 0
        for dt_ in range(8):
            if dt_ >= EARLY:
                wg = ring.take("gate2")
                g3 = wg[0].rearrange("p (j n) -> p j n", j=8)
            if dt_ % 2 == 0:
                wu = ring.take("up2")
            u5 = wu[0].rearrange("p (d b j n) -> p d b j n", d=2, b=3, j=4)
            acc = mT[:, dt_, :]
            tprev = None
            for br in range(3):
                b = 4 + n % 4
                yT = (yaT, ybT, zA)[br]
                logit = GT[:, dt_, br, :] if dt_ < EARLY else PB[b][:, 0:256]
                if dt_ >= EARLY:
                    tile_T(logit, g3, 8, br * 128, 128, xT, wg[1], bfree[b])
                for j in range(4):
                    f = P.mml if j == 3 else P.mm
                    p2 = f(PB[b][:, 256:512], u5[:, dt_ % 2, br, j, :], yT[:, j, :], j == 0, j == 3, wu[1], ydeps, bfree[b])
                gs = gtile[n % 4]
                t = P.act(lambda e, gs=gs, logit=logit, br=br, dt_=dt_: e.activation(gs, logit, ACT.Tanh, scale=0.5,
                                                            bias=gh2[:, br * 8 + dt_:br * 8 + dt_ + 1]),
                          tgl[(dt_, br)] if dt_ < EARLY else p2, th2, gfree[n % 4], t_rw, tz)
                t = P.dve(lambda e, gs=gs: e.tensor_scalar(gs, gs, 0.5, 0.5, ALU.mult, ALU.add), t)
                if br == 0:
                    t = P.dve(lambda e, gs=gs, b=b, acc=acc: e.tensor_tensor(acc, gs, PB[b][:, 256:512], ALU.mult), t, p2, t_rw)
                    bfree[b] = t
                else:
                    t = P.dve(lambda e, gs=gs, b=b: e.tensor_tensor(gs, gs, PB[b][:, 256:512], ALU.mult), t, p2)
                    bfree[b] = t
                    t = P.dve(lambda e, gs=gs, acc=acc: e.tensor_tensor(acc, acc, gs, ALU.add), t, tprev)
                gfree[n % 4] = t
                tprev = t
                n += 1
            tm.append(tprev)
            if dt_ % 2:
                ring.release(p2)
            if dt_ >= EARLY:
                ring.release(p2)
        dump("merged", mT, tm)
        s_r2 = sem("s_r2")
        t_r = P.dma("act", RW, dr["wr2"], s_r2, 16, tm)
        tk = w_out("wo2", mT, tm)
        tx = add_norm(ALPHA2, tk, t_gb)
        dump("ln4", x3, tx)
        t_gb = load_gb(5, tx)
        txT = transpose_rows(xT, x3, tx, [4, 5, 6, 7])

        G2 = ar(512, 2, 32)
        Lg = ar(1024, 2, 36)
        E2 = ar(1152, 2, 32)
        O2 = ar(1280, 2, 2, 32)
        gt2 = ar(1408, 2, 2)
        Lp = ar(1420, 2, 8)
        OG = ar(1440, 2, 8)
        pe_ = ar(1456, 2, 4)
        m_ = P.dve(lambda e: e.memset(Lp, -3e38), tk[(1, 1)])
        warm(ACT.Exp)
        for tt in range(2):
            p_ = rows(PB[3][:, tt * 36:tt * 36 + 36], xT, tt, RW, 8, 0, 36, t_r, txT, bfree[3] if tt == 0 else None)
        b36 = v["br2"].unsqueeze(1).to_broadcast([128, 2, 36])
        t = P.dve(lambda e: e.tensor_tensor(Lg, PB[3][:, 0:72].rearrange("p (t k) -> p t k", t=2), b36, ALU.add), p_, tk[(1, 1)])
        bfree[3] = t
        t = P.dve(lambda e: e.tensor_copy(Lp[:, :, 0:4], Lg[:, :, 0:4]), t, m_)
        mx = SM[:, 700:716].rearrange("p (t k) -> p t k", t=2)
        ixf = SM[:, 716:732].rearrange("p (t k) -> p t k", t=2)
        ixg = IX[:, 16:32].rearrange("p (t k) -> p t k", t=2)
        eg = SM[:, 780:788].rearrange("p (t k) -> p t k", t=2)
        pg = SM[:, 788:790].unsqueeze(2)
        for tt in range(2):
            a = P.dve(lambda e, tt=tt: e.max(mx[:, tt, :], Lp[:, tt, :]), t, par=tt == 1)
        for tt in range(2):
            b = P.dve(lambda e, tt=tt: e.max_index(ixg[:, tt, :], mx[:, tt, :], Lp[:, tt, :]), a, par=tt == 1)
        a = P.dve(lambda e: e.tensor_tensor(eg, Lg[:, :, 0:4], mx[:, :, 0:1].to_broadcast([128, 2, 4]), ALU.subtract), par=True)
        a = P.act(lambda e: e.activation(eg, eg, ACT.Exp), a)
        b = P.dve(lambda e: e.tensor_copy(ixf, ixg), b)
        i8 = c["iota"][:, 0:8].unsqueeze(1).to_broadcast([128, 2, 8])
        oh = P.dve(lambda e: e.tensor_tensor(OG, i8, ixf[:, :, 0:1].to_broadcast([128, 2, 8]), ALU.is_equal), b)
        pen = P.dve(lambda e: e.tensor_scalar(pe_, OG[:, :, 0:4], 3e38, -3e38, ALU.mult, ALU.add), oh)
        for tt in range(2):
            e4 = E2[:, tt, :].rearrange("p (g k) -> p g k", g=4)
            l4 = Lg[:, tt, 4:36].rearrange("p (g k) -> p g k", g=4)
            o4 = OG[:, tt, 0:4].unsqueeze(2).to_broadcast([128, 4, 8])
            t = P.dve(lambda e, e4=e4, l4=l4, o4=o4: e.tensor_tensor(e4, l4, o4, ALU.mult), oh, par=True)
        for tt in range(2):
            e4 = E2[:, tt, :].rearrange("p (g k) -> p g k", g=4)
            pb4 = pe_[:, tt, :].unsqueeze(2).to_broadcast([128, 4, 8])
            t = P.dve(lambda e, e4=e4, pb4=pb4: e.tensor_tensor(e4, e4, pb4, ALU.add), pen, t, par=tt == 1)
        tpg = P.dve(lambda e: e.tensor_reduce(pg, eg, AX.X, ALU.add), a, par=True)
        tpg = P.dve(lambda e: e.reciprocal(pg, pg), tpg)
        toh, tg_ = top2(E2, 32, O2, gt2, t, 740, (pg, tpg))

        def tgate2():
            return gates(G2, O2, gt2, 32, [toh, tg_])

        def moe2():
            pos, over, cnt = ar(1504, 2, 32), ar(448, 2, 32), ar(1568, 2, 32)
            flag, flagf = IX[:, 33:34], SM[:, 851:852]
            tpos, rest = slots(NE2, 32, O2, G2, pos, over, cnt, flag, flagf, toh, tgate2)
            o = 1664
            PS, PG = [ar(o + 256 * i, 2, 128) for i in range(2)], [ar(o + 512 + 256 * i, 2, 128) for i in range(2)]
            PGT = [ar(o + 1024 + 256 * i, 256) for i in range(2)]
            XG = [ar(o + 1536 + 1024 * i, 8, 128) for i in range(2)]
            HN = [ar(o + 3584 + 256 * i, 256) for i in range(2)]
            HT = [ar(o + 4096 + 256 * i, 2, 128) for i in range(2)]
            YS = [ar(o + 4608 + 1024 * i, 1024) for i in range(2)]
            acc = {}
            NQ = NE2 // 4
            st = [dict() for _ in range(NQ)]
            io = c["iota"][:, 0:32].unsqueeze(1).to_broadcast([128, 4, 32])

            def old(q, k):
                return st[q - 2][k] if q >= 2 else None

            def select(q):
                i = q % 2
                for tt in range(2):
                    po = pos[:, tt, 4 * q:4 * q + 4].unsqueeze(2).to_broadcast([128, 4, 32])
                    ga = G2[:, tt, 4 * q:4 * q + 4].unsqueeze(2).to_broadcast([128, 4, 32])
                    ps_ = PS[i][:, tt, :].rearrange("p (a b) -> p a b", a=4)
                    pg_ = PG[i][:, tt, :].rearrange("p (a b) -> p a b", a=4)
                    P.dve(lambda e, ps_=ps_, po=po: e.tensor_tensor(ps_, io, po, ALU.is_equal), tpos, old(q, "gath"))
                    t = P.dve(lambda e, ps_=ps_, pg_=pg_, ga=ga: e.tensor_tensor(pg_, ps_, ga, ALU.mult), old(q, "pgt"))
                st[q]["sel"] = t

            def gather(q):
                i, d = q % 2, st[q]
                d["xg"] = []
                for g in range(2):
                    b = 6 + g
                    for k in range(4):
                        for tt in range(2):
                            dt_ = 4 * g + k
                            tk = (P.mml if tt else P.mm)(PB[b][:, k * 128:(k + 1) * 128], x3[:, tt, dt_ * 128:(dt_ + 1) * 128], PS[i][:, tt, :],
                                                         tt == 0, tt == 1, d["sel"], tx, bfree[b])
                    bfree[b] = evac(XG[i][:, 4 * g:4 * g + 4, :].rearrange("p a b -> p (a b)"), PB[b][:, :], tk, "dve", None, old(q, "in"))
                    d["xg"].append(bfree[b])
                d["gath"] = tk
                for tt in range(2):
                    tk = P.tr(PB[6][:, tt * 128:(tt + 1) * 128], PG[i][:, tt, :], ident, bfree[6])
                d["pgt"] = tk
                bfree[6] = evac(PGT[i], PB[6][:, 0:256], tk, "act", None, old(q, "scat"))
                d["pg"] = bfree[6]

            def scatter(q):
                i, d = q % 2, st[q]
                for tt in range(2):
                    for h in range(2):
                        b = 2 + h
                        tk = P.mml(PB[b][:, :], PGT[i][:, tt * 128:(tt + 1) * 128], YS[i][:, h * 512:(h + 1) * 512], True, True,
                                   d["pg"], d["ys"], bfree[b])
                        ys = y3[:, tt, h * 512:(h + 1) * 512]
                        bfree[b] = P.dve(lambda e, ys=ys, b=b: e.tensor_tensor(ys, ys, PB[b][:, :], ALU.add), tk, acc[(tt, h)])
                        acc[(tt, h)] = bfree[b]
                d["scat"] = tk

            select(0)
            gather(0)
            rest()
            tz = P.dve(lambda e: e.tensor_scalar(Y[:, :], X[:, :], ALPHA2, None, ALU.mult), tx)
            for tt in range(2):
                for h in range(2):
                    acc[(tt, h)] = tz
            for q in range(NQ):
                i, d = q % 2, st[q]
                b = 4 + i
                for ci in range(4):
                    w = ring2.take("e2in")
                    w4 = w[0].rearrange("p (k j n) -> p k j n", k=2, j=4)
                    for kk in range(2):
                        k = 2 * ci + kk
                        for j in range(4):
                            tk = (P.mml if j == 3 else P.mm)(PB[b][32 * j:32 * j + 32, :], XG[i][:, k, 32 * j:32 * j + 32], w4[:, kk, j, :],
                                                             k == 0, k == 7, w[1], d["xg"], bfree[b] if k == 0 else None)
                    ring2.release(tk)
                d["in"] = tk
                hn = HN[i]
                t1 = P.act(lambda e, hn=hn, b=b: e.activation(hn, PB[b][:, 0:256], ACT.Silu), tk, old(q, "turn"))
                t2 = P.dve(lambda e, hn=hn, b=b: e.tensor_tensor(hn, hn, PB[b][:, 256:512], ALU.mult), t1)
                bfree[b] = t2
                if q + 1 < NQ:
                    select(q + 1)
                if q:
                    scatter(q - 1)
                if q + 1 < NQ:
                    gather(q + 1)
                for k in range(2):
                    tk = P.tr(PB[7][:, k * 128:(k + 1) * 128], hn[:, k * 128:(k + 1) * 128], ident, t2, bfree[7])
                d["turn"] = tk
                bfree[7] = evac(HT[i].rearrange("p a b -> p (a b)"), PB[7][:, 0:256], tk, "act", None, old(q, "down"))
                th_ = bfree[7]
                for f in range(2):
                    w = ring2.take("e2out")
                    w3 = w[0].rearrange("p (j n) -> p j n", j=4)
                    for h in range(2):
                        for j in range(4):
                            tk = (P.mml if j == 3 else P.mm)(PB[h][32 * j:32 * j + 32, :], HT[i][:, f, 32 * j:32 * j + 32],
                                                             w3[:, j, h * 512:(h + 1) * 512], f == 0, f == 1,
                                                             w[1], th_, bfree[h] if f == 0 else None)
                    ring2.release(tk)
                d["down"] = tk
                bfree[0] = evac(YS[i][:, 0:512], PB[0][:, :], tk, "act", None, old(q, "scat"))
                bfree[1] = evac(YS[i][:, 512:1024], PB[1][:, :], tk, "dve", None, old(q, "scat"))
                d["ys"] = [bfree[0], bfree[1]]
            scatter(NQ - 1)
            pl = []
            for e_ in range(NE2):
                q, j = e_ // 4, e_ % 4
                ein = dr["e2in"][q].rearrange("c p (k j n) -> p c k j n", k=2, j=4)[:, :, :, j, :]
                pl.append(("e2in", ein, SLOT))
                eo = dr["e2out"][q].rearrange("f p (j n) -> p f j n", j=4)[:, :, j, :]
                pl.append(("e2out", eo, 2048))
            overflow("o2", pl, "e2in", "e2out", NE2, 2, over, flag[0:1, :])
            return [[acc[(tt, h)] for h in range(2)] for tt in range(2)]

        acct = moe2()
        tx = layer_norm(None, lambda tt, h: (y3[:, tt, h * 512:(h + 1) * 512], acct[tt][h]), lambda *a: None, t_gb)
        s_o = sem("s_o")
        o3 = out.rearrange("a (t p) d -> p (a t) d", p=128)
        to = P.dma("sp", o3[:, 0, :], x3[:, 0, :], s_o, 16, tx[0])
        to = P.dma("act", o3[:, 1, :], x3[:, 1, :], s_o, 32, tx[1])
        P.wait("sp", [to])

        block = ctx.enter_context(nc.Block())
        block.sync(P.run("sp"))
        block.scalar(P.run("act"))
        block.vector(P.run("dve"))
        block.gpsimd(P.run("pool"))
        block.tensor(P.run("pe"))


def cols(w, groups, kt=8):
    out = []
    for g in groups:
        a = w[:, g]
        out.append(a.reshape(kt, 128, a.shape[1]).transpose(1, 0, 2).reshape(128, -1))
    return np.ascontiguousarray(np.stack(out))


def rowsk(w, nk=4):
    k = w.shape[0] // 128
    a = w.reshape(k, 128, 1024).transpose(1, 0, 2)
    n = -(-k // nk)
    o = np.zeros((n, 128, nk * 1024), w.dtype)
    for i in range(n):
        b = a[:, i * nk:(i + 1) * nk]
        o[i, :, :b.shape[1] * 1024] = b.reshape(128, -1)
    return o


def pairs(n):
    return [np.r_[i:i + 256, n + i:n + i + 256] for i in range(0, n, 256)]


def col4(a):
    return a.reshape(-1, 128).T


def layout(I):
    I = {k: np.asarray(a) for k, a in I.items()}
    r = lambda a, b: np.arange(a, b)
    A = {}
    A["x"], A["mem"] = I["x"], I["mem"]
    A["cst"] = CT
    A["pos"] = np.ascontiguousarray(np.broadcast_to(I["positions"].reshape(1, T), (128, T)))
    sw, fo = I["w_in_swa"][0], I["w_in_fox"][0]
    A["wkv"] = np.concatenate([cols(I["w_mem_kv"][i], [r(0, 512)]) for i in range(2)])
    k0 = 768
    kd = np.concatenate([np.r_[k0 + 64 * g:k0 + 64 * g + 64, k0 + 64 * g:k0 + 64 * g + 64] for g in range(3)])
    A["swT"] = cols(sw, [r(0, 512), np.r_[512:768, 1152:1408]])
    A["swk"] = cols(sw, [kd])
    A["swv"] = cols(sw, [r(960, 1152)])
    A["wo"] = np.concatenate([cols(I["w_out"][i], [r(0, 512), r(512, 1024)]) for i in range(2)])
    A["fin"] = cols(I["w_ffn_in"][0], pairs(DFF))
    A["fout"] = rowsk(I["w_ffn_out"][0])
    A["foT"] = cols(fo, [r(512 * i, 512 * i + 512) for i in range(3)])
    A["foqf"] = cols(fo, [r(2304, 2572)])
    A["fov"] = cols(fo, [r(1536, 2048)])
    A["fov2"] = cols(fo, [r(2048, 2304)])
    A["ein"] = np.stack([cols(w, pairs(DFF)) for w in I["w_exp_in"][0]])
    A["eout"] = np.stack([rowsk(w) for w in I["w_exp_out"][0]])
    w2 = I["w_in_2"][0]
    A["z2"] = cols(w2, [r(0, 512), r(512, 1024), r(1024, 1536)])
    A["z2b"] = cols(w2, [r(1536, 1792)])
    A["mqk2"] = cols(w2, [r(1792, 2304), r(2304, 2816)])
    A["mv2"] = cols(w2, [r(2816, 3328)])
    A["u2"] = cols(w2, [r(3328, 3840)])
    A["gate2"] = cols(w2, [np.concatenate([3840 + 1024 * b + r(128 * d, 128 * d + 128) for b in range(3)]) for d in range(8)])
    up = np.stack([I["w_up_rwkv_2"][0], I["w_up_moba_2"][0], I["w_up_ssm_2"][0]])
    A["up2"] = np.ascontiguousarray(up.reshape(3, 4, 128, 4, 2, 128).transpose(3, 2, 4, 0, 1, 5).reshape(4, 128, 3072))
    A["glu"] = cols(I["ssm_glu_w_2"][0], [r(0, 1024)], 4)
    A["wo2"] = cols(I["w_out_2"][0], [r(0, 512), r(512, 1024)])
    gu = np.concatenate([I["expert_w_gate_2"][0], I["expert_w_up_2"][0]], 2).reshape(8, 4, 4, 2, 128, 512)
    A["e2in"] = np.ascontiguousarray(gu.transpose(0, 2, 4, 3, 1, 5).reshape(8, 4, 128, 4096))
    dn = I["expert_w_down_2"][0].reshape(8, 4, 2, 128, 1024)
    A["e2out"] = np.ascontiguousarray(dn.transpose(0, 2, 3, 1, 4).reshape(8, 2, 128, 4096))
    gb = [np.concatenate([I["ln_attn_g"][0], I["ln_attn_b"][0]]), np.concatenate([I["ln_ffn_g"][0], I["ln_ffn_b"][0]]),
          np.concatenate([I["ln_attn_g"][1], I["ln_attn_b"][1]]), np.concatenate([I["ln_ffn_g"][1], I["ln_ffn_b"][1]]),
          np.concatenate([I["ln1_w_2"][0], I["ln1_b_2"][0]]), np.concatenate([I["ln2_w_2"][0], I["ln2_b_2"][0]])]
    A["gb"] = np.ascontiguousarray(np.broadcast_to(np.stack(gb)[:, None, :], (6, 128, 2048)))
    kp = lambda w: np.ascontiguousarray(w.reshape(8, 128, -1).transpose(1, 0, 2))
    A["wr1"] = kp(I["w_router"][0])
    A["wr2"] = kp(np.concatenate([I["router_group_w_2"][0], I["router_expert_w_2"][0]], 1))
    A["lora"] = np.ascontiguousarray(np.concatenate([np.concatenate([I["rwkv_w2_2"][0], I["rwkv_a2_2"][0]], 0), I["rwkv_g2_2"][0]], 1))
    V = np.zeros((128, NVEC), np.float32)

    def put(n, a):
        o, w = VOFF[n]
        V[0:a.shape[0], o:o + w] = a
    bc = lambda a: np.broadcast_to(a[None, :], (128, a.shape[0]))
    put("sink", bc(I["attn_sinks"][0]))
    put("bf", I["b_forget"][0][:, None])
    put("mu", col4(I["rwkv_mu_2"][0]))
    for n, k in (("w0", "rwkv_w0_2"), ("a0", "rwkv_a0_2"), ("kk", "rwkv_k_k_2"), ("ka", "rwkv_k_a_2"), ("rk", "rwkv_r_k_2"),
                 ("lnw", "rwkv_ln_w_2"), ("lnb", "rwkv_ln_b_2"), ("are", "ssm_a_re_2"), ("aim", "ssm_a_im_2"), ("sd", "ssm_d_2"),
                 ("gb", "ssm_glu_b_2"), ("gateb", "gate_b_2")):
        put(n, col4(I[k][0].reshape(-1)))
    put("ldt", np.repeat(I["ssm_log_dt_2"][0], 64).reshape(16, 128).T)
    put("br1", bc(I["b_router"][0]))
    put("br2", bc(np.concatenate([I["router_group_b_2"][0], I["router_expert_b_2"][0]])))
    A["vec"] = V
    b5 = [I[k][0].reshape(16, 128, 16).transpose(1, 0, 2).reshape(128, 256) for k in ("ssm_b_re_2", "ssm_b_im_2")]
    A["s5b"] = np.ascontiguousarray(np.concatenate(b5, 1))
    c5 = [I[k][0].reshape(4, 128, 64).transpose(1, 0, 2).reshape(128, 256) for k in ("ssm_c_re_2", "ssm_c_im_2")]
    A["s5c"] = np.ascontiguousarray(np.concatenate(c5, 1))
    return A


def program(nc, arrays, dbg=()):
    dr = {n: nc.dram_tensor("in_" + n, a.shape, mybir.dt.from_np(a.dtype), kind="ExternalInput").ap() for n, a in arrays.items()}
    out = nc.dram_tensor("out_0", (1, T, D), F32, kind="ExternalOutput").ap()
    d = {n: nc.dram_tensor("dbg_" + n, s, F32, kind="ExternalOutput").ap() for n, s in dbg}
    build(nc, dr, out, d)


def kernel(**inputs):
    import concourse.bacc as _bacc
    from concourse.bass_utils import run_bass_kernel_spmd as _run

    arrays = layout(inputs)
    nc = _bacc.Bacc("TRN2", target_bir_lowering=False, num_devices=1)
    program(nc, arrays)
    r = _run(nc, [{"in_" + n: a for n, a in arrays.items()}], core_ids=[0])
    return r.results[0]["out_0"]
```
